# Optimizing a Trainium2 kernel written in Bass

```python
import jax, jax.numpy as jnp
from jax import lax
import numpy as np

D_MODEL = 2048
BATCH = 1
SEQ = 256
DEPTH = 1

N_META = 16
CHUNK = 64
CONV_K = 4
NORM_EPS = 1e-6
L2_EPS = 1e-6

SSD_HEADS = 32
SSD_HEAD_DIM = 64
SSD_D_INNER = SSD_HEADS * SSD_HEAD_DIM
SSD_GROUPS = 4
SSD_STATE = 128
SSD_CONV_DIM = SSD_D_INNER + 2 * SSD_GROUPS * SSD_STATE

GDN_HEADS = 16
GDN_DK = 128
GDN_DV = 128
GDN_DQK = GDN_HEADS * GDN_DK
GDN_DVW = GDN_HEADS * GDN_DV
GDN_CONV_DIM = 2 * GDN_DQK + GDN_DVW

N_BRANCH = 2

PEER_HEADS = 8
PEER_N_KEYS = 128
PEER_N_EXPERTS = PEER_N_KEYS * PEER_N_KEYS
PEER_TOPK = 16
PEER_D_KEY = 128
PEER_POS_BLOCK = 16

IN_WIDTHS = (SSD_D_INNER, SSD_CONV_DIM, SSD_HEADS, GDN_CONV_DIM, GDN_DVW, GDN_HEADS, GDN_HEADS, N_BRANCH * D_MODEL)
IN_DIM = sum(IN_WIDTHS)
IN_SPLITS = tuple(sum(IN_WIDTHS[:i + 1]) for i in range(len(IN_WIDTHS) - 1))

kernel_name = "hybrid_ssd_gdn_peer_block"

def _rms(x):
    xf = x.astype(jnp.float32)
    return (xf * lax.rsqrt(jnp.mean(xf * xf, axis=-1, keepdims=True) + NORM_EPS)).astype(x.dtype)

def _rmsnorm(x, w):
    return _rms(x) * w

def _group_rmsnorm(y, w):
    shp = y.shape
    yg = _rms(y.reshape(shp[:-1] + (SSD_GROUPS, shp[-1] // SSD_GROUPS)))
    return yg.reshape(shp) * w

def _l2norm(x):
    xf = x.astype(jnp.float32)
    return (xf * lax.rsqrt(jnp.sum(xf * xf, axis=-1, keepdims=True) + L2_EPS)).astype(x.dtype)

def _causal_dwconv(x, w):
    return lax.conv_general_dilated(
        x, w[:, None, :].astype(x.dtype), window_strides=(1,), padding=((CONV_K - 1, 0),),
        dimension_numbers=("NWC", "WIO", "NWC"), feature_group_count=x.shape[-1])

def _decay_matrix(cs):
    q = cs.shape[-1]
    mask = jnp.tril(jnp.ones((q, q), dtype=bool))
    diff = cs[..., :, None] - cs[..., None, :]
    return jnp.exp(jnp.where(mask, diff, -jnp.inf))

def _ssd_chunked(x, dt, A, Bm, Cm):
    b, lp = x.shape[:2]
    nc = lp // CHUNK
    r = SSD_HEADS // SSD_GROUPS
    cdt = x.dtype
    xc = (x * dt[..., None].astype(cdt)).reshape(b, nc, CHUNK, SSD_GROUPS, r, SSD_HEAD_DIM)
    bc = Bm.reshape(b, nc, CHUNK, SSD_GROUPS, SSD_STATE)
    cc = Cm.reshape(b, nc, CHUNK, SSD_GROUPS, SSD_STATE)
    a = (dt * A).reshape(b, nc, CHUNK, SSD_GROUPS, r).transpose(0, 3, 4, 1, 2)
    a_cs = jnp.cumsum(a, axis=-1)
    cb = jnp.einsum("bclgn,bcsgn->bgcls", cc, bc)
    w_intra = cb[:, :, None] * _decay_matrix(a_cs).astype(cdt)
    y_diag = jnp.einsum("bgrcls,bcsgrp->bclgrp", w_intra, xc)
    to_end = jnp.exp(a_cs[..., -1:] - a_cs).astype(cdt).transpose(0, 3, 4, 1, 2)
    states = jnp.einsum("bcsgn,bcsgrp->bcgrpn", bc, xc * to_end[..., None])
    chunk_decay = jnp.exp(a_cs[..., -1]).astype(cdt)

    def step(s, inp):
        st, dec = inp
        return s * dec[..., None, None] + st, s

    s0 = jnp.zeros(states.shape[:1] + states.shape[2:], states.dtype)
    _, prev = lax.scan(step, s0, (jnp.moveaxis(states, 1, 0), jnp.moveaxis(chunk_decay, 3, 0)))
    prev = jnp.moveaxis(prev, 0, 1)
    from_start = jnp.exp(a_cs).astype(cdt).transpose(0, 3, 4, 1, 2)
    y_off = jnp.einsum("bclgn,bcgrpn->bclgrp", cc, prev) * from_start[..., None]
    return (y_diag + y_off).reshape(b, lp, SSD_HEADS, SSD_HEAD_DIM)

def _gated_delta_chunked(q, k, v, g, beta):
    b, lp = q.shape[:2]
    nc = lp // CHUNK
    cdt = q.dtype

    def chunks(t):
        return jnp.moveaxis(t.reshape(b, nc, CHUNK, GDN_HEADS, t.shape[-1]), 3, 1)

    q = chunks(q) * (GDN_DK ** -0.5)
    k = chunks(k)
    v = chunks(v)
    g_cs = jnp.cumsum(jnp.moveaxis(g.reshape(b, nc, CHUNK, GDN_HEADS), 3, 1), axis=-1)
    beta = jnp.moveaxis(beta.reshape(b, nc, CHUNK, GDN_HEADS), 3, 1)[..., None].astype(cdt)
    decay = _decay_matrix(g_cs)
    kb = k * beta
    strict = jnp.tril(jnp.ones((CHUNK, CHUNK), dtype=bool), -1)
    lm = jnp.where(strict, jnp.einsum("bhcid,bhcjd->bhcij", kb, k).astype(jnp.float32) * decay, 0.0)
    eye = jnp.eye(CHUNK, dtype=jnp.float32)
    tinv = lax.linalg.triangular_solve(lm + eye, jnp.broadcast_to(eye, lm.shape),
                                       left_side=True, lower=True, unit_diagonal=True)
    u = jnp.einsum("bhcij,bhcje->bhcie", tinv, (v * beta).astype(jnp.float32)).astype(cdt)
    w = jnp.einsum("bhcij,bhcjd->bhcid", tinv,
                   kb.astype(jnp.float32) * jnp.exp(g_cs)[..., None]).astype(cdt)
    qk = (jnp.einsum("bhcid,bhcjd->bhcij", q, k).astype(jnp.float32) * decay).astype(cdt)
    qg = (q.astype(jnp.float32) * jnp.exp(g_cs)[..., None]).astype(cdt)
    kd = (k.astype(jnp.float32) * jnp.exp(g_cs[..., -1:] - g_cs)[..., None]).astype(cdt)
    dl = jnp.exp(g_cs[..., -1]).astype(cdt)

    def step(s, inp):
        qg_c, w_c, u_c, kd_c, qk_c, dl_c = inp
        v_new = u_c - jnp.einsum("bhid,bhde->bhie", w_c, s)
        o = jnp.einsum("bhid,bhde->bhie", qg_c, s) + jnp.einsum("bhij,bhje->bhie", qk_c, v_new)
        s = s * dl_c[..., None, None] + jnp.einsum("bhid,bhie->bhde", kd_c, v_new)
        return s, o

    s0 = jnp.zeros((b, GDN_HEADS, GDN_DK, GDN_DV), cdt)
    xs = tuple(jnp.moveaxis(t, 2, 0) for t in (qg, w, u, kd, qk, dl))
    _, o = lax.scan(step, s0, xs)
    return jnp.transpose(o, (1, 0, 3, 2, 4)).reshape(b, lp, GDN_HEADS, GDN_DV)

def _hybrid_mixer(h, w_in, ssd_conv_w, ssd_conv_b, ssd_dt_bias, ssd_A_log, ssd_D, ssd_norm_w,
                  gdn_conv_w, gdn_dt_bias, gdn_A_log, gdn_norm_w, w_branch_ssd, w_branch_gdn, w_out):
    b, l, _ = h.shape
    pad = CHUNK - N_META
    lp = l + pad
    proj = h @ w_in
    z, xbc, dt_raw, qkv, gate, a_raw, b_raw, merge_logits = jnp.split(proj, IN_SPLITS, axis=-1)
    valid = (jnp.arange(lp) >= pad).astype(h.dtype)[None, :, None]

    def front_pad(t):
        return jnp.pad(t, ((0, 0), (pad, 0), (0, 0)))

    xbc = jax.nn.silu(_causal_dwconv(front_pad(xbc), ssd_conv_w) + ssd_conv_b) * valid
    xs, bs, cs = jnp.split(xbc, [SSD_D_INNER, SSD_D_INNER + SSD_GROUPS * SSD_STATE], axis=-1)
    xs = xs.reshape(b, lp, SSD_HEADS, SSD_HEAD_DIM)
    dt = jax.nn.softplus(front_pad(dt_raw).astype(jnp.float32) + ssd_dt_bias.astype(jnp.float32))
    A = -jnp.exp(ssd_A_log.astype(jnp.float32))
    y = _ssd_chunked(xs, dt, A, bs.reshape(b, lp, SSD_GROUPS, SSD_STATE),
                     cs.reshape(b, lp, SSD_GROUPS, SSD_STATE)) + ssd_D[:, None] * xs
    y = y[:, pad:].reshape(b, l, SSD_D_INNER)
    y_ssd = _group_rmsnorm(y * jax.nn.silu(z), ssd_norm_w)

    qkv = jax.nn.silu(_causal_dwconv(front_pad(qkv), gdn_conv_w)) * valid
    q, k, v = jnp.split(qkv, [GDN_DQK, 2 * GDN_DQK], axis=-1)
    q = _l2norm(q.reshape(b, lp, GDN_HEADS, GDN_DK))
    k = _l2norm(k.reshape(b, lp, GDN_HEADS, GDN_DK))
    v = v.reshape(b, lp, GDN_HEADS, GDN_DV)
    g = -jnp.exp(gdn_A_log.astype(jnp.float32)) * jax.nn.softplus(
        front_pad(a_raw).astype(jnp.float32) + gdn_dt_bias.astype(jnp.float32))
    beta = jax.nn.sigmoid(front_pad(b_raw)) * valid
    o = _gated_delta_chunked(q, k, v, g, beta)[:, pad:]
    o = _rmsnorm(o, gdn_norm_w) * jax.nn.silu(gate).reshape(b, l, GDN_HEADS, GDN_DV)
    y_gdn = o.reshape(b, l, GDN_DVW)

    gate_ssd, gate_gdn = jnp.split(merge_logits, N_BRANCH, axis=-1)
    m = jax.nn.sigmoid(gate_ssd) * (y_ssd @ w_branch_ssd) + jax.nn.sigmoid(gate_gdn) * (y_gdn @ w_branch_gdn)
    return m @ w_out

def _peer(h, w_query, sub_keys, expert_down, expert_up):
    b, l, d = h.shape
    q = (h @ w_query).reshape(b, l, PEER_HEADS, 2, PEER_D_KEY)
    s = jnp.einsum("blhkd,knd->blhkn", q, sub_keys).astype(jnp.float32)
    top_s, top_i = lax.top_k(s, PEER_TOPK)
    cand_s = (top_s[..., 0, :, None] + top_s[..., 1, None, :]).reshape(b, l, PEER_HEADS, PEER_TOPK * PEER_TOPK)
    cand_i = (top_i[..., 0, :, None] * PEER_N_KEYS + top_i[..., 1, None, :]).reshape(b, l, PEER_HEADS, PEER_TOPK * PEER_TOPK)
    best_s, pos = lax.top_k(cand_s, PEER_TOPK)
    idx = jnp.take_along_axis(cand_i, pos, axis=-1)
    gates = jax.nn.softmax(best_s, axis=-1).astype(h.dtype)

    nb = l // PEER_POS_BLOCK

    def blocks(t):
        return jnp.moveaxis(t.reshape((b, nb, PEER_POS_BLOCK) + t.shape[2:]), 1, 0)

    def expert_block(args):
        hb, ib, gb = args
        act = jax.nn.gelu(jnp.einsum("btd,bthkd->bthk", hb, expert_down[ib]), approximate=False) * gb
        return jnp.einsum("bthk,bthkd->btd", act, expert_up[ib])

    out = lax.map(expert_block, (blocks(h), blocks(idx), blocks(gates)))
    return jnp.moveaxis(out, 0, 1).reshape(b, l, d)

def setup_inputs(seed: int = 0) -> dict:
    key = jax.random.key(seed)
    ks = jax.random.split(key, 24)
    f32 = jnp.float32

    def nrm(k, shape, scale):
        return jax.random.normal(k, shape, f32) * scale

    def gain(k, shape):
        return 1.0 + 0.02 * jax.random.normal(k, shape, f32)

    def dt_bias(k, shape):
        dt = jnp.exp(jax.random.uniform(k, shape, f32, minval=np.log(1e-3), maxval=np.log(1e-1)))
        return dt + jnp.log(-jnp.expm1(-dt))

    def a_log(k, shape):
        return jnp.log(jax.random.uniform(k, shape, f32, minval=1.0, maxval=16.0))

    return {
        "x": nrm(ks[0], (BATCH, SEQ, D_MODEL), 1.0),
        "meta_tokens": nrm(ks[1], (N_META, D_MODEL), 1.0),
        "norm_mix_w": gain(ks[2], (DEPTH, D_MODEL)),
        "w_in": nrm(ks[3], (DEPTH, D_MODEL, IN_DIM), D_MODEL ** -0.5),
        "ssd_conv_w": nrm(ks[4], (DEPTH, CONV_K, SSD_CONV_DIM), CONV_K ** -0.5),
        "ssd_conv_b": nrm(ks[5], (DEPTH, SSD_CONV_DIM), 0.02),
        "ssd_dt_bias": dt_bias(ks[6], (DEPTH, SSD_HEADS)),
        "ssd_A_log": a_log(ks[7], (DEPTH, SSD_HEADS)),
        "ssd_D": 1.0 + 0.1 * jax.random.normal(ks[8], (DEPTH, SSD_HEADS), f32),
        "ssd_norm_w": gain(ks[9], (DEPTH, SSD_D_INNER)),
        "gdn_conv_w": nrm(ks[10], (DEPTH, CONV_K, GDN_CONV_DIM), CONV_K ** -0.5),
        "gdn_dt_bias": dt_bias(ks[11], (DEPTH, GDN_HEADS)),
        "gdn_A_log": a_log(ks[12], (DEPTH, GDN_HEADS)),
        "gdn_norm_w": gain(ks[13], (DEPTH, GDN_DV)),
        "w_branch_ssd": nrm(ks[14], (DEPTH, SSD_D_INNER, D_MODEL), SSD_D_INNER ** -0.5),
        "w_branch_gdn": nrm(ks[15], (DEPTH, GDN_DVW, D_MODEL), GDN_DVW ** -0.5),
        "w_out": nrm(ks[16], (DEPTH, D_MODEL, D_MODEL), D_MODEL ** -0.5),
        "norm_ffn_w": gain(ks[17], (DEPTH, D_MODEL)),
        "peer_w_query": nrm(ks[18], (DEPTH, D_MODEL, PEER_HEADS * 2 * PEER_D_KEY), D_MODEL ** -0.5),
        "peer_sub_keys": nrm(ks[19], (DEPTH, 2, PEER_N_KEYS, PEER_D_KEY), PEER_D_KEY ** -0.5),
        "peer_expert_down": nrm(ks[20], (DEPTH, PEER_N_EXPERTS, D_MODEL), D_MODEL ** -0.5),
        "peer_expert_up": nrm(ks[21], (DEPTH, PEER_N_EXPERTS, D_MODEL), 0.5),
        "final_norm_w": gain(ks[22], (D_MODEL,)),
    }

def reference(x, meta_tokens, norm_mix_w, w_in, ssd_conv_w, ssd_conv_b, ssd_dt_bias, ssd_A_log, ssd_D,
              ssd_norm_w, gdn_conv_w, gdn_dt_bias, gdn_A_log, gdn_norm_w, w_branch_ssd, w_branch_gdn,
              w_out, norm_ffn_w, peer_w_query, peer_sub_keys, peer_expert_down, peer_expert_up,
              final_norm_w):
    b = x.shape[0]
    meta = jnp.broadcast_to(meta_tokens[None].astype(x.dtype), (b, N_META, D_MODEL))
    h = jnp.concatenate([meta, x], axis=1)
    for i in range(DEPTH):
        h = h + _hybrid_mixer(_rmsnorm(h, norm_mix_w[i]), w_in[i], ssd_conv_w[i], ssd_conv_b[i],
                              ssd_dt_bias[i], ssd_A_log[i], ssd_D[i], ssd_norm_w[i], gdn_conv_w[i],
                              gdn_dt_bias[i], gdn_A_log[i], gdn_norm_w[i], w_branch_ssd[i],
                              w_branch_gdn[i], w_out[i])
        h = h + _peer(_rmsnorm(h, norm_ffn_w[i]), peer_w_query[i], peer_sub_keys[i],
                      peer_expert_down[i], peer_expert_up[i])
    return _rmsnorm(h, final_norm_w)[:, N_META:]


_drawn_inputs = setup_inputs


def setup_inputs(seed=0):
    import zlib

    import numpy as np

    out = dict(_drawn_inputs(seed))
    spreads = {}
    factors = {}
    for name, (base, spread) in spreads.items():
        noise = np.random.default_rng([zlib.crc32(name.encode()), seed]).standard_normal(out[name].shape)
        drawn = base * np.exp(spread * noise) if base else spread * noise
        out[name] = __import__('jax').numpy.asarray(drawn.astype(out[name].dtype))
    for name, factor in factors.items():
        out[name] = (out[name] * factor).astype(out[name].dtype)
    return out
```

```python
import concourse.bass as bass
from concourse import mybir
from contextlib import ExitStack

F32 = mybir.dt.float32
U32 = mybir.dt.uint32
ALU = mybir.AluOpType
ACT = mybir.ActivationFunctionType
AX = mybir.AxisListType
ds = bass.ds

P = 128
D_MODEL = 2048
KT = D_MODEL // P
N_META = 16
SEQ = 256
L = N_META + SEQ
Q = 128
NC = 3
TC = NC * Q
PAD = TC - L
TAPS = 4
SSD_HEADS, SSD_HD, SSD_GROUPS, SSD_STATE = 32, 64, 4, 128
R = SSD_HEADS // SSD_GROUPS
XB = R * SSD_HD // P
GDN_HEADS, DK = 16, 128
PEER_HEADS, N_KEYS, TOPK = 8, 128, 16
HK = PEER_HEADS * TOPK
EPS = 1e-6
NEG = -1e30

SLOTS = 4
G_TILES, S_TILES, M_TILES, O_TILES, Q_TILES = 4, 2 + 2 * XB, 4, 16, 16
G_AT = 1
S_AT = G_AT + G_TILES * GDN_HEADS
M_AT = S_AT + S_TILES * SSD_GROUPS
O_AT = M_AT + M_TILES * KT
Q_AT = O_AT + O_TILES
N_TILES = Q_AT + Q_TILES


def slot_uses():
    base, at = {}, [1, 0, 0, 0]
    for name, per, times in (("G", 4, GDN_HEADS), ("S", S_TILES, SSD_GROUPS), ("M", 4, KT), ("O", 4, 4),
                             ("Q", 4, 4), ("D", 4, N_KEYS // 4), ("U", 4, N_KEYS // 4)):
        count = [len(range(s, per, SLOTS)) for s in range(SLOTS)]
        base[name] = (list(at), count)
        at = [a + c * times for a, c in zip(at, count)]
    return base


USES = slot_uses()


def use_no(segment, it, j):
    base, count = USES[segment]
    return base[j % SLOTS] + it * count[j % SLOTS] + j // SLOTS


def back(segment, j, after_s):
    if j >= SLOTS or not after_s:
        return SLOTS if (segment, j) != ("first", 0) else 1
    return 2 if j < 2 else 6


CONST = {}
_at = 0
for _name, _n in (("ident", P), ("ones", P), ("same16", P), ("level", 3 * P), ("below", P), ("upto", 2 * P),
                  ("iota", P), ("rank", TOPK), ("g_conv", 48 * TAPS), ("s_conv", 24 * TAPS), ("s_convb", 24), ("s_D", 16),
                  ("s_nw", 16), ("g_nw", 1), ("w_mix", 16), ("w_ffn", 16), ("w_fin", 16), ("dtb", 1),
                  ("alog", 1), ("eps", 1), ("keysT", 2 * N_KEYS)):
    CONST[_name] = (_at, _n)
    _at += _n
N_CONST = _at


def build(nc, xT_d, w_d, down_d, up_d, const_d, out_d):
    ctx = ExitStack()
    with ctx:
        N_ARENA = 52000
        arena = ctx.enter_context(nc.sbuf_tensor("arena", [P, N_ARENA], F32))
        banks = [ctx.enter_context(nc.psum_tensor(f"bank{i}", [P, 512], F32)) for i in range(8)]
        PA = banks[0:2]
        m = banks[2:8]
        gcs_d = nc.dram_tensor("gcs_scratch", [64, TC], F32, kind="Internal").ap()
        h2_d = nc.dram_tensor("h2_scratch", [P, KT * SEQ], F32, kind="Internal").ap()

        def sem(name):
            return ctx.enter_context(nc.semaphore(name))

        top = [0]

        def take(*shape, at=None):
            n = 1
            for s in shape:
                n *= s
            if at is not None:
                top[0] = at
            a = arena[:, top[0]:top[0] + n]
            top[0] += n
            assert top[0] <= N_ARENA, (top[0], shape)
            if len(shape) == 2:
                return a.rearrange("p (a b) -> p a b", b=shape[1])
            if len(shape) == 3:
                return a.rearrange("p (a b c) -> p a b c", b=shape[1], c=shape[2])
            if len(shape) == 4:
                return a.rearrange("p (a b c d) -> p a b c d", b=shape[1], c=shape[2], d=shape[3])
            return a

        const = take(N_CONST)
        C = {k: const[:, a:a + n] for k, (a, n) in CONST.items()}
        ident, ones, iota = C["ident"], C["ones"], C["iota"]
        level = C["level"].rearrange("p (a b) -> p a b", b=P)
        ring = take(SLOTS, KT * P)
        ringk = [ring[:, s, :].rearrange("p (k c) -> p k c", c=P) for s in range(SLOTS)]
        low_end = top[0]

        nT = take(KT, L)
        decay_rows = take(SSD_HEADS * 2 * Q)
        g_rows = decay_rows[:, 0:GDN_HEADS * TC].rearrange("p (h t) -> p h t", t=TC)
        s_rows = decay_rows[:, :].rearrange("p (h t) -> p h t", t=2 * Q)
        y_gdn = take(KT, SEQ)
        y_ssd = take(KT, SEQ)
        col_gcs, col_ngcs, col_te, col_dt, col_eg = (take(NC, 64) for _ in range(5))
        col_beta, col_nbeta, col_nbeg = (take(NC, 16) for _ in range(3))
        g_raw = take(3, TAPS - 1 + L)
        gate_raw = take(SEQ)
        s_raw = take(2 + XB, TAPS - 1 + L)
        z_raw = take(XB, SEQ)
        local = top[0]

        xT = take(KT, L, at=local)
        x_sq = take(KT, L)
        x_rn = take(L)
        rows = take(18, TC)
        cv = take(3, L, at=local)
        qkv = take(3, TC)
        qk_sq = take(2, L)
        qk_n = take(2, L)
        qk_rn = take(2, L)
        KN = take(NC, Q)
        QN = take(2, Q)
        QG = take(2, Q)
        EG = take(2, Q)
        GE = take(NC, Q)
        GT = take(2, Q)
        E = take(NC, Q)
        ET = take(2, Q)
        X = take(NC, Q)
        VB = take(NC, Q)
        KD = take(2, Q)
        AT = take(2, Q)
        B, BT, PP = take(NC, Q), take(NC, Q), take(NC, Q)
        LT = take(3, 2, Q)
        B2, B2T, B4, B4T, B8T = (take(NC, Q) for _ in range(5))
        T, TT = take(NC, Q), take(NC, Q)
        Y = take(2, Q)
        VN, RR, S = take(Q), take(Q), take(Q)
        gate_s, o_sq, o_n, o_rn = (take(SEQ) for _ in range(4))
        assert top[0] <= N_ARENA
        cv6 = take(2 + XB, L, at=local)
        xbc = take(2 + XB, TC)
        Btok = take(2, Q)
        XC = take(NC, R * SSD_HD)
        XE = take(2, R * SSD_HD)
        WE = take(R, 2 * Q)
        EC = take(R, 2 * Q)
        SS = take(2, R * SSD_HD)
        z_s = take(XB, SEQ)
        y_sq = take(XB, SEQ)
        decay_s = take(R)
        y_rn = take(SEQ)
        y_g = take(XB, SEQ)
        h_in = take(KT, SEQ, at=local)
        mT = take(KT, SEQ)
        m_sig = take(2, SEQ)
        m_mul = take(2, SEQ)
        h2, h2_sq = h_in, y_gdn
        nf = take(KT, SEQ, at=low_end)
        tab_hk = take(3, SEQ)
        f_rn = take(SEQ)
        gelu = take(2, SEQ)
        oh = take(2, 4, 2, P)
        gates_at = top[0]
        gates = take(N_KEYS, SEQ)
        tab_t = take(3, 2, HK, at=gates_at)
        qT = take(4, SEQ)
        sc = take(2, 4, N_KEYS)
        sc2 = take(4, N_KEYS)
        top_s, top_i = take(4, TOPK), take(4, TOPK)
        top_u = take(4 * TOPK).bitcast(U32).rearrange("p (a b) -> p a b", b=TOPK)
        cand = take(2, TOPK, TOPK)
        cand2 = take(2, TOPK * TOPK)
        best = take(2, TOPK)
        pos_u, pos_hi, pos_lo = (take(2 * TOPK).bitcast(U32).rearrange("p (a b) -> p a b", b=TOPK) for _ in range(3))
        pos_f = take(2, 2, TOPK)
        pick = take(2, 2 * TOPK, TOPK)
        soft = take(3, 2)
        ebest = take(2, TOPK)
        h3 = take(KT, SEQ, at=gates_at)
        h2b = take(KT, SEQ)
        h3_sq = take(KT, SEQ)
        h3_rn = take(SEQ)

        names = """const_in x_in tile_done w_in0 w_in1 w_in2 w_in3
            n_done z1 absz u_done w1 ln_done sp_part
            beta_rows negA csum te_rows eg_rows colps colcp colder gcs_out rows_in srows_in zeroed
            projev conv_tap silu_done gsilu gm_done e_done et_done eg_done
            qk_sqd qk_ss qk_std qk_rec qn_done kn_done vt_done kt_done kk_done qk_done vb_done kd_done
            x_done at_done xt_done b_done bt_done lt_done p1_done b2_done b2s_done b4_done b4s_done p2_done
            b8_done b8s_done p3_done pb8_done t0_done t0t_done t0ts_done y_done ys_done tn_done tu_done
            vn0_done vn0s_done s1_done s1s_done ks_done r_done vn_done vns_done su_done s2_done qg_done
            o_done osq_done on_done onstd_done onrec_done og_done
            norm_sq norm_ss norm_std norm_rec s_zero s_tap s_silu s_zsilu s_gm s_we s_ec s_dec s_cg s_bt s_btok s_xt s_cbt s_xc s_xe s_w s_s1 s_s1c
            s_su s_s2a s_s2 s_y s_yd s_yz s_ysq s_ss s_std s_rec s_out
            m_sigd m_muld m_out h_in_d h2_done nf_done h2_out
            q_copy sc_ps sc_cp r_top r_idx r_cast r_cand r_best r_pos r_bits r_pick r_mul r_neg r_neg2 r_exp
            r_gate t_ps t_cp oh_d oh_ps oh_cp d_gelu d_gate h2b_in h3_done
            out_done out_in""".split()
        K = {n: sem(n) for n in names}
        W_IN = [K[f"w_in{s}"] for s in range(SLOTS)]

        mm = nc.tensor.matmul
        tr = nc.tensor.transpose
        V = nc.vector
        A = nc.scalar.activation
        G = nc.gpsimd

        def is_first(n):
            return type(n) is int and n == 0

        def plus1(eng, n):
            return n + 1 if type(n) is int else eng.snap(n + 1)

        def bc(ap, shape):
            return ap.to_broadcast(shape)

        def quarters(step, n_tiles, steps):
            n = 4 * n_tiles
            return range(step * n // steps, (step + 1) * n // steps)

        def tiles_done(step, n_tiles, steps):
            return [q // 4 for q in quarters(step, n_tiles, steps) if q % 4 == 3]

        G_STEPS = 20
        S_STEPS = 7

        block = ctx.enter_context(nc.Block())

        @block.sync
        def _(sp):
            sp.dma_start(xT[:, :, :], xT_d).then_inc(K["x_in"], 16)
            sp.dma_start(const[:, :], const_d).then_inc(K["const_in"], 16)

            def load(segment, it, j, tile, first=False, after_s=False, src=None):
                if not first:
                    sp.wait_ge(K["tile_done"], tile - back(segment, j, after_s) + 1)
                sp.dma_start(ring[:, j % SLOTS, :], w_d[tile] if src is None else src.rearrange("o p n -> (o p) n")) \
                    .then_inc(W_IN[j % SLOTS], 16)

            sp.dma_start(ring[:, 0, :], w_d[0]).then_inc(W_IN[0], 16)
            for j in range(G_TILES):
                load("first", 0, j, G_AT + j, first=j > 0)
            sp.wait_ge(K["gcs_out"], 16)
            sp.dma_start(decay_rows[:, 0:GDN_HEADS * TC],
                         gcs_d[32:48, :].rearrange("h t -> (h t)").partition_broadcast(P)).then_inc(K["rows_in"], 16)
            with sp.Fori(1, GDN_HEADS) as h:
                for j in range(G_TILES):
                    load("G", h, j, G_AT + h * G_TILES + j)
            for j in range(SLOTS):
                load("S", 0, j, S_AT + j)
            sp.wait_ge(K["gm_done"], 2 * GDN_HEADS)
            sp.wait_ge(K["eg_done"], GDN_HEADS)
            sp.dma_start(s_rows, bc(gcs_d[0:SSD_HEADS, Q:TC].unsqueeze(0), [P, SSD_HEADS, 2 * Q])) \
                .then_inc(K["srows_in"], 16)
            for j in range(SLOTS, S_TILES):
                load("S", 0, j, S_AT + j)
            with sp.Fori(1, SSD_GROUPS) as g:
                for j in range(S_TILES):
                    load("S", g, j, S_AT + g * S_TILES + j, after_s=True)
            for j in range(SLOTS):
                load("M", 0, j, M_AT + j, after_s=True)
            with sp.Fori(1, KT) as n:
                for j in range(SLOTS):
                    load("M", n, j, M_AT + n * SLOTS + j)
            with sp.Fori(0, O_TILES // SLOTS) as n:
                for j in range(SLOTS):
                    load("O", n, j, O_AT + n * SLOTS + j)
            with sp.Fori(0, Q_TILES // SLOTS) as n:
                for j in range(SLOTS):
                    load("Q", n, j, Q_AT + n * SLOTS + j)
            with sp.Fori(0, N_KEYS // SLOTS) as n:
                for j in range(SLOTS):
                    load("D", n, j, N_TILES + n * SLOTS + j, src=down_d[ds(n * SLOTS + j, 1)])
            with sp.Fori(0, N_KEYS // SLOTS) as n:
                for j in range(SLOTS):
                    load("U", n, j, N_TILES + N_KEYS + n * SLOTS + j, src=up_d[ds(n * SLOTS + j, 1)])
        @block.tensor
        def _(pe):
            def project(segment, it, j, part, tokens, n_before, evac_before):
                s = j % SLOTS
                if part == 0:
                    pe.wait_ge(W_IN[s], 16 * (use_no(segment, it, j) + 1))
                    if evac_before:
                        pe.wait_ge(K["projev"], n_before)
                lo = 0 if tokens == L else N_META
                for k in range(4 * part, 4 * part + 4):
                    last = mm(PA[j % 2][:, 0:tokens], ringk[s][:, k, :], nT[:, k, lo:L],
                              start=(k == 0), stop=(k == KT - 1))
                if part == 3:
                    last.then_inc(K["tile_done"], 1)

            def project_g(h, q, first=False):
                j, part = q // 4, q % 4
                last = project("G", h, j, part, L if j < 3 else SEQ, h * G_TILES + j - 1,
                               not (first and j < 2))

            def project_s(g, q):
                j, part = q // 4, q % 4
                project("S", g, j, part, L if j < 2 + XB else SEQ, GDN_HEADS * G_TILES + g * S_TILES + j - 1, True)

            def mixer_g(h, fill):
                h1 = plus1(pe, h)
                w = pe.wait_ge
                w(K["qk_sqd"], h1)
                if not is_first(h):
                    w(K["og_done"], h)
                mm(m[0][:, 0:L], ones, qk_sq[:, 0, :], start=True, stop=True)
                mm(m[1][:, 0:L], ones, qk_sq[:, 1, :], start=True, stop=True).then_inc(K["qk_ss"], 1)
                for c in range(NC):
                    last = tr(m[2][:, c * Q:(c + 1) * Q], qkv[:, 2, c * Q:(c + 1) * Q], ident)
                last.then_inc(K["vt_done"], 1)
                fill(0)
                w(K["kn_done"], h1)
                for c in range(NC):
                    last = mm(m[4][:, c * Q:(c + 1) * Q], KN[:, c, :], KN[:, c, :], start=True, stop=True)
                last.then_inc(K["kk_done"], 1)
                w(K["qn_done"], h1)
                for c in range(2):
                    last = mm(m[5][:, c * Q:(c + 1) * Q], KN[:, c + 1, :], QN[:, c, :], start=True, stop=True)
                last.then_inc(K["qk_done"], 1)
                for c in range(2):
                    last = tr(m[3][:, c * Q:(c + 1) * Q], KN[:, c, :], ident)
                last.then_inc(K["kt_done"], 1)
                fill(1)
                w(K["x_done"], 3 * h1)
                for c in range(NC):
                    last = tr(m[0][:, c * Q:(c + 1) * Q], X[:, c, :], ident)
                last.then_inc(K["xt_done"], 1)
                fill(2)
                w(K["b_done"], h1)
                w(K["bt_done"], h1)
                w(K["vb_done"], h1)
                for c in range(NC):
                    mm(m[1][:, c * Q:(c + 1) * Q], BT[:, c, :], B[:, c, :], start=True, stop=True)
                    last = mm(m[2][:, c * Q:(c + 1) * Q], B[:, c, :], BT[:, c, :], start=True, stop=True)
                last.then_inc(K["b2_done"], 1)
                fill(3)
                w(K["b2s_done"], 2 * h1)
                w(K["lt_done"], 3 * h1)
                w(K["kd_done"], h1)
                w(K["p1_done"], h1)
                for c in range(NC):
                    mm(m[0][:, c * Q:(c + 1) * Q], B2T[:, c, :], B2[:, c, :], start=True, stop=True)
                    mm(m[3][:, c * Q:(c + 1) * Q], B2[:, c, :], B2T[:, c, :], start=True, stop=True)
                    last = mm(m[4][:, c * Q:(c + 1) * Q], B2T[:, c, :], PP[:, c, :], start=True, stop=True)
                last.then_inc(K["b4_done"], 1)
                fill(4)
                w(K["b4s_done"], 2 * h1)
                w(K["p2_done"], h1)
                for c in range(NC):
                    mm(m[1][:, c * Q:(c + 1) * Q], B4[:, c, :], B4T[:, c, :], start=True, stop=True)
                    last = mm(m[2][:, c * Q:(c + 1) * Q], B4T[:, c, :], PP[:, c, :], start=True, stop=True)
                last.then_inc(K["b8_done"], 1)
                fill(5)
                w(K["b8s_done"], h1)
                w(K["p3_done"], h1)
                for c in range(NC):
                    last = mm(m[0][:, c * Q:(c + 1) * Q], B8T[:, c, :], PP[:, c, :], start=True, stop=True)
                last.then_inc(K["pb8_done"], 1)
                fill(6)
                w(K["t0_done"], h1)
                for c in range(NC):
                    last = tr(m[3][:, c * Q:(c + 1) * Q], T[:, c, :], ident)
                last.then_inc(K["t0t_done"], 1)
                fill(7)
                w(K["t0ts_done"], h1)
                for c in range(2):
                    last = mm(m[1][:, c * Q:(c + 1) * Q], LT[:, 0, c, :], T[:, 1 + c, :], start=True, stop=True)
                last.then_inc(K["y_done"], 1)
                mm(m[4][:, 0:Q], TT[:, 0, :], VB[:, 0, :], start=True, stop=True).then_inc(K["vn0_done"], 1)
                fill(8)

                def both(bank, n):
                    w(K["ys_done"], 3 * h + n)
                    for c in range(2):
                        mm(bank[:, c * Q:(c + 1) * Q], TT[:, 1 + c, :], Y[:, c, :], start=True, stop=True)
                        x = mm(bank[:, (2 + c) * Q:(3 + c) * Q], Y[:, c, :], TT[:, 1 + c, :], start=True, stop=True)
                    x.then_inc(K["tn_done"], 1)

                both(m[2], 1)
                w(K["vn0s_done"], h1)
                w(K["at_done"], h1)
                mm(m[5][:, 0:Q], KD[:, 0, :], VN, start=True, stop=True).then_inc(K["s1_done"], 1)
                fill(9)
                w(K["tu_done"], 5 * h + 2)
                for c in range(2):
                    last = mm(m[0][:, c * Q:(c + 1) * Q], LT[:, 1, c, :], T[:, 1 + c, :], start=True, stop=True)
                last.then_inc(K["y_done"], 1)
                w(K["s1s_done"], h1)
                mm(m[4][:, 0:Q], KN[:, 1, :], S, start=True, stop=True).then_inc(K["ks_done"], 1)
                fill(10)
                both(m[3], 2)
                fill(11)
                w(K["tu_done"], 5 * h + 4)
                for c in range(2):
                    last = mm(m[1][:, c * Q:(c + 1) * Q], LT[:, 2, c, :], T[:, 1 + c, :], start=True, stop=True)
                last.then_inc(K["y_done"], 1)
                fill(12)
                w(K["ys_done"], 3 * h + 3)
                for c in range(2):
                    last = mm(m[2][:, c * Q:(c + 1) * Q], Y[:, c, :], TT[:, 1 + c, :], start=True, stop=True)
                last.then_inc(K["tn_done"], 1)
                fill(13)
                w(K["tu_done"], 5 * h + 5)
                w(K["r_done"], 2 * h + 1)
                mm(m[5][:, 0:Q], TT[:, 1, :], RR, start=True, stop=True).then_inc(K["vn_done"], 1)
                fill(14)
                w(K["vns_done"], 2 * h + 1)
                mm(m[0][:, 0:Q], KD[:, 1, :], VN, start=True, stop=True).then_inc(K["su_done"], 1)
                w(K["qg_done"], h1)
                mm(m[1][:, 0:Q], S, QG[:, 0, :], start=True, stop=False)
                mm(m[1][:, 0:Q], VN, AT[:, 0, :], start=False, stop=True).then_inc(K["o_done"], 1)
                fill(15)
                w(K["s2_done"], h1)
                mm(m[4][:, 0:Q], KN[:, 2, :], S, start=True, stop=True).then_inc(K["ks_done"], 1)
                fill(16)
                w(K["r_done"], 2 * h + 2)
                mm(m[5][:, 0:Q], TT[:, 2, :], RR, start=True, stop=True).then_inc(K["vn_done"], 1)
                fill(17)
                w(K["vns_done"], 2 * h + 2)
                mm(m[1][:, Q:2 * Q], S, QG[:, 1, :], start=True, stop=False)
                mm(m[1][:, Q:2 * Q], VN, AT[:, 1, :], start=False, stop=True).then_inc(K["o_done"], 1)
                fill(18)
                w(K["osq_done"], h1)
                mm(m[0][:, 0:SEQ], ones, o_sq, start=True, stop=True).then_inc(K["on_done"], 1)
                fill(19)

            pe.wait_ge(K["const_in"], 16)
            pe.wait_ge(K["norm_sq"], 1)
            for k in range(KT):
                last = mm(m[0][:, 0:L], ones, x_sq[:, k, :], start=(k == 0), stop=(k == KT - 1))
            last.then_inc(K["norm_ss"], 1)
            pe.wait_ge(W_IN[0], 16)
            pe.wait_ge(K["n_done"], KT)
            for k in range(KT):
                last = mm(m[1][:, 0:L], ringk[0][:, k, :], nT[:, k, :], start=(k == 0), stop=(k == KT - 1))
            last.then_inc(K["tile_done"], 1)
            for q in range(4 * G_TILES):
                project_g(0, q, first=True)
            for n, (src, key) in enumerate(((5, "csum"), (6, "te_rows"), (7, "sp_part"), (8, "eg_rows"), (9, "beta_rows"))):
                if n in (0, 1, 3):
                    pe.wait_ge(K[key], NC)
                elif n == 2:
                    pe.wait_ge(K[key], 9)
                else:
                    pe.wait_ge(K[key], 1)
                if n >= 2:
                    pe.wait_ge(K["colcp"], n - 1)
                for c in range(NC):
                    last = tr(m[2 + n % 2][:, c * 64:(c + 1) * 64],
                              rows[0:64, src, c * Q:(c + 1) * Q], ident[0:64, 0:64])
                last.then_inc(K["colps"], 1)

            mixer_g(0, lambda s: [project_g(1, q) for q in quarters(s, G_TILES, G_STEPS)])
            with pe.Fori(1, GDN_HEADS - 1) as h:
                mixer_g(h, lambda s: [project_g(h + 1, q) for q in quarters(s, G_TILES, G_STEPS)])
            mixer_g(GDN_HEADS - 1, lambda s: [project_s(0, q) for q in quarters(s, S_TILES, G_STEPS)])

            def group_s(g, fill):
                g1 = plus1(pe, g)
                w = pe.wait_ge
                fill(0)
                w(K["s_silu"], g1)
                if not is_first(g):
                    w(K["s_yd"], XB * g)
                for c in range(2):
                    last = tr(m[0][:, c * Q:(c + 1) * Q], xbc[:, 0, c * Q:(c + 1) * Q], ident)
                last.then_inc(K["s_bt"], 1)
                for c in range(NC):
                    for b in range(XB):
                        last = tr(m[1 + c][:, b * P:(b + 1) * P], xbc[:, 2 + b, c * Q:(c + 1) * Q], ident)
                    last.then_inc(K["s_xt"], 1)
                for c in range(2):
                    tok = slice((c + 1) * Q, (c + 2) * Q)
                    last = mm(m[4][:, c * Q:(c + 1) * Q], xbc[:, 0, tok], xbc[:, 1, tok], start=True, stop=True)
                last.then_inc(K["s_cbt"], 1)
                fill(1)
                w(K["s_btok"], g1)
                w(K["s_xe"], 2 * g + 1)
                if not is_first(g):
                    w(K["s_std"], g)
                mm(m[5][:, :], Btok[:, 0, :], XE[:, 0, :], start=True, stop=True).then_inc(K["s_s1"], 1)
                fill(2)
                w(K["s_xe"], 2 * g + 2)
                mm(m[0][:, :], Btok[:, 1, :], XE[:, 1, :], start=True, stop=True).then_inc(K["s_su"], 1)
                fill(3)
                for c in range(2):
                    if c == 0:
                        w(K["s_xc"], NC * g1)
                        w(K["s_s1c"], g1)
                        w(K["s_cg"], g1)
                    else:
                        w(K["s_s2"], g1)
                    w(K["s_w"], 2 * g1)
                    for b in range(XB):
                        for e in range(2):
                            r = 2 * b + e
                            rows_ = slice(e * SSD_HD, (e + 1) * SSD_HD)
                            ch = slice(r * SSD_HD, (r + 1) * SSD_HD)
                            tok = slice(c * Q, (c + 1) * Q)
                            mm(m[1 + b][rows_, tok], XC[:, 1 + c, ch], WE[:, r, tok], start=True, stop=False)
                            last = mm(m[1 + b][rows_, tok], SS[:, c, ch], EC[:, r, tok], start=False, stop=True)
                    last.then_inc(K["s_y"], 1)
                    fill(4 + c)
                w(K["s_ysq"], g1)
                for b in range(XB):
                    last = mm(m[5][:, 0:SEQ], ones, y_sq[:, b, :], start=(b == 0), stop=(b == XB - 1))
                last.then_inc(K["s_ss"], 1)
                fill(6)

            group_s(0, lambda s: [project_s(1, q) for q in quarters(s, S_TILES, S_STEPS)])
            with pe.Fori(1, SSD_GROUPS - 1) as g:
                group_s(g, lambda s: [project_s(g + 1, q) for q in quarters(s, S_TILES, S_STEPS)])
            group_s(SSD_GROUPS - 1, lambda s: None)

            def tile(segment, it, j, bank, moving):
                s = j % SLOTS
                pe.wait_ge(W_IN[s], 16 * (use_no(segment, it, j) + 1))
                for k in range(KT):
                    last = mm(bank[:, 0:SEQ], ringk[s][:, k, :], moving[:, k, :], start=(k == 0), stop=(k == KT - 1))
                last.then_inc(K["tile_done"], 1)

            n_tok = nT[:, :, N_META:L]
            m_banks = (PA[0], PA[1], m[0], m[1])
            pe.wait_ge(K["s_std"], SSD_GROUPS)

            def merge(n):
                for j in range(M_TILES):
                    if j == 0:
                        if is_first(n):
                            pe.wait_ge(K["projev"], GDN_HEADS * G_TILES + SSD_GROUPS * S_TILES)
                            pe.wait_ge(K["s_out"], SSD_HEADS // 2)
                        else:
                            pe.wait_ge(K["m_muld"], 2 * n - 1)
                    elif j == 2 and not is_first(n):
                        pe.wait_ge(K["m_muld"], 2 * n)
                    tile("M", n, j, m_banks[j], (y_ssd, n_tok, y_gdn, n_tok)[j])

            merge(0)
            with pe.Fori(1, KT) as n:
                merge(n)

            o_banks = (m[2], m[3], m[4], m[5])
            pe.wait_ge(K["m_out"], KT)

            def residual(n):
                for j in range(SLOTS):
                    if not is_first(n):
                        pe.wait_ge(K["h2_done"], SLOTS * n + j - 3)
                    tile("O", n, j, o_banks[j], mT)

            residual(0)
            with pe.Fori(1, O_TILES // SLOTS) as n:
                residual(n)
            pe.wait_ge(K["norm_sq"], 2)
            for k in range(KT):
                last = mm(m[0][:, 0:SEQ], ones, h2_sq[:, k, :], start=(k == 0), stop=(k == KT - 1))
            last.then_inc(K["norm_ss"], 1)
            pe.wait_ge(K["nf_done"], KT)

            def queries(n):
                for e in range(2):
                    for k in range(2):
                        j = 2 * e + k
                        tile("Q", n, j, (m[2], m[3], m[4], m[5])[j], nf)
                for e in range(2):
                    pe.wait_ge(K["q_copy"], 4 * n + 2 * e + 2)
                    if not is_first(n):
                        pe.wait_ge(K["sc_cp"], 2 * n + e - 1)
                    for k in range(2):
                        for half in range(2):
                            last = mm(PA[e][:, (2 * k + half) * N_KEYS:(2 * k + half + 1) * N_KEYS],
                                      qT[:, 2 * e + k, half * P:(half + 1) * P],
                                      C["keysT"][:, k * N_KEYS:(k + 1) * N_KEYS], start=True, stop=True)
                    last.then_inc(K["sc_ps"], 1)

            queries(0)
            with pe.Fori(1, Q_TILES // SLOTS) as n:
                queries(n)

            pe.wait_ge(K["r_pick"], 4 * PEER_HEADS)
            pe.wait_ge(K["r_gate"], 2 * PEER_HEADS)
            for f in range(3):
                for half in range(2):
                    last = tr(m[0 if f < 2 else 1][:, (2 * (f % 2) + half) * P:(2 * (f % 2) + half + 1) * P],
                              tab_t[:, f, half, :], ident)
            last.then_inc(K["t_ps"], 1)
            pe.wait_ge(K["t_cp"], 2)

            def spread(n):
                for e in range(2):
                    pe.wait_ge(K["oh_d"], 16 * n + 8 * e + 8)
                    if not is_first(n):
                        pe.wait_ge(K["oh_cp"], 2 * n + e - 1)
                    for u in range(4):
                        last = mm(m[2 + e][:, u * P:(u + 1) * P], oh[:, e, u, 1, :], oh[:, e, u, 0, :],
                                  start=True, stop=True)
                    last.then_inc(K["oh_ps"], 1)

            spread(0)
            with pe.Fori(1, SEQ // 8) as n:
                spread(n)

            def down(n):
                for j in range(SLOTS):
                    if not is_first(n):
                        pe.wait_ge(K["d_gelu"], SLOTS * n + j - 3)
                    elif j == 0:
                        pe.wait_ge(K["oh_cp"], SEQ // 4)
                    tile("D", n, j, m[2 + j], nf)

            down(0)
            with pe.Fori(1, N_KEYS // SLOTS) as n:
                down(n)

            pe.wait_ge(K["d_gate"], N_KEYS)

            def up(n):
                for j in range(SLOTS):
                    pe.wait_ge(W_IN[j], 16 * (use_no("U", n, j) + 1))
                    for d in range(KT):
                        last = mm(banks[d // 2][:, (d % 2) * SEQ:(d % 2 + 1) * SEQ], ring[:, j, d * P:(d + 1) * P],
                                  gates[:, n * SLOTS + j, :], start=(is_first(n) and j == 0 and d % 2 == 0),
                                  stop=False, skip_group_check=True)
                    last.then_inc(K["tile_done"], 1)

            up(0)
            with pe.Fori(1, N_KEYS // SLOTS) as n:
                up(n)
            pe.wait_ge(K["norm_sq"], 3)
            for k in range(KT):
                last = mm(banks[0][:, 0:SEQ], ones, h3_sq[:, k, :], start=(k == 0), stop=(k == KT - 1),
                          skip_group_check=True)
            last.then_inc(K["norm_ss"], 1)

        @block.scalar
        def _(act):
            act.wait_ge(K["x_in"], 16)
            A(x_sq[:, :, :], xT[:, :, :], ACT.Square).then_inc(K["norm_sq"], 1)
            act.wait_ge(K["const_in"], 16)
            act.wait_ge(K["norm_ss"], 1)
            A(x_rn, m[0][:, 0:L], ACT.Sqrt, bias=C["eps"], scale=1.0 / D_MODEL).then_inc(K["norm_std"], 1)
            act.wait_ge(K["z1"], 1)
            A(rows[0:64, 1, 0:L], rows[0:64, 0, 0:L], ACT.Abs).then_inc(K["absz"], 1)
            act.wait_ge(K["absz"], 1)
            A(rows[0:64, 2, 0:L], rows[0:64, 1, 0:L], ACT.Exp, scale=-1.0).then_inc(K["u_done"], 1)
            A(C["alog"][0:64, :], C["alog"][0:64, :], ACT.Exp).then_inc(K["negA"], 1)
            act.wait_ge(K["w1"], 1)
            A(rows[0:64, 4, 0:L], rows[0:64, 3, 0:L], ACT.Ln).then_inc(K["ln_done"], 1)
            act.wait_ge(K["zeroed"], 1)
            act.wait_ge(K["tile_done"], 1)
            A(rows[0:16, 9, PAD:TC], m[1][64:80, 0:L], ACT.Sigmoid).then_inc(K["beta_rows"], 1)
            act.wait_ge(K["csum"], NC)
            for c in range(NC):
                A(rows[0:64, 6, c * Q:(c + 1) * Q], rows[0:64, 5, c * Q:(c + 1) * Q], ACT.Exp, scale=-1.0,
                  bias=rows[0:64, 5, (c + 1) * Q - 1:(c + 1) * Q]).then_inc(K["te_rows"], 1)
                A(rows[0:64, 8, c * Q:(c + 1) * Q], rows[0:64, 5, c * Q:(c + 1) * Q], ACT.Exp) \
                    .then_inc(K["eg_rows"], 1)
            act.dma_start(gcs_d, rows[0:64, 5, :]).then_inc(K["gcs_out"], 16)

            def evac_g(h, j):
                act.wait_ge(K["tile_done"], G_AT + h * G_TILES + j + 1)
                if j < 3:
                    nc.scalar.copy(g_raw[:, j, TAPS - 1:], PA[j % 2][:, 0:L]).then_inc(K["projev"], 1)
                else:
                    nc.scalar.copy(gate_raw, PA[j % 2][:, 0:SEQ]).then_inc(K["projev"], 1)

            for j in range(G_TILES):
                evac_g(0, j)
            act.wait_ge(K["rows_in"], 16)
            act.wait_ge(K["colder"], 4)

            def mixer_g(h, evac):
                h1 = plus1(act, h)
                w = act.wait_ge
                w(K["gm_done"], 2 * h1)
                for c in range(NC):
                    A(E[:, c, :], GE[:, c, :], ACT.Exp, bias=col_gcs[:, c, ds(32 + h, 1)]).then_inc(K["e_done"], 1)
                for c in range(2):
                    A(ET[:, c, :], GT[:, c, :], ACT.Exp, bias=col_ngcs[:, 1 + c, ds(32 + h, 1)]) \
                        .then_inc(K["et_done"], 1)
                A(EG[:, :, :], g_rows[:, h, Q:TC].rearrange("p (c q) -> p c q", q=Q), ACT.Exp).then_inc(K["eg_done"], 1)
                w(K["conv_tap"], 3 * TAPS * h1)
                A(qkv[:, :, PAD:TC], cv[:, :, :], ACT.Silu).then_inc(K["silu_done"], 1)
                w(K["projev"], G_TILES * h1)
                if not is_first(h):
                    w(K["og_done"], h)
                A(gate_s, gate_raw, ACT.Silu).then_inc(K["gsilu"], 1)
                w(K["silu_done"], h1)
                A(qk_sq[:, :, :], qkv[:, 0:2, PAD:TC], ACT.Square).then_inc(K["qk_sqd"], 1)
                w(K["qk_ss"], h1)
                for i in range(2):
                    A(qk_n[:, i, :], m[i][:, 0:L], ACT.Sqrt, bias=C["eps"]).then_inc(K["qk_std"], 1)
                evac(0)
                evac(1)
                evac(2)
                w(K["b2_done"], h1)
                nc.scalar.copy(B2[:, :, :], m[1][:, 0:TC].rearrange("p (c q) -> p c q", q=Q)).then_inc(K["b2s_done"], 1)
                nc.scalar.copy(B2T[:, :, :], m[2][:, 0:TC].rearrange("p (c q) -> p c q", q=Q)).then_inc(K["b2s_done"], 1)
                evac(3)
                w(K["b4_done"], h1)
                nc.scalar.copy(B4[:, :, :], m[0][:, 0:TC].rearrange("p (c q) -> p c q", q=Q)).then_inc(K["b4s_done"], 1)
                nc.scalar.copy(B4T[:, :, :], m[3][:, 0:TC].rearrange("p (c q) -> p c q", q=Q)).then_inc(K["b4s_done"], 1)
                evac(4)
                w(K["b8_done"], h1)
                nc.scalar.copy(B8T[:, :, :], m[1][:, 0:TC].rearrange("p (c q) -> p c q", q=Q)).then_inc(K["b8s_done"], 1)
                evac(5)
                evac(6)
                w(K["t0t_done"], h1)
                nc.scalar.copy(TT[:, :, :], m[3][:, 0:TC].rearrange("p (c q) -> p c q", q=Q)).then_inc(K["t0ts_done"], 1)
                evac(7)

                def copy_y(bank, n):
                    w(K["y_done"], 3 * h + n)
                    nc.scalar.copy(Y[:, :, :], bank[:, 0:2 * Q].rearrange("p (c q) -> p c q", q=Q)) \
                        .then_inc(K["ys_done"], 1)

                copy_y(m[1], 1)
                evac(8)
                w(K["s1_done"], h1)
                nc.scalar.copy(S, m[5][:, 0:Q]).then_inc(K["s1s_done"], 1)
                evac(9)
                copy_y(m[0], 2)
                evac(10)
                evac(11)
                copy_y(m[1], 3)
                for s in range(12, 18):
                    evac(s)
                w(K["o_done"], 2 * h1)
                A(o_sq, m[1][:, 0:SEQ], ACT.Square).then_inc(K["osq_done"], 1)
                evac(18)
                w(K["on_done"], h1)
                A(o_n, m[0][:, 0:SEQ], ACT.Sqrt, bias=C["eps"], scale=1.0 / DK).then_inc(K["onstd_done"], 1)
                evac(19)

            mixer_g(0, lambda s: [evac_g(1, j) for j in tiles_done(s, G_TILES, G_STEPS)])
            with act.Fori(1, GDN_HEADS - 1) as h:
                mixer_g(h, lambda s: [evac_g(h + 1, j) for j in tiles_done(s, G_TILES, G_STEPS)])
            def evac_s(g, j):
                act.wait_ge(K["tile_done"], S_AT + g * S_TILES + j + 1)
                if j < 2 + XB:
                    nc.scalar.copy(s_raw[:, j, TAPS - 1:], PA[j % 2][:, 0:L]).then_inc(K["projev"], 1)
                else:
                    nc.scalar.copy(z_raw[:, j - 2 - XB, :], PA[j % 2][:, 0:SEQ]).then_inc(K["projev"], 1)

            mixer_g(GDN_HEADS - 1, lambda s: [evac_s(0, j) for j in tiles_done(s, S_TILES, G_STEPS)])
            act.wait_ge(K["srows_in"], 16)
            act.wait_ge(K["og_done"], GDN_HEADS)

            def group_s(g, evac):
                g1 = plus1(act, g)
                w = act.wait_ge
                if not is_first(g):
                    w(K["s_y"], 2 * g)
                A(EC[:, :, :], s_rows[:, ds(R * g, R), :], ACT.Exp).then_inc(K["s_ec"], 1)
                w(K["s_ec"], g1)
                if not is_first(g):
                    w(K["s_s2"], g)
                nc.scalar.copy(decay_s, EC[:, :, Q - 1]).then_inc(K["s_dec"], 1)
                w(K["s_gm"], g1)
                for r in range(R):
                    for c in range(2):
                        A(WE[:, r, c * Q:(c + 1) * Q], WE[:, r, c * Q:(c + 1) * Q], ACT.Exp,
                          bias=col_ngcs[:, 1 + c, ds(R * g + r, 1)]).then_inc(K["s_we"], 1)
                w(K["s_tap"], (2 + XB) * TAPS * g1)
                A(xbc[:, :, PAD:TC], cv6[:, :, :], ACT.Silu).then_inc(K["s_silu"], 1)
                w(K["projev"], GDN_HEADS * G_TILES + S_TILES * g1)
                A(z_s[:, :, :], z_raw[:, :, :], ACT.Silu).then_inc(K["s_zsilu"], 1)
                evac(0)
                w(K["s_bt"], g1)
                nc.scalar.copy(Btok[:, :, :], m[0][:, 0:2 * Q].rearrange("p (c q) -> p c q", q=Q)) \
                    .then_inc(K["s_btok"], 1)
                evac(1)
                w(K["s_s1"], g1)
                nc.scalar.copy(SS[:, 0, :], m[5][:, :]).then_inc(K["s_s1c"], 1)
                for s in range(2, 6):
                    evac(s)
                w(K["s_yz"], g1)
                A(y_sq[:, :, :], y_g[:, :, :], ACT.Square).then_inc(K["s_ysq"], 1)
                w(K["s_ss"], g1)
                A(y_rn, m[5][:, 0:SEQ], ACT.Sqrt, bias=C["eps"], scale=1.0 / (XB * P)).then_inc(K["s_std"], 1)
                evac(6)

            group_s(0, lambda s: [evac_s(1, j) for j in tiles_done(s, S_TILES, S_STEPS)])
            with act.Fori(1, SSD_GROUPS - 1) as g:
                group_s(g, lambda s: [evac_s(g + 1, j) for j in tiles_done(s, S_TILES, S_STEPS)])
            group_s(SSD_GROUPS - 1, lambda s: None)
            act.wait_ge(K["s_out"], SSD_HEADS // 2)
            act.dma_start(h_in[:, :, :], xT_d[:, :, N_META:L]).then_inc(K["h_in_d"], 16)

            def merge(n):
                if not is_first(n):
                    act.wait_ge(K["m_muld"], 2 * n)
                for i in range(2):
                    act.wait_ge(K["tile_done"], M_AT + n * M_TILES + 2 * i + 2)
                    A(m_sig[:, i, :], (PA[1], m[1])[i][:, 0:SEQ], ACT.Sigmoid).then_inc(K["m_sigd"], 1)

            merge(0)
            with act.Fori(1, KT) as n:
                merge(n)
            act.wait_ge(K["h2_done"], KT)
            A(h2_sq[:, :, :], h2[:, :, :], ACT.Square).then_inc(K["norm_sq"], 1)
            act.dma_start(h2_d, h2[:, :, :].rearrange("p k t -> p (k t)")).then_inc(K["h2_out"], 16)
            act.wait_ge(K["norm_ss"], 2)
            A(f_rn, m[0][:, 0:SEQ], ACT.Sqrt, bias=C["eps"], scale=1.0 / D_MODEL).then_inc(K["norm_std"], 1)

            def queries(n):
                for e in range(2):
                    if not is_first(n):
                        act.wait_ge(K["sc_ps"], 2 * n + e - 1)
                    for k in range(2):
                        j = 2 * e + k
                        act.wait_ge(K["tile_done"], Q_AT + n * SLOTS + j + 1)
                        nc.scalar.copy(qT[:, j, :], (m[2], m[3], m[4], m[5])[j][:, 0:SEQ]).then_inc(K["q_copy"], 1)
                for e in range(2):
                    for half in range(2):
                        act.wait_ge(K["r_neg"], 2 * (2 * n + e) + 2)
                        A(ebest[:, half, :], best[:, half, :], ACT.Exp, bias=soft[:, 0, half:half + 1],
                          accum_out=soft[:, 1, half:half + 1]).then_inc(K["r_exp"], 1)

            queries(0)
            with act.Fori(1, Q_TILES // SLOTS) as n:
                queries(n)

            def spread(n):
                for e in range(2):
                    act.wait_ge(K["oh_ps"], 2 * n + e + 1)
                    nc.scalar.copy(gates[:, :, ds(8 * n + 4 * e, 4)].rearrange("p i u -> p u i"),
                                   m[2 + e][:, :].rearrange("p (u i) -> p u i", i=P)).then_inc(K["oh_cp"], 1)

            act.wait_ge(K["t_cp"], 2)
            act.wait_ge(K["h2_out"], 16)
            spread(0)
            with act.Fori(1, SEQ // 8) as n:
                spread(n)

            def down(n):
                for j in range(SLOTS):
                    act.wait_ge(K["tile_done"], N_TILES + n * SLOTS + j + 1)
                    if not (is_first(n) and j < 2):
                        act.wait_ge(K["d_gate"], SLOTS * n + j - 1)
                    A(gelu[:, j % 2, :], m[2 + j][:, 0:SEQ], ACT.Gelu).then_inc(K["d_gelu"], 1)

            down(0)
            with act.Fori(1, N_KEYS // SLOTS) as n:
                down(n)
            act.wait_ge(K["tile_done"], N_TILES + 2 * N_KEYS)
            act.dma_start(h2b[:, :, :].rearrange("p k t -> p (k t)"), h2_d).then_inc(K["h2b_in"], 16)
            act.wait_ge(K["h3_done"], KT // 2)
            A(h3_sq[:, :, :], h3[:, :, :], ACT.Square).then_inc(K["norm_sq"], 1)
            act.wait_ge(K["norm_ss"], 3)
            A(h3_rn, banks[0][:, 0:SEQ], ACT.Sqrt, bias=C["eps"], scale=1.0 / D_MODEL).then_inc(K["norm_std"], 1)
            act.wait_ge(K["out_done"], KT)
            act.dma_start(out_d, h3[:, :, :].rearrange("p k t -> p (k t)")).then_inc(K["out_in"], 16)
            act.wait_ge(K["out_in"], 16)

        @block.vector
        def _(dve):
            V.memset(rows[0:64, 5:10, :], 0.0).then_inc(K["zeroed"], 1)
            V.memset(rows[0:64, 10, :], 0.0).then_inc(K["zeroed"], 1)
            V.memset(rows[0:64, 11, :], 1.0).then_inc(K["zeroed"], 1)
            V.memset(g_raw[:, :, 0:TAPS - 1], 0.0).then_inc(K["zeroed"], 1)
            V.memset(s_raw[:, :, 0:TAPS - 1], 0.0).then_inc(K["zeroed"], 1)
            dve.wait_ge(K["norm_std"], 1)
            V.reciprocal(x_rn, x_rn).then_inc(K["norm_rec"], 1)
            dve.wait_ge(K["norm_rec"], 1)
            for k in range(KT):
                V.scalar_tensor_tensor(out=nT[:, k, :], in0=xT[:, k, :], scalar=C["w_mix"][:, k:k + 1], in1=x_rn,
                                       op0=ALU.mult, op1=ALU.mult).then_inc(K["n_done"], 1)
            dve.wait_ge(K["tile_done"], 1)
            V.tensor_scalar(rows[0:64, 0, 0:L], m[1][0:64, 0:L], C["dtb"][0:64, :], None, ALU.add).then_inc(K["z1"], 1)
            dve.wait_ge(K["u_done"], 1)
            V.tensor_scalar(rows[0:64, 3, 0:L], rows[0:64, 2, 0:L], 1.0, None, ALU.add).then_inc(K["w1"], 1)
            sp = K["sp_part"]
            dve.wait_ge(K["w1"], 1)
            V.tensor_scalar(rows[0:64, 12, 0:L], rows[0:64, 3, 0:L], -1.0, None, ALU.add).then_inc(sp, 1)
            dve.wait_ge(sp, 1)
            V.tensor_tensor(rows[0:64, 13, 0:L], rows[0:64, 2, 0:L], rows[0:64, 12, 0:L], ALU.subtract).then_inc(sp, 1)
            V.reciprocal(rows[0:64, 14, 0:L], rows[0:64, 3, 0:L]).then_inc(sp, 1)
            dve.wait_ge(sp, 3)
            V.tensor_tensor(rows[0:64, 15, 0:L], rows[0:64, 13, 0:L], rows[0:64, 14, 0:L], ALU.mult).then_inc(sp, 1)
            dve.wait_ge(K["ln_done"], 1)
            dve.wait_ge(sp, 4)
            V.tensor_tensor(rows[0:64, 16, 0:L], rows[0:64, 4, 0:L], rows[0:64, 15, 0:L], ALU.add).then_inc(sp, 1)
            dve.wait_ge(sp, 5)
            dve.wait_ge(K["zeroed"], 5)
            V.scalar_tensor_tensor(out=rows[0:64, 7, PAD:TC], in0=rows[0:64, 0, 0:L], scalar=0.0,
                                   in1=rows[0:64, 16, 0:L], op0=ALU.max, op1=ALU.add).then_inc(sp, 1)
            dve.wait_ge(K["negA"], 1)
            V.tensor_scalar(C["alog"][0:64, :], C["alog"][0:64, :], -1.0, None, ALU.mult).then_inc(sp, 1)
            dve.wait_ge(sp, 7)
            V.tensor_scalar(rows[0:64, 10, PAD:TC], rows[0:64, 7, PAD:TC], C["alog"][0:64, :], None, ALU.mult) \
                .then_inc(sp, 1)
            dve.wait_ge(sp, 8)
            for c in range(NC):
                V.tensor_tensor_scan(out=rows[0:64, 5, c * Q:(c + 1) * Q], data0=rows[0:64, 11, c * Q:(c + 1) * Q],
                                     data1=rows[0:64, 10, c * Q:(c + 1) * Q], initial=0.0, op0=ALU.mult,
                                     op1=ALU.add).then_inc(K["csum"], 1)
            V.tensor_copy(rows[0:1, 17, 0:8], rows[0:1, 11, 0:8]).then_inc(sp, 1)
            for n, dst in enumerate((col_gcs, col_te, col_dt, col_eg)):
                dve.wait_ge(K["colps"], n + 1)
                V.tensor_copy(dst[:, :, :], m[2 + n % 2][:, 0:NC * 64].rearrange("p (c h) -> p c h", h=64)) \
                    .then_inc(K["colcp"], 1)
            dve.wait_ge(K["colps"], 5)
            V.tensor_copy(col_beta[:, :, :], m[2][:, 0:NC * 64].rearrange("p (c h) -> p c h", h=64)[:, :, 0:16]) \
                .then_inc(K["colcp"], 1)
            dve.wait_ge(K["colcp"], 5)
            V.tensor_scalar(col_ngcs[:, :, :], col_gcs[:, :, :], -1.0, None, ALU.mult).then_inc(K["colder"], 1)
            V.tensor_scalar(col_nbeta[:, :, :], col_beta[:, :, :], -1.0, None, ALU.mult).then_inc(K["colder"], 1)
            dve.wait_ge(K["colder"], 2)
            V.tensor_tensor(col_nbeg[:, :, :], col_nbeta[:, :, :], col_eg[:, :, 32:48], ALU.mult).then_inc(K["colder"], 1)
            V.memset(qkv[:, :, 0:PAD], 0.0).then_inc(K["colder"], 1)
            V.memset(KN[:, 0, :], 0.0).then_inc(K["colder"], 1)
            dve.wait_ge(K["colder"], 5)

            def conv(raw, n, weights, block_of, acc, out, done, bias=None):
                for tap in range(TAPS):
                    if tap:
                        dve.wait_ge(K[acc], done + n * tap)
                    for b in range(n):
                        wcol = weights[:, ds(block_of(b) * TAPS + tap, 1)]
                        src = raw[:, b, tap:tap + L]
                        if tap == 0:
                            V.tensor_scalar(out[:, b, :], src, wcol, None if bias is None else bias[:, ds(block_of(b), 1)],
                                            ALU.mult, ALU.bypass if bias is None else ALU.add).then_inc(K[acc], 1)
                        else:
                            V.scalar_tensor_tensor(out=out[:, b, :], in0=src, scalar=wcol, in1=out[:, b, :],
                                                   op0=ALU.mult, op1=ALU.add).then_inc(K[acc], 1)

            def three(bank, n=NC):
                return bank[:, 0:n * Q].rearrange("p (c q) -> p c q", q=Q)

            def mixer_g(h):
                h1 = plus1(dve, h)
                w = dve.wait_ge
                w(K["projev"], h * G_TILES + 3)
                conv(g_raw, 3, C["g_conv"], lambda b: b * GDN_HEADS + h, "conv_tap", cv, 3 * TAPS * h)
                w(K["qk_std"], 2 * h1)
                V.reciprocal(qk_rn[:, :, :], qk_n[:, :, :]).then_inc(K["qk_rec"], 1)
                w(K["qk_rec"], h1)
                V.tensor_tensor(arena_kn, qkv[:, 1, PAD:TC], qk_rn[:, 1, :], ALU.mult).then_inc(K["kn_done"], 1)
                V.scalar_tensor_tensor(out=QN[:, :, :], in0=three2(qkv[:, 0, Q:TC]), scalar=DK ** -0.5,
                                       in1=three2(qk_rn[:, 0, N_META:L]), op0=ALU.mult, op1=ALU.mult) \
                    .then_inc(K["qn_done"], 1)
                w(K["vt_done"], h1)
                V.tensor_tensor(VB[:, :, :], three(m[2]), bc(col_beta[:, :, ds(h, 1)], [P, NC, Q]), ALU.mult) \
                    .then_inc(K["vb_done"], 1)
                w(K["e_done"], 3 * h1)
                w(K["kk_done"], h1)
                for c in range(NC):
                    V.scalar_tensor_tensor(out=X[:, c, :], in0=m[4][:, c * Q:(c + 1) * Q],
                                           scalar=col_nbeta[:, c, ds(h, 1)], in1=E[:, c, :], op0=ALU.mult,
                                           op1=ALU.mult).then_inc(K["x_done"], 1)
                w(K["x_done"], 3 * h1)
                V.tensor_tensor(B[:, :, :], X[:, :, :], bc(C["same16"].unsqueeze(1), [P, NC, Q]), ALU.mult) \
                    .then_inc(K["b_done"], 1)
                w(K["qk_done"], h1)
                w(K["et_done"], 2 * h1)
                V.tensor_tensor(AT[:, :, :], three(m[5], 2), ET[:, :, :], ALU.mult).then_inc(K["at_done"], 1)
                w(K["kt_done"], h1)
                V.tensor_tensor(KD[:, :, :], three(m[3], 2), bc(col_te[:, 0:2, ds(32 + h, 1)], [P, 2, Q]), ALU.mult) \
                    .then_inc(K["kd_done"], 1)
                w(K["xt_done"], h1)
                V.tensor_tensor(BT[:, :, :], three(m[0]), bc(C["same16"].unsqueeze(1), [P, NC, Q]), ALU.mult) \
                    .then_inc(K["bt_done"], 1)
                w(K["b_done"], h1)
                V.tensor_tensor(PP[:, :, :], B[:, :, :], bc(ident.unsqueeze(1), [P, NC, Q]), ALU.add) \
                    .then_inc(K["p1_done"], 1)
                for n in range(3):
                    V.tensor_tensor(LT[:, n, :, :], m[0][:, Q:TC].rearrange("p (c q) -> p c q", q=Q),
                                    bc(level[:, n:n + 1, :], [P, 2, Q]), ALU.mult).then_inc(K["lt_done"], 1)
                w(K["b4_done"], h1)
                w(K["p1_done"], h1)
                V.tensor_tensor(PP[:, :, :], three(m[4]), PP[:, :, :], ALU.add).then_inc(K["p2_done"], 1)
                w(K["b8_done"], h1)
                w(K["p2_done"], h1)
                V.tensor_tensor(PP[:, :, :], three(m[2]), PP[:, :, :], ALU.add).then_inc(K["p3_done"], 1)
                w(K["pb8_done"], h1)
                w(K["p3_done"], h1)
                V.tensor_tensor(T[:, :, :], three(m[0]), PP[:, :, :], ALU.add).then_inc(K["t0_done"], 1)
                w(K["vn0_done"], h1)
                V.tensor_copy(VN, m[4][:, 0:Q]).then_inc(K["vn0s_done"], 1)

                def grow(bank, n):
                    w(K["tn_done"], 3 * h + n)
                    V.tensor_tensor(T[:, 1:3, :], bank[:, 0:2 * Q].rearrange("p (c q) -> p c q", q=Q), T[:, 1:3, :],
                                    ALU.add).then_inc(K["tu_done"], 1)
                    V.tensor_tensor(TT[:, 1:3, :], bank[:, 2 * Q:4 * Q].rearrange("p (c q) -> p c q", q=Q),
                                    TT[:, 1:3, :], ALU.add).then_inc(K["tu_done"], 1)

                w(K["t0_done"], h1)
                w(K["t0ts_done"], h1)
                grow(m[2], 1)
                w(K["ks_done"], 2 * h + 1)
                V.scalar_tensor_tensor(out=RR, in0=m[4][:, 0:Q], scalar=col_nbeg[:, 1, ds(h, 1)], in1=VB[:, 1, :],
                                       op0=ALU.mult, op1=ALU.add).then_inc(K["r_done"], 1)
                grow(m[3], 2)
                w(K["tn_done"], 3 * h + 3)
                V.tensor_tensor(TT[:, 1:3, :], m[2][:, 0:2 * Q].rearrange("p (c q) -> p c q", q=Q), TT[:, 1:3, :],
                                ALU.add).then_inc(K["tu_done"], 1)
                w(K["vn_done"], 2 * h + 1)
                V.tensor_copy(VN, m[5][:, 0:Q]).then_inc(K["vns_done"], 1)
                w(K["su_done"], h1)
                w(K["eg_done"], h1)
                w(K["o_done"], 2 * h + 1)
                V.scalar_tensor_tensor(out=S, in0=S, scalar=EG[:, 0, Q - 1:Q], in1=m[0][:, 0:Q], op0=ALU.mult,
                                       op1=ALU.add).then_inc(K["s2_done"], 1)
                w(K["ks_done"], 2 * h + 2)
                V.scalar_tensor_tensor(out=RR, in0=m[4][:, 0:Q], scalar=col_nbeg[:, 2, ds(h, 1)], in1=VB[:, 2, :],
                                       op0=ALU.mult, op1=ALU.add).then_inc(K["r_done"], 1)
                w(K["vn_done"], 2 * h + 2)
                V.tensor_copy(VN, m[5][:, 0:Q]).then_inc(K["vns_done"], 1)
                w(K["onstd_done"], h1)
                V.reciprocal(o_rn, o_n).then_inc(K["onrec_done"], 1)
                w(K["gsilu"], h1)
                w(K["onrec_done"], 2 * h + 1)
                V.scalar_tensor_tensor(out=o_rn, in0=o_rn, scalar=C["g_nw"], in1=gate_s, op0=ALU.mult,
                                       op1=ALU.mult).then_inc(K["onrec_done"], 1)
                w(K["onrec_done"], 2 * h + 2)
                V.tensor_tensor(y_gdn[:, h, :], m[1][:, 0:SEQ], o_rn, ALU.mult).then_inc(K["og_done"], 1)

            arena_kn = KN[:, :, :].rearrange("p c q -> p (c q)")[:, PAD:TC]

            def three2(ap):
                return ap.rearrange("p (c q) -> p c q", q=Q)

            mixer_g(0)
            with dve.Fori(1, GDN_HEADS) as h:
                mixer_g(h)
            V.memset(xbc[:, :, 0:PAD], 0.0).then_inc(K["s_zero"], 1)
            dve.wait_ge(K["s_zero"], 1)

            def group_s(g):
                g1 = plus1(dve, g)
                w = dve.wait_ge
                w(K["projev"], GDN_HEADS * G_TILES + g * S_TILES + 2 + XB)
                conv(s_raw, 2 + XB, C["s_conv"],
                     lambda b: (XB * SSD_GROUPS + SSD_GROUPS * b + g) if b < 2 else (XB * g + b - 2),
                     "s_tap", cv6, (2 + XB) * TAPS * g, bias=C["s_convb"])
                for c in range(NC):
                    w(K["s_xt"], NC * g + c + 1)
                    V.tensor_tensor(XC[:, c, :].rearrange("p (r d) -> p r d", d=SSD_HD),
                                    m[1 + c][:, :].rearrange("p (r d) -> p r d", d=SSD_HD),
                                    bc(col_dt[:, c, ds(R * g, R)].unsqueeze(2), [P, R, SSD_HD]), ALU.mult) \
                        .then_inc(K["s_xc"], 1)
                w(K["s_we"], 2 * R * g1)
                w(K["s_cbt"], g1)
                for c in range(2):
                    tok = slice(c * Q, (c + 1) * Q)
                    V.tensor_tensor(WE[:, :, tok], WE[:, :, tok], bc(m[4][:, tok].unsqueeze(1), [P, R, Q]),
                                    ALU.mult).then_inc(K["s_w"], 1)
                w(K["s_dec"], g1)
                w(K["s_s1c"], g1)
                V.tensor_tensor(SS[:, 1, :].rearrange("p (r d) -> p r d", d=SSD_HD),
                                SS[:, 0, :].rearrange("p (r d) -> p r d", d=SSD_HD),
                                bc(decay_s.unsqueeze(2), [P, R, SSD_HD]), ALU.mult).then_inc(K["s_s2a"], 1)
                w(K["s_s2a"], g1)
                w(K["s_su"], g1)
                V.tensor_tensor(SS[:, 1, :], m[0][:, :], SS[:, 1, :], ALU.add).then_inc(K["s_s2"], 1)
                w(K["s_y"], 2 * g1)
                for b in range(XB):
                    V.scalar_tensor_tensor(out=y_g[:, b, :], in0=xbc[:, 2 + b, Q:TC],
                                           scalar=C["s_D"][:, ds(XB * g + b, 1)], in1=m[1 + b][:, 0:SEQ],
                                           op0=ALU.mult, op1=ALU.add).then_inc(K["s_yd"], 1)
                w(K["s_yd"], XB * g1)
                w(K["s_zsilu"], g1)
                V.tensor_tensor(y_g[:, :, :], y_g[:, :, :], z_s[:, :, :], ALU.mult).then_inc(K["s_yz"], 1)
                w(K["s_std"], g1)
                V.reciprocal(y_rn, y_rn).then_inc(K["s_rec"], 1)
                w(K["s_rec"], g1)
                for b in range(XB):
                    V.scalar_tensor_tensor(out=y_ssd[:, XB * g + b, :], in0=y_g[:, b, :],
                                           scalar=C["s_nw"][:, ds(XB * g + b, 1)], in1=y_rn, op0=ALU.mult,
                                           op1=ALU.mult).then_inc(K["s_out"], 1)

            group_s(0)
            with dve.Fori(1, SSD_GROUPS) as g:
                group_s(g)

            def merge(n):
                n1 = plus1(dve, n)
                if not is_first(n):
                    dve.wait_ge(K["m_out"], n)
                for i in range(2):
                    dve.wait_ge(K["m_sigd"], 2 * n + i + 1)
                    V.tensor_tensor(m_mul[:, i, :], (PA[0], m[0])[i][:, 0:SEQ], m_sig[:, i, :], ALU.mult) \
                        .then_inc(K["m_muld"], 1)
                dve.wait_ge(K["m_muld"], 2 * n1)
                V.tensor_tensor(mT[:, n, :], m_mul[:, 0, :], m_mul[:, 1, :], ALU.add).then_inc(K["m_out"], 1)

            merge(0)
            with dve.Fori(1, KT) as n:
                merge(n)
            dve.wait_ge(K["h_in_d"], 16)
            o_banks = (m[2], m[3], m[4], m[5])
            with dve.Fori(0, O_TILES // SLOTS) as n:
                for j in range(SLOTS):
                    dve.wait_ge(K["tile_done"], O_AT + n * SLOTS + j + 1)
                    V.tensor_tensor(h2[:, n * SLOTS + j, :], h2[:, n * SLOTS + j, :], o_banks[j][:, 0:SEQ], ALU.add) \
                        .then_inc(K["h2_done"], 1)
            dve.wait_ge(K["norm_std"], 2)
            V.reciprocal(f_rn, f_rn).then_inc(K["norm_rec"], 1)
            dve.wait_ge(K["norm_rec"], 2)
            for k in range(KT):
                V.scalar_tensor_tensor(out=nf[:, k, :], in0=h2[:, k, :], scalar=C["w_ffn"][:, k:k + 1], in1=f_rn,
                                       op0=ALU.mult, op1=ALU.mult).then_inc(K["nf_done"], 1)

            def top16(values, spare, n, out_s, out_i, top_key, idx_key, done, ready, n_ready):
                def w(key, value):
                    dve.wait_ge(K[key], value)
                    V.memset(soft[:, 2, :], 0.0)

                w(ready, n_ready)
                for r in range(n):
                    V.max(out_s[:, r, 0:8], values[r]).then_inc(K[top_key], 1)
                w(top_key, done + n)
                for r in range(n):
                    V.match_replace(out=spare[r], in_to_replace=out_s[:, r, 0:8], in_values=values[r],
                                    imm_value=-3.0e38).then_inc(K[top_key], 1)
                for r in range(n):
                    V.max_index(out_i[:, r, 0:8], out_s[:, r, 0:8], values[r]).then_inc(K[idx_key], 1)
                w(top_key, done + 2 * n)
                for r in range(n):
                    V.max(out_s[:, r, 8:16], spare[r]).then_inc(K[top_key], 1)
                w(top_key, done + 3 * n)
                for r in range(n):
                    V.max_index(out_i[:, r, 8:16], out_s[:, r, 8:16], spare[r]).then_inc(K[idx_key], 1)

            def route(n, e):
                hd = 2 * n + e
                hd1 = plus1(dve, hd)
                w = dve.wait_ge
                w(K["sc_ps"], hd1)
                V.tensor_copy(sc[:, e, :, :], PA[e][:, :].rearrange("p (a b) -> p a b", b=N_KEYS)).then_inc(K["sc_cp"], 1)
                top16([sc[:, e, a, :] for a in range(4)], [sc2[:, a, :] for a in range(4)], 4, top_s, top_u,
                      "r_top", "r_idx", 12 * hd, "sc_cp", hd1)
                w(K["r_idx"], 8 * hd1)
                V.tensor_copy(top_i[:, :, :], top_u).then_inc(K["r_cast"], 1)
                for half in range(2):
                    V.tensor_tensor(cand[:, half, :, :], bc(top_s[:, half, :].unsqueeze(2), [P, TOPK, TOPK]),
                                    bc(top_s[:, 2 + half, :].unsqueeze(1), [P, TOPK, TOPK]), ALU.add) \
                        .then_inc(K["r_cand"], 1)
                top16([cand[:, a, :, :].rearrange("p a b -> p (a b)") for a in range(2)],
                      [cand2[:, a, :] for a in range(2)], 2, best, pos_u, "r_best", "r_pos", 6 * hd, "r_cand", 2 * hd1)
                for half in range(2):
                    V.tensor_scalar(soft[:, 0, half:half + 1], best[:, half, 0:1], -1.0, None, ALU.mult) \
                        .then_inc(K["r_neg"], 1)
                w(K["r_pos"], 4 * hd1)
                V.tensor_scalar(pos_hi, pos_u, 4, None, ALU.logical_shift_right).then_inc(K["r_bits"], 1)
                V.tensor_scalar(pos_lo, pos_u, 15, None, ALU.bitwise_and).then_inc(K["r_bits"], 1)
                w(K["r_bits"], 4 * hd + 2)
                V.tensor_copy(pos_f[:, 0, :, :], pos_hi).then_inc(K["r_bits"], 1)
                V.tensor_copy(pos_f[:, 1, :, :], pos_lo).then_inc(K["r_bits"], 1)
                w(K["r_bits"], 4 * hd + 4)
                w(K["r_cast"], hd1)
                for f in range(2):
                    V.tensor_tensor(pick[:, f, :, :],
                                    bc(pos_f[:, f, :, :].rearrange("p a b -> p (a b)").unsqueeze(2), [P, 2 * TOPK, TOPK]),
                                    bc(C["rank"].unsqueeze(1), [P, 2 * TOPK, TOPK]), ALU.is_equal) \
                        .then_inc(K["r_mul"], 1)
                w(K["r_mul"], 6 * hd + 2)
                for f in range(2):
                    for half in range(2):
                        V.tensor_tensor(pick[:, f, half * TOPK:(half + 1) * TOPK, :],
                                        pick[:, f, half * TOPK:(half + 1) * TOPK, :],
                                        bc(top_i[:, 2 * f + half, :].unsqueeze(1), [P, TOPK, TOPK]), ALU.mult) \
                            .then_inc(K["r_mul"], 1)
                w(K["r_mul"], 6 * hd1)
                for f in range(2):
                    for half in range(2):
                        V.tensor_reduce(tab_t[:, f, half, ds(hd * TOPK, TOPK)],
                                        pick[:, f, half * TOPK:(half + 1) * TOPK, :], AX.X, ALU.add) \
                            .then_inc(K["r_pick"], 1)
                w(K["r_exp"], 2 * hd1)
                V.reciprocal(soft[:, 2, :], soft[:, 1, :]).then_inc(K["r_neg2"], 1)
                w(K["r_neg2"], hd1)
                for half in range(2):
                    V.tensor_scalar(tab_t[:, 2, half, ds(hd * TOPK, TOPK)], ebest[:, half, :],
                                    soft[:, 2, half:half + 1], None, ALU.mult).then_inc(K["r_gate"], 1)

            for e in range(2):
                route(0, e)
            with dve.Fori(1, Q_TILES // SLOTS) as n:
                for e in range(2):
                    route(n, e)

            dve.wait_ge(K["t_ps"], 1)
            V.tensor_copy(tab_hk[:, 0:2, :], m[0][:, :].rearrange("p (f t) -> p f t", t=SEQ)).then_inc(K["t_cp"], 1)
            V.tensor_copy(tab_hk[:, 2, :], m[1][:, 0:SEQ]).then_inc(K["t_cp"], 1)
            dve.wait_ge(K["t_cp"], 2)

            def spread(n):
                for e in range(2):
                    if not is_first(n):
                        dve.wait_ge(K["oh_ps"], 2 * n + e - 1)
                    for u in range(4):
                        t = n * 8 + 4 * e + u
                        V.tensor_scalar(oh[:, e, u, 0, :], iota, tab_hk[:, 0, ds(t, 1)], None, ALU.is_equal) \
                            .then_inc(K["oh_d"], 1)
                        V.tensor_scalar(oh[:, e, u, 1, :], iota, tab_hk[:, 1, ds(t, 1)], tab_hk[:, 2, ds(t, 1)],
                                        ALU.is_equal, ALU.mult).then_inc(K["oh_d"], 1)

            spread(0)
            with dve.Fori(1, SEQ // 8) as n:
                spread(n)
            dve.wait_ge(K["oh_cp"], SEQ // 4)

            with dve.Fori(0, N_KEYS // SLOTS) as n:
                for j in range(SLOTS):
                    i = n * SLOTS + j
                    dve.wait_ge(K["d_gelu"], i + 1)
                    V.tensor_tensor(gates[:, i, :], gates[:, i, :], gelu[:, j % 2, :], ALU.mult) \
                        .then_inc(K["d_gate"], 1)
            dve.wait_ge(K["tile_done"], N_TILES + 2 * N_KEYS)
            dve.wait_ge(K["h2b_in"], 16)
            for b in range(KT // 2):
                V.tensor_tensor(h3[:, 2 * b:2 * b + 2, :], banks[b][:, :].rearrange("p (a t) -> p a t", t=SEQ),
                                h2b[:, 2 * b:2 * b + 2, :], ALU.add).then_inc(K["h3_done"], 1)
            dve.wait_ge(K["norm_std"], 3)
            V.reciprocal(h3_rn, h3_rn).then_inc(K["norm_rec"], 1)
            dve.wait_ge(K["norm_rec"], 3)
            for k in range(KT):
                V.scalar_tensor_tensor(out=h3[:, k, :], in0=h3[:, k, :], scalar=C["w_fin"][:, k:k + 1], in1=h3_rn,
                                       op0=ALU.mult, op1=ALU.mult).then_inc(K["out_done"], 1)

        @block.gpsimd
        def _(pool):
            pool.wait_ge(K["rows_in"], 16)
            pool.wait_ge(K["colder"], 5)

            def mixer_g(h):
                h1 = plus1(pool, h)
                if not is_first(h):
                    pool.wait_ge(K["eg_done"], h)
                rows3 = g_rows[:, h, :].rearrange("p (c q) -> p c q", q=Q)
                G.tensor_tensor(GE[:, :, :], bc(C["below"].unsqueeze(1), [P, NC, Q]), rows3, ALU.subtract) \
                    .then_inc(K["gm_done"], 1)
                G.tensor_tensor(GT[:, :, :], rows3[:, 1:3, :], C["upto"].rearrange("p (c q) -> p c q", q=Q), ALU.add) \
                    .then_inc(K["gm_done"], 1)
                pool.wait_ge(K["eg_done"], h1)
                pool.wait_ge(K["qn_done"], h1)
                G.tensor_tensor(QG[:, :, :], QN[:, :, :], EG[:, :, :], ALU.mult).then_inc(K["qg_done"], 1)

            mixer_g(0)
            with pool.Fori(1, GDN_HEADS) as h:
                mixer_g(h)
            pool.wait_ge(K["srows_in"], 16)
            pool.wait_ge(K["og_done"], GDN_HEADS)

            def group_s(g):
                g1 = plus1(pool, g)
                if not is_first(g):
                    pool.wait_ge(K["s_y"], 2 * g)
                G.tensor_tensor(WE[:, :, :], s_rows[:, ds(R * g, R), :], bc(C["upto"].unsqueeze(1), [P, R, 2 * Q]),
                                ALU.add).then_inc(K["s_gm"], 1)
                pool.wait_ge(K["s_dec"], g1)
                pool.wait_ge(K["s_silu"], g1)
                G.tensor_tensor(EC[:, :, :], EC[:, :, :], bc(xbc[:, 1:2, Q:TC], [P, R, 2 * Q]), ALU.mult) \
                    .then_inc(K["s_cg"], 1)
                for c in range(2):
                    pool.wait_ge(K["s_xc"], NC * g + c + 1)
                    G.tensor_tensor(XE[:, c, :].rearrange("p (r d) -> p r d", d=SSD_HD),
                                    XC[:, c, :].rearrange("p (r d) -> p r d", d=SSD_HD),
                                    bc(col_te[:, c, ds(R * g, R)].unsqueeze(2), [P, R, SSD_HD]), ALU.mult) \
                        .then_inc(K["s_xe"], 1)

            group_s(0)
            with pool.Fori(1, SSD_GROUPS) as g:
                group_s(g)


def layout(x, meta_tokens, norm_mix_w, w_in, ssd_conv_w, ssd_conv_b, ssd_dt_bias, ssd_A_log, ssd_D,
           ssd_norm_w, gdn_conv_w, gdn_dt_bias, gdn_A_log, gdn_norm_w, w_branch_ssd, w_branch_gdn,
           w_out, norm_ffn_w, peer_w_query, peer_sub_keys, peer_expert_down, peer_expert_up, final_norm_w):
    import numpy as np

    f = np.float32
    h = np.concatenate([np.asarray(meta_tokens), np.asarray(x)[0]], 0)
    xT = np.ascontiguousarray(h.T.reshape(KT, P, L).transpose(1, 0, 2))

    w = np.asarray(w_in)[0]
    d_inner, conv = SSD_HEADS * SSD_HD, SSD_HEADS * SSD_HD + 2 * SSD_GROUPS * SSD_STATE
    z0, x0 = 0, d_inner
    b0 = x0 + d_inner
    c0 = b0 + SSD_GROUPS * SSD_STATE
    dt0 = x0 + conv
    q0 = dt0 + SSD_HEADS
    k0, v0 = q0 + GDN_HEADS * DK, q0 + 2 * GDN_HEADS * DK
    gate0 = v0 + GDN_HEADS * DK
    a0 = gate0 + GDN_HEADS * DK
    bb0 = a0 + GDN_HEADS
    m0 = bb0 + GDN_HEADS
    stream = np.zeros((N_TILES, P, KT * P), f)

    def put(n, mat, col, width=P, at=0):
        stream[n].reshape(P, KT, P)[:, :, at:at + width] = \
            mat[:, col:col + width].reshape(KT, P, width).transpose(1, 0, 2)

    put(0, w, dt0, SSD_HEADS, 0)
    put(0, w, a0, GDN_HEADS, 32)
    put(0, w, bb0, GDN_HEADS, 64)
    for i in range(GDN_HEADS):
        for j, c in enumerate((q0, k0, v0, gate0)):
            put(G_AT + G_TILES * i + j, w, c + i * P)
    for g in range(SSD_GROUPS):
        put(S_AT + S_TILES * g, w, b0 + g * P)
        put(S_AT + S_TILES * g + 1, w, c0 + g * P)
        for b in range(XB):
            put(S_AT + S_TILES * g + 2 + b, w, x0 + (g * XB + b) * P)
            put(S_AT + S_TILES * g + 2 + XB + b, w, z0 + (g * XB + b) * P)
    ws, wg, wo, wq = (np.asarray(a)[0] for a in (w_branch_ssd, w_branch_gdn, w_out, peer_w_query))
    for n in range(KT):
        put(M_AT + M_TILES * n, ws, n * P)
        put(M_AT + M_TILES * n + 1, w, m0 + n * P)
        put(M_AT + M_TILES * n + 2, wg, n * P)
        put(M_AT + M_TILES * n + 3, w, m0 + D_MODEL + n * P)
        put(O_AT + n, wo, n * P)
        put(Q_AT + n, wq, n * P)

    down = np.asarray(peer_expert_down)[0].reshape(N_KEYS, P, KT, P)
    down = np.ascontiguousarray(down.transpose(0, 3, 2, 1)).reshape(N_KEYS, P, KT * P)
    up = np.ascontiguousarray(np.asarray(peer_expert_up)[0].reshape(N_KEYS, P, D_MODEL))

    c = np.zeros((P, N_CONST), f)

    def const(name, a):
        at, n = CONST[name]
        a = np.asarray(a).reshape(-1, n)
        c[0:len(a), at:at + n] = a

    i = np.arange(P)
    const("ident", i[:, None] == i)
    const("ones", np.ones((P, P)))
    const("same16", (i[:, None] // 16) == (i // 16))
    const("level", np.concatenate([((i[:, None] // (2 * s)) == (i // (2 * s))) & ((i[:, None] // s) != (i // s))
                                   for s in (16, 32, 64)], 1))
    const("below", np.where(i[:, None] > i, 0.0, NEG))
    const("upto", np.tile(np.where(i[:, None] <= i, 0.0, NEG), (1, 2)))
    const("iota", np.tile(i, (P, 1)))
    const("rank", np.tile(np.arange(TOPK), (P, 1)))

    def blocks(a):
        t = a.shape[0]
        return a.reshape(t, -1, P).transpose(2, 1, 0).reshape(P, -1)

    const("g_conv", blocks(np.asarray(gdn_conv_w)[0]))
    const("s_conv", blocks(np.asarray(ssd_conv_w)[0]))
    const("s_convb", blocks(np.asarray(ssd_conv_b)))
    const("s_D", blocks(np.repeat(np.asarray(ssd_D)[0], SSD_HD)[None]))
    const("s_nw", blocks(np.asarray(ssd_norm_w)))
    const("g_nw", np.asarray(gdn_norm_w)[0])
    const("w_mix", blocks(np.asarray(norm_mix_w)))
    const("w_ffn", blocks(np.asarray(norm_ffn_w)))
    const("w_fin", blocks(np.asarray(final_norm_w)[None]))
    const("dtb", np.concatenate([np.asarray(ssd_dt_bias)[0], np.asarray(gdn_dt_bias)[0]]))
    const("alog", np.concatenate([np.asarray(ssd_A_log)[0], np.asarray(gdn_A_log)[0]]))
    const("eps", np.full((P, 1), EPS))
    const("keysT", np.asarray(peer_sub_keys)[0].transpose(2, 0, 1).reshape(P, -1))
    return xT, stream, down, up, c


def kernel(**inputs):
    import numpy as np
    import concourse.bacc as bacc
    from concourse.bass_utils import run_bass_kernel_spmd as run

    nc = bacc.Bacc("TRN2", target_bir_lowering=False, num_devices=1)
    names = ("xT", "w_stream", "down", "up", "const")
    arrays = dict(zip(names, layout(**inputs)))
    args = [nc.dram_tensor(n, arrays[n].shape, F32, kind="ExternalInput").ap() for n in names]
    out = nc.dram_tensor("out", (P, KT * SEQ), F32, kind="ExternalOutput").ap()
    build(nc, *args, out)
    r = run(nc, [arrays], core_ids=[0])
    o = r.results[0]["out"].reshape(P, KT, SEQ)
    return np.ascontiguousarray(o.transpose(2, 1, 0)).reshape(1, SEQ, D_MODEL)
```

```python
import concourse.bass as bass
from concourse import mybir
from contextlib import ExitStack

F32 = mybir.dt.float32
F32R = mybir.dt.float32r
U32 = mybir.dt.uint32
ALU = mybir.AluOpType
ACT = mybir.ActivationFunctionType
AX = mybir.AxisListType
ds = bass.ds

P = 128
D_MODEL = 2048
KT = D_MODEL // P
N_META = 16
SEQ = 256
L = N_META + SEQ
Q = 128
NC = 3
TC = NC * Q
PAD = TC - L
TAPS = 4
SSD_HEADS, SSD_HD, SSD_GROUPS, SSD_STATE = 32, 64, 4, 128
R = SSD_HEADS // SSD_GROUPS
XB = R * SSD_HD // P
GDN_HEADS, DK = 16, 128
PEER_HEADS, N_KEYS, TOPK = 8, 128, 16
HK = PEER_HEADS * TOPK
EPS = 1e-6
NEG = -1e30

G_TILES, S_TILES, M_TILES, O_TILES, Q_TILES = 4, 2 + 2 * XB, 4, 16, 16
ROUND = 4
G_AT = 1
S_AT = G_AT + G_TILES * GDN_HEADS
M_AT = S_AT + S_TILES * SSD_GROUPS
O_AT = M_AT + M_TILES * KT
Q_AT = O_AT + O_TILES
N_TILES = Q_AT + Q_TILES
D_AT, U_AT = N_TILES, N_TILES + N_KEYS
END = U_AT + N_KEYS
SEGMENTS = {"G": (G_AT, G_TILES), "S": (S_AT, S_TILES), "M": (M_AT, ROUND), "O": (O_AT, ROUND),
            "Q": (Q_AT, ROUND), "D": (D_AT, ROUND), "U": (U_AT, ROUND)}
QT = KT // 4
QW = QT * P
HALVES = 4


def tile_no(segment, it, j):
    at, per = SEGMENTS[segment]
    return at + j + per * it


def half_slot(segment, j, half):
    return (2 * (SEGMENTS[segment][0] + j) + half) % HALVES


def half_use(segment, it, j, half):
    at, per = SEGMENTS[segment]
    return (2 * (at + j) + half) // HALVES + (per // 2) * it


G_FILL = (3, 3, 1, 1, 1, 1, 1, 1, 1, 1, 1, 1, 0, 0, 0, 0, 0, 0, 0, 0, 0)
G_FILL_LAST = (5, 5, 2, 2, 2, 2, 2, 2, 2, 2, 1, 1, 1, 1, 1, 2, 1, 2, 2, 1, 1)
S_FILL = (8, 6, 4, 6, 6, 4, 4, 2)
assert sum(G_FILL) == 4 * G_TILES and sum(G_FILL_LAST) == sum(S_FILL) == 4 * S_TILES


def filled(fill, n):
    before = sum(fill[:n])
    return range(before, before + fill[n])


CONST = {}
_at = 0
for _name, _n in (("ident", P), ("ones", P), ("same16", P), ("level", 3 * P), ("below", P), ("upto", 2 * P),
                  ("iota", P), ("rank", TOPK), ("g_conv", 48 * TAPS), ("s_conv", 24 * TAPS), ("s_convb", 24), ("s_D", 16),
                  ("s_nw", 16), ("g_nw", 1), ("w_mix", 16), ("w_ffn", 16), ("w_fin", 16), ("dtb", 1),
                  ("alog", 1), ("eps", 1), ("keysT", 2 * N_KEYS)):
    CONST[_name] = (_at, _n)
    _at += _n
N_CONST = _at


def build(nc, xT_d, w_d, down_d, up_d, const_d, out_d):
    ctx = ExitStack()
    with ctx:
        N_ARENA = 44608
        ring = ctx.enter_context(nc.sbuf_tensor("ring", [P, HALVES, 2 * QW], F32))
        hi = ctx.enter_context(nc.sbuf_tensor("w_hi", [P, 4, QW], F32R))
        w_hi_at = nc.sbuf_base - 4 * 4 * QW
        lo = ctx.enter_context(nc.sbuf_tensor("w_lo", [P, 4, QW], F32R))
        arena = ctx.enter_context(nc.sbuf_tensor("arena", [P, N_ARENA], F32))
        base = nc.sbuf_base - 4 * N_ARENA
        banks = [ctx.enter_context(nc.psum_tensor(f"bank{i}", [P, 512], F32)) for i in range(8)]
        PA = banks[0:2]
        m = banks[2:8]
        gcs_d = nc.dram_tensor("gcs_scratch", [64, TC], F32, kind="Internal").ap()
        h2_d = nc.dram_tensor("h2_scratch", [P, KT * SEQ], F32, kind="Internal").ap()

        def sem(name):
            return ctx.enter_context(nc.semaphore(name))

        top = [0]

        def take(*shape, at=None):
            n = 1
            for s in shape:
                n *= s
            if at is not None:
                top[0] = at
            a = arena[:, top[0]:top[0] + n]
            top[0] += n
            assert top[0] <= N_ARENA, (top[0], shape)
            if len(shape) == 2:
                return a.rearrange("p (a b) -> p a b", b=shape[1])
            if len(shape) == 3:
                return a.rearrange("p (a b c) -> p a b c", b=shape[1], c=shape[2])
            if len(shape) == 4:
                return a.rearrange("p (a b c d) -> p a b c d", b=shape[1], c=shape[2], d=shape[3])
            return a

        def in_parts(name, at, *shape):
            n = shape[0] * shape[1]
            return [nc.alloc_sbuf_tensor_at(f"{name}_{part}", [P, *shape], F32R, offset=base + 4 * (at + n * i))[:, :, :]
                    for i, part in enumerate(("hi", "lo"))]

        const = take(N_CONST)
        take(-N_CONST % 8)
        C = {k: const[:, a:a + n] for k, (a, n) in CONST.items()}
        ident, ones, iota = C["ident"], C["ones"], C["iota"]
        level = C["level"].rearrange("p (a b) -> p a b", b=P)
        low_end = top[0]

        n_hl = in_parts("n", low_end, KT, L)
        take(2 * KT, L)
        g_row = take(NC, Q)
        s_row = take(R, 2 * Q)
        y_at = top[0]
        y_gdn = take(KT, SEQ)
        y_ssd = take(KT, SEQ)
        col_gcs, col_ngcs, col_te, col_dt, col_eg = (take(NC, 64) for _ in range(5))
        col_beta, col_nbeta, col_nbeg = (take(NC, 16) for _ in range(3))
        raw_at = top[0]
        g_raw = take(3, TAPS - 1 + L)
        gate_raw = take(SEQ)
        s_raw = take(2 + XB, TAPS - 1 + L)
        z_raw = take(XB, SEQ)
        local = top[0] + -top[0] % 8

        xT = take(KT, L, at=local)
        x_sq = take(KT, L)
        x_rn = take(L)
        rows = take(18, TC)
        cv = take(3, L, at=local)
        qkv = take(3, TC)
        qk_sq = take(2, L)
        qk_n = take(2, L)
        qk_rn = take(2, L)
        KN = take(NC, Q)
        QN = take(2, Q)
        QG = take(2, Q)
        EG = take(2, Q)
        GE = take(NC, Q)
        GT = take(2, Q)
        E = take(NC, Q)
        ET = take(2, Q)
        X = take(NC, Q)
        VB = take(NC, Q)
        KD = take(2, Q)
        AT = take(2, Q)
        B, BT, PP = take(NC, Q), take(NC, Q), take(NC, Q)
        LT = take(3, 2, Q)
        B2, B2T, B4, B4T, B8T = (take(NC, Q) for _ in range(5))
        T, TT = take(NC, Q), take(NC, Q)
        Y = take(2, Q)
        VN, RR, S = take(Q), take(Q), take(Q)
        gate_s, o_sq, o_n, o_rn = (take(SEQ) for _ in range(4))
        assert top[0] <= N_ARENA
        cv6 = take(2 + XB, L, at=local)
        xbc = take(2 + XB, TC)
        Btok = take(2, Q)
        XC = take(NC, R * SSD_HD)
        XE = take(2, R * SSD_HD)
        WE = take(R, 2 * Q)
        EC = take(R, 2 * Q)
        SS = take(2, R * SSD_HD)
        z_s = take(XB, SEQ)
        y_sq = take(XB, SEQ)
        decay_s = take(R)
        y_rn = take(SEQ)
        y_g = take(XB, SEQ)
        y_hl = [in_parts(f"y{i}", local + 2 * KT * SEQ * i, KT, SEQ) for i in range(2)]
        take(4 * KT, SEQ, at=local)
        m_hl = in_parts("m", y_at, KT, SEQ)
        m_sig = take(2, SEQ, at=raw_at)
        m_mul = take(3, SEQ)
        h_in = take(KT, SEQ, at=local)
        h2, h2_sq = h_in, take(KT, SEQ)
        nf = in_parts("nf", low_end, KT, SEQ)
        a_hl = in_parts("a", low_end, 2, SEQ)
        oh = nc.alloc_sbuf_tensor_at("one_hots", [P, 2, 4, 2, P], F32, offset=w_hi_at)
        take(2 * KT, SEQ, at=low_end)
        tab_hk = take(3, SEQ)
        f_rn = take(SEQ)
        gelu = take(2, SEQ)
        gates_at = top[0]
        gates = take(N_KEYS, SEQ)
        tab_t = take(3, 2, HK, at=gates_at)
        qT = take(4, SEQ)
        sc = take(2, 4, N_KEYS)
        sc2 = take(4, N_KEYS)
        top_s, top_i = take(4, TOPK), take(4, TOPK)
        top_u = take(4 * TOPK).bitcast(U32).rearrange("p (a b) -> p a b", b=TOPK)
        cand = take(2, TOPK, TOPK)
        cand2 = take(2, TOPK * TOPK)
        best = take(2, TOPK)
        pos_u, pos_hi, pos_lo = (take(2 * TOPK).bitcast(U32).rearrange("p (a b) -> p a b", b=TOPK) for _ in range(3))
        pos_f = take(2, 2, TOPK)
        pick = take(2, 2 * TOPK, TOPK)
        soft = take(3, 2)
        ebest = take(2, TOPK)
        h3 = take(KT, SEQ, at=gates_at)
        h2b = take(KT, SEQ)
        h3_sq = take(KT, SEQ)
        h3_rn = take(SEQ)

        names = """const_in x_in quarter_done cut_h cut_l x_hi x_lo m_lo a_hi a_lo w_in0 w_in1 w_in2 w_in3
            normed sp_act sp_part
            beta_rows csum row_exps colps colcp colder gcs_out rows_in srows_in zeroed
            projev conv_tap silu_done gsilu gm_done e_done et_done eg_done
            qk_sqd qk_ss qk_std qk_rec qn_done kn_done vt_done kt_done kk_done qk_done vb_done kd_done
            x_done at_done xt_done b_done bt_done lt_done p1_done b2_done b2s_done b4_done b4s_done p2_done
            b8_done b8s_done p3_done pb8_done t0_done t0t_done t0ts_done y_done ys_done tn_done tu_done
            vn0_done vn0s_done s1_done s1s_done ks_done r_done vn_done vns_done su_done s2_done qg_done
            o_done osq_done on_done onstd_done onrec_done og_done
            norm_sq norm_ss norm_std norm_rec s_zero s_tap s_silu s_zsilu s_gm s_we s_ec s_dec s_cg s_bt s_btok s_xt s_cbt s_xc s_xe s_w s_s1 s_s1c
            s_su s_s2a s_s2 s_y s_yd s_yz s_ysq s_ss s_std s_rec s_out
            m_sigd m_muld m_out h_moved h2_done
            q_copy sc_ps sc_cp r_top r_idx r_cast r_cand r_best r_pos r_bits r_pick r_mul r_neg r_neg2 r_exp
            r_gate t_ps t_cp oh_d oh_ps oh_cp d_gelu d_gate h3_done
            out_done out_in""".split()
        K = {n: sem(n) for n in names}
        W_IN = [K[f"w_in{s}"] for s in range(HALVES)]

        mm = nc.tensor.matmul
        tr = nc.tensor.transpose
        V = nc.vector
        A = nc.scalar.activation
        G = nc.gpsimd

        def is_first(n):
            return type(n) is int and n == 0

        def plus1(eng, n):
            return n + 1 if type(n) is int else eng.snap(n + 1)

        def bc(ap, shape):
            return ap.to_broadcast(shape)

        def cuts(cut, segment, it, fill, n):
            for q in filled(fill, n):
                cut(segment, it, (q + 4) // 4, (q + 4) % 4)

        block = ctx.enter_context(nc.Block())

        @block.sync
        def _(sp):
            sp.dma_start(xT[:, :, :], xT_d).then_inc(K["x_in"], 16)
            sp.dma_start(const[:, :], const_d).then_inc(K["const_in"], 16)

            def load(segment, it, j, src=None):
                t = tile_no(segment, it, j)
                for half in range(2):
                    if not (type(t) is int and t < HALVES // 2):
                        sp.wait_ge(K["cut_l"], 4 * t + 2 * half - 6)
                    w = w_d[t] if src is None else src.rearrange("o p n -> (o p) n")
                    slot = half_slot(segment, j, half)
                    sp.dma_start(ring[:, slot, :], w[:, half * 2 * QW:(half + 1) * 2 * QW]).then_inc(W_IN[slot], 16)

            load("G", 0, -1)
            for j in range(G_TILES):
                load("G", 0, j)
            with sp.Fori(1, GDN_HEADS) as h:
                for j in range(G_TILES):
                    load("G", h, j)
            with sp.Fori(0, SSD_GROUPS) as g:
                for j in range(S_TILES):
                    load("S", g, j)
            with sp.Fori(0, KT) as n:
                for j in range(ROUND):
                    load("M", n, j)
            for segment, tiles in (("O", O_TILES), ("Q", Q_TILES)):
                with sp.Fori(0, tiles // ROUND) as n:
                    for j in range(ROUND):
                        load(segment, n, j)
            for segment, table in (("D", down_d), ("U", up_d)):
                with sp.Fori(0, N_KEYS // ROUND) as n:
                    for j in range(ROUND):
                        load(segment, n, j, src=table[ds(n * ROUND + j, 1)])

        @block.tensor
        def _(pe):
            def quarter(segment, it, j, part, out, moving, tokens=slice(None)):
                q = 4 * tile_no(segment, it, j) + part
                pe.wait_ge(K["cut_l"], q + 1)
                for k in range(QT):
                    kk = part * QT + k
                    w = slice(k * P, (k + 1) * P)
                    x_hi, x_lo = moving[0][:, kk, tokens], moving[1][:, kk, tokens]
                    mm(out, hi[:, part, w], x_hi, start=(kk == 0), stop=False)
                    mm(out, hi[:, part, w], x_lo, start=False, stop=False)
                    last = mm(out, lo[:, part, w], x_hi, start=False, stop=(kk == KT - 1))
                last.then_inc(K["quarter_done"], 1)

            def project_g(h, q, first=False):
                j, part = q // 4, q % 4
                n = L if j < 3 else SEQ
                if part == 0 and not (first and j < 2):
                    pe.wait_ge(K["projev"], h * G_TILES + j - 1)
                quarter("G", h, j, part, PA[j % 2][:, 0:n], n_hl, slice(L - n, L))

            def project_s(g, q):
                j, part = q // 4, q % 4
                n = L if j < 2 + XB else SEQ
                if part == 0:
                    pe.wait_ge(K["projev"], GDN_HEADS * G_TILES + g * S_TILES + j - 1)
                quarter("S", g, j, part, PA[j % 2][:, 0:n], n_hl, slice(L - n, L))

            def mixer_g(h, fill):
                h1 = plus1(pe, h)
                w = pe.wait_ge
                fill(0)
                w(K["qk_sqd"], h1)
                if not is_first(h):
                    w(K["og_done"], h)
                mm(m[0][:, 0:L], ones, qk_sq[:, 0, :], start=True, stop=True)
                mm(m[1][:, 0:L], ones, qk_sq[:, 1, :], start=True, stop=True).then_inc(K["qk_ss"], 1)
                for c in range(NC):
                    last = tr(m[2][:, c * Q:(c + 1) * Q], qkv[:, 2, c * Q:(c + 1) * Q], ident)
                last.then_inc(K["vt_done"], 1)
                fill(1)
                w(K["kn_done"], h1)
                for c in range(NC):
                    last = mm(m[4][:, c * Q:(c + 1) * Q], KN[:, c, :], KN[:, c, :], start=True, stop=True)
                last.then_inc(K["kk_done"], 1)
                w(K["qn_done"], h1)
                for c in range(2):
                    last = mm(m[5][:, c * Q:(c + 1) * Q], KN[:, c + 1, :], QN[:, c, :], start=True, stop=True)
                last.then_inc(K["qk_done"], 1)
                for c in range(2):
                    last = tr(m[3][:, c * Q:(c + 1) * Q], KN[:, c, :], ident)
                last.then_inc(K["kt_done"], 1)
                fill(2)
                w(K["x_done"], 3 * h1)
                for c in range(NC):
                    last = tr(m[0][:, c * Q:(c + 1) * Q], X[:, c, :], ident)
                last.then_inc(K["xt_done"], 1)
                fill(3)
                w(K["b_done"], h1)
                w(K["bt_done"], h1)
                w(K["vb_done"], h1)
                for c in range(NC):
                    mm(m[1][:, c * Q:(c + 1) * Q], BT[:, c, :], B[:, c, :], start=True, stop=True)
                    last = mm(m[2][:, c * Q:(c + 1) * Q], B[:, c, :], BT[:, c, :], start=True, stop=True)
                last.then_inc(K["b2_done"], 1)
                fill(4)
                w(K["b2s_done"], 2 * h1)
                w(K["lt_done"], 3 * h1)
                w(K["kd_done"], h1)
                w(K["p1_done"], h1)
                for c in range(NC):
                    mm(m[0][:, c * Q:(c + 1) * Q], B2T[:, c, :], B2[:, c, :], start=True, stop=True)
                    mm(m[3][:, c * Q:(c + 1) * Q], B2[:, c, :], B2T[:, c, :], start=True, stop=True)
                    last = mm(m[4][:, c * Q:(c + 1) * Q], B2T[:, c, :], PP[:, c, :], start=True, stop=True)
                last.then_inc(K["b4_done"], 1)
                fill(5)
                w(K["b4s_done"], 2 * h1)
                w(K["p2_done"], h1)
                for c in range(NC):
                    mm(m[1][:, c * Q:(c + 1) * Q], B4[:, c, :], B4T[:, c, :], start=True, stop=True)
                    last = mm(m[2][:, c * Q:(c + 1) * Q], B4T[:, c, :], PP[:, c, :], start=True, stop=True)
                last.then_inc(K["b8_done"], 1)
                fill(6)
                w(K["b8s_done"], h1)
                w(K["p3_done"], h1)
                for c in range(NC):
                    last = mm(m[0][:, c * Q:(c + 1) * Q], B8T[:, c, :], PP[:, c, :], start=True, stop=True)
                last.then_inc(K["pb8_done"], 1)
                fill(7)
                w(K["t0_done"], h1)
                for c in range(NC):
                    last = tr(m[3][:, c * Q:(c + 1) * Q], T[:, c, :], ident)
                last.then_inc(K["t0t_done"], 1)
                fill(8)
                w(K["t0ts_done"], h1)
                for c in range(2):
                    last = mm(m[1][:, c * Q:(c + 1) * Q], LT[:, 0, c, :], T[:, 1 + c, :], start=True, stop=True)
                last.then_inc(K["y_done"], 1)
                mm(m[4][:, 0:Q], TT[:, 0, :], VB[:, 0, :], start=True, stop=True).then_inc(K["vn0_done"], 1)
                fill(9)

                def both(bank, n):
                    w(K["ys_done"], 3 * h + n)
                    for c in range(2):
                        mm(bank[:, c * Q:(c + 1) * Q], TT[:, 1 + c, :], Y[:, c, :], start=True, stop=True)
                        x = mm(bank[:, (2 + c) * Q:(3 + c) * Q], Y[:, c, :], TT[:, 1 + c, :], start=True, stop=True)
                    x.then_inc(K["tn_done"], 1)

                both(m[2], 1)
                w(K["vn0s_done"], h1)
                w(K["at_done"], h1)
                mm(m[5][:, 0:Q], KD[:, 0, :], VN, start=True, stop=True).then_inc(K["s1_done"], 1)
                fill(10)
                w(K["tu_done"], 5 * h + 2)
                for c in range(2):
                    last = mm(m[0][:, c * Q:(c + 1) * Q], LT[:, 1, c, :], T[:, 1 + c, :], start=True, stop=True)
                last.then_inc(K["y_done"], 1)
                w(K["s1s_done"], h1)
                mm(m[4][:, 0:Q], KN[:, 1, :], S, start=True, stop=True).then_inc(K["ks_done"], 1)
                fill(11)
                both(m[3], 2)
                fill(12)
                w(K["tu_done"], 5 * h + 4)
                for c in range(2):
                    last = mm(m[1][:, c * Q:(c + 1) * Q], LT[:, 2, c, :], T[:, 1 + c, :], start=True, stop=True)
                last.then_inc(K["y_done"], 1)
                fill(13)
                w(K["ys_done"], 3 * h + 3)
                for c in range(2):
                    last = mm(m[2][:, c * Q:(c + 1) * Q], Y[:, c, :], TT[:, 1 + c, :], start=True, stop=True)
                last.then_inc(K["tn_done"], 1)
                fill(14)
                w(K["tu_done"], 5 * h + 5)
                w(K["r_done"], 2 * h + 1)
                mm(m[5][:, 0:Q], TT[:, 1, :], RR, start=True, stop=True).then_inc(K["vn_done"], 1)
                fill(15)
                w(K["vns_done"], 2 * h + 1)
                mm(m[0][:, 0:Q], KD[:, 1, :], VN, start=True, stop=True).then_inc(K["su_done"], 1)
                w(K["qg_done"], h1)
                mm(m[1][:, 0:Q], S, QG[:, 0, :], start=True, stop=False)
                mm(m[1][:, 0:Q], VN, AT[:, 0, :], start=False, stop=True).then_inc(K["o_done"], 1)
                fill(16)
                w(K["s2_done"], h1)
                mm(m[4][:, 0:Q], KN[:, 2, :], S, start=True, stop=True).then_inc(K["ks_done"], 1)
                fill(17)
                w(K["r_done"], 2 * h + 2)
                mm(m[5][:, 0:Q], TT[:, 2, :], RR, start=True, stop=True).then_inc(K["vn_done"], 1)
                fill(18)
                w(K["vns_done"], 2 * h + 2)
                mm(m[1][:, Q:2 * Q], S, QG[:, 1, :], start=True, stop=False)
                mm(m[1][:, Q:2 * Q], VN, AT[:, 1, :], start=False, stop=True).then_inc(K["o_done"], 1)
                fill(19)
                w(K["osq_done"], h1)
                mm(m[0][:, 0:SEQ], ones, o_sq, start=True, stop=True).then_inc(K["on_done"], 1)
                fill(20)

            pe.wait_ge(K["const_in"], 16)
            pe.wait_ge(K["norm_sq"], 1)
            for k in range(KT):
                last = mm(m[0][:, 0:L], ones, x_sq[:, k, :], start=(k == 0), stop=(k == KT - 1))
            last.then_inc(K["norm_ss"], 1)
            for part in range(4):
                pe.wait_ge(K["x_lo"], part + 1)
                quarter("G", 0, -1, part, m[1][:, 0:L], n_hl)
            for q in range(4 * G_TILES):
                project_g(0, q, first=True)
            for n, (src, key) in enumerate(((5, "csum"), (6, "row_exps"), (7, "sp_part"), (8, "row_exps"), (9, "beta_rows"))):
                if n == 0:
                    pe.wait_ge(K[key], NC)
                elif n in (1, 3):
                    pe.wait_ge(K[key], 2 * NC)
                elif n == 2:
                    pe.wait_ge(K[key], 10)
                else:
                    pe.wait_ge(K[key], 1)
                if n >= 2:
                    pe.wait_ge(K["colcp"], n - 1)
                for c in range(NC):
                    last = tr(m[2 + n % 2][:, c * 64:(c + 1) * 64],
                              rows[0:64, src, c * Q:(c + 1) * Q], ident[0:64, 0:64])
                last.then_inc(K["colps"], 1)

            mixer_g(0, lambda n: [project_g(1, q) for q in filled(G_FILL, n)])
            with pe.Fori(1, GDN_HEADS - 1) as h:
                mixer_g(h, lambda n: [project_g(h + 1, q) for q in filled(G_FILL, n)])
            mixer_g(GDN_HEADS - 1, lambda n: [project_s(0, q) for q in filled(G_FILL_LAST, n)])

            def group_s(g, fill):
                g1 = plus1(pe, g)
                w = pe.wait_ge
                fill(0)
                fill(1)
                w(K["s_silu"], g1)
                if not is_first(g):
                    w(K["s_yd"], XB * g)
                for c in range(2):
                    last = tr(m[0][:, c * Q:(c + 1) * Q], xbc[:, 0, c * Q:(c + 1) * Q], ident)
                last.then_inc(K["s_bt"], 1)
                for c in range(NC):
                    for b in range(XB):
                        last = tr(m[1 + c][:, b * P:(b + 1) * P], xbc[:, 2 + b, c * Q:(c + 1) * Q], ident)
                    last.then_inc(K["s_xt"], 1)
                for c in range(2):
                    tok = slice((c + 1) * Q, (c + 2) * Q)
                    last = mm(m[4][:, c * Q:(c + 1) * Q], xbc[:, 0, tok], xbc[:, 1, tok], start=True, stop=True)
                last.then_inc(K["s_cbt"], 1)
                fill(2)
                w(K["s_btok"], g1)
                w(K["s_xe"], 2 * g + 1)
                if not is_first(g):
                    w(K["s_std"], g)
                mm(m[5][:, :], Btok[:, 0, :], XE[:, 0, :], start=True, stop=True).then_inc(K["s_s1"], 1)
                fill(3)
                w(K["s_xe"], 2 * g + 2)
                mm(m[0][:, :], Btok[:, 1, :], XE[:, 1, :], start=True, stop=True).then_inc(K["s_su"], 1)
                fill(4)
                for c in range(2):
                    if c == 0:
                        w(K["s_xc"], NC * g1)
                        w(K["s_s1c"], g1)
                        w(K["s_cg"], g1)
                    else:
                        w(K["s_s2"], g1)
                    w(K["s_w"], 2 * g1)
                    for b in range(XB):
                        for e in range(2):
                            r = 2 * b + e
                            rows_ = slice(e * SSD_HD, (e + 1) * SSD_HD)
                            ch = slice(r * SSD_HD, (r + 1) * SSD_HD)
                            tok = slice(c * Q, (c + 1) * Q)
                            mm(m[1 + b][rows_, tok], XC[:, 1 + c, ch], WE[:, r, tok], start=True, stop=False)
                            last = mm(m[1 + b][rows_, tok], SS[:, c, ch], EC[:, r, tok], start=False, stop=True)
                    last.then_inc(K["s_y"], 1)
                    fill(5 + c)
                w(K["s_ysq"], g1)
                for b in range(XB):
                    last = mm(m[5][:, 0:SEQ], ones, y_sq[:, b, :], start=(b == 0), stop=(b == XB - 1))
                last.then_inc(K["s_ss"], 1)
                fill(7)

            group_s(0, lambda n: [project_s(1, q) for q in filled(S_FILL, n)])
            with pe.Fori(1, SSD_GROUPS - 1) as g:
                group_s(g, lambda n: [project_s(g + 1, q) for q in filled(S_FILL, n)])
            group_s(SSD_GROUPS - 1, lambda n: None)

            def tile(segment, it, j, out, moving, tokens=slice(None)):
                for part in range(4):
                    quarter(segment, it, j, part, out, moving, tokens)

            tok = slice(N_META, L)
            pe.wait_ge(K["s_std"], SSD_GROUPS)

            def merge(n):
                if is_first(n):
                    pe.wait_ge(K["projev"], GDN_HEADS * G_TILES + SSD_GROUPS * S_TILES)
                else:
                    pe.wait_ge(K["m_muld"], 2 * n - 1)
                tile("M", n, 0, PA[0][:, 0:SEQ], n_hl, tok)
                if is_first(n):
                    for part in range(4):
                        pe.wait_ge(K["x_lo"], 4 + part + 1)
                        quarter("M", n, 1, part, PA[1][:, 0:SEQ], y_hl[0])
                else:
                    tile("M", n, 1, PA[1][:, 0:SEQ], y_hl[0])
                    pe.wait_ge(K["m_muld"], 2 * n)
                tile("M", n, 2, m[0][:, 0:SEQ], n_hl, tok)
                if is_first(n):
                    pe.wait_ge(K["x_lo"], 12)
                tile("M", n, 3, m[1][:, 0:SEQ], y_hl[1])

            merge(0)
            with pe.Fori(1, KT) as n:
                merge(n)

            o_banks = (m[2], m[3], m[4], m[5])
            pe.wait_ge(K["m_lo"], KT)

            def residual(n):
                for j in range(ROUND):
                    if not is_first(n):
                        pe.wait_ge(K["h2_done"], ROUND * n + j - 3)
                    tile("O", n, j, o_banks[j][:, 0:SEQ], m_hl)

            residual(0)
            with pe.Fori(1, O_TILES // ROUND) as n:
                residual(n)
            pe.wait_ge(K["norm_sq"], 2)
            for k in range(KT):
                last = mm(m[0][:, 0:SEQ], ones, h2_sq[:, k, :], start=(k == 0), stop=(k == KT - 1))
            last.then_inc(K["norm_ss"], 1)
            pe.wait_ge(K["x_lo"], 16)

            def queries(n):
                for e in range(2):
                    for k in range(2):
                        j = 2 * e + k
                        tile("Q", n, j, (m[2], m[3], m[4], m[5])[j][:, 0:SEQ], nf)
                for e in range(2):
                    pe.wait_ge(K["q_copy"], 4 * n + 2 * e + 2)
                    if not is_first(n):
                        pe.wait_ge(K["sc_cp"], 2 * n + e - 1)
                    for k in range(2):
                        for half in range(2):
                            last = mm(PA[e][:, (2 * k + half) * N_KEYS:(2 * k + half + 1) * N_KEYS],
                                      qT[:, 2 * e + k, half * P:(half + 1) * P],
                                      C["keysT"][:, k * N_KEYS:(k + 1) * N_KEYS], start=True, stop=True)
                    last.then_inc(K["sc_ps"], 1)

            queries(0)
            with pe.Fori(1, Q_TILES // ROUND) as n:
                queries(n)

            pe.wait_ge(K["r_pick"], 4 * PEER_HEADS)
            pe.wait_ge(K["r_gate"], 2 * PEER_HEADS)
            for f in range(3):
                for half in range(2):
                    last = tr(m[0 if f < 2 else 1][:, (2 * (f % 2) + half) * P:(2 * (f % 2) + half + 1) * P],
                              tab_t[:, f, half, :], ident)
            last.then_inc(K["t_ps"], 1)
            pe.wait_ge(K["t_cp"], 2)

            def spread(n):
                for e in range(2):
                    pe.wait_ge(K["oh_d"], 16 * n + 8 * e + 8)
                    if not is_first(n):
                        pe.wait_ge(K["oh_cp"], 2 * n + e - 1)
                    for u in range(4):
                        last = mm(m[2 + e][:, u * P:(u + 1) * P], oh[:, e, u, 1, :], oh[:, e, u, 0, :],
                                  start=True, stop=True)
                    last.then_inc(K["oh_ps"], 1)

            spread(0)
            with pe.Fori(1, SEQ // 8) as n:
                spread(n)

            def down(n):
                for j in range(ROUND):
                    if not is_first(n):
                        pe.wait_ge(K["d_gelu"], ROUND * n + j - 3)
                    elif j == 0:
                        pe.wait_ge(K["oh_cp"], SEQ // 4)
                    tile("D", n, j, m[2 + j][:, 0:SEQ], nf)

            down(0)
            with pe.Fori(1, N_KEYS // ROUND) as n:
                down(n)

            def up(n):
                for j in range(ROUND):
                    i = n * ROUND + j
                    pe.wait_ge(K["a_lo"], i + 1)
                    for part in range(4):
                        pe.wait_ge(K["cut_l"], 4 * tile_no("U", n, j) + part + 1)
                        for b in range(QT):
                            d = QT * part + b
                            out = banks[d // 2][:, (d % 2) * SEQ:(d % 2 + 1) * SEQ]
                            w = slice(b * P, (b + 1) * P)
                            first = is_first(n) and j == 0 and d % 2 == 0
                            mm(out, hi[:, part, w], a_hl[0][:, j % 2, :], start=first, stop=False, skip_group_check=True)
                            mm(out, hi[:, part, w], a_hl[1][:, j % 2, :], start=False, stop=False, skip_group_check=True)
                            last = mm(out, lo[:, part, w], a_hl[0][:, j % 2, :], start=False, stop=False,
                                      skip_group_check=True)
                        last.then_inc(K["quarter_done"], 1)

            up(0)
            with pe.Fori(1, N_KEYS // ROUND) as n:
                up(n)
            pe.wait_ge(K["norm_sq"], 3)
            for k in range(KT):
                last = mm(banks[0][:, 0:SEQ], ones, h3_sq[:, k, :], start=(k == 0), stop=(k == KT - 1),
                          skip_group_check=True)
            last.then_inc(K["norm_ss"], 1)

        @block.scalar
        def _(act):
            def cut(segment, it, j, part):
                q = 4 * tile_no(segment, it, j) + part
                half = part // 2
                slot = half_slot(segment, j, half)
                if part % 2 == 0:
                    act.wait_ge(W_IN[slot], 16 * (half_use(segment, it, j, half) + 1))
                if not (type(q) is int and q < 4):
                    act.wait_ge(K["quarter_done"], q - 3)
                nc.scalar.copy(hi[:, part, :], ring[:, slot, (part % 2) * QW:(part % 2 + 1) * QW]) \
                    .then_inc(K["cut_h"], 1)

            def cut_tile(segment, it, j):
                for part in range(4):
                    cut(segment, it, j, part)

            act.wait_ge(K["x_in"], 16)
            A(x_sq[:, :, :], xT[:, :, :], ACT.Square).then_inc(K["norm_sq"], 1)
            act.wait_ge(K["const_in"], 16)
            act.wait_ge(K["norm_ss"], 1)
            A(x_rn, m[0][:, 0:L], ACT.Sqrt, bias=C["eps"], scale=1.0 / D_MODEL).then_inc(K["norm_std"], 1)
            cut_tile("G", 0, -1)
            for part in range(4):
                act.wait_ge(K["normed"], QT * (part + 1))
                ks = slice(part * QT, (part + 1) * QT)
                nc.scalar.copy(n_hl[0][:, ks, :], xT[:, ks, :]).then_inc(K["x_hi"], 1)
            cut_tile("G", 0, 0)
            act.wait_ge(K["sp_part"], 1)
            A(rows[0:64, 1, 0:L], rows[0:64, 0, 0:L], ACT.Abs).then_inc(K["sp_act"], 1)
            act.wait_ge(K["sp_act"], 1)
            A(rows[0:64, 2, 0:L], rows[0:64, 1, 0:L], ACT.Exp, scale=-1.0).then_inc(K["sp_act"], 1)
            A(C["alog"][0:64, :], C["alog"][0:64, :], ACT.Exp).then_inc(K["sp_act"], 1)
            act.wait_ge(K["sp_part"], 2)
            A(rows[0:64, 4, 0:L], rows[0:64, 3, 0:L], ACT.Ln).then_inc(K["sp_act"], 1)
            act.wait_ge(K["zeroed"], 1)
            act.wait_ge(K["quarter_done"], 4)
            A(rows[0:16, 9, PAD:TC], m[1][64:80, 0:L], ACT.Sigmoid).then_inc(K["beta_rows"], 1)
            act.wait_ge(K["csum"], NC)
            for c in range(NC):
                A(rows[0:64, 6, c * Q:(c + 1) * Q], rows[0:64, 5, c * Q:(c + 1) * Q], ACT.Exp, scale=-1.0,
                  bias=rows[0:64, 5, (c + 1) * Q - 1:(c + 1) * Q]).then_inc(K["row_exps"], 1)
                A(rows[0:64, 8, c * Q:(c + 1) * Q], rows[0:64, 5, c * Q:(c + 1) * Q], ACT.Exp) \
                    .then_inc(K["row_exps"], 1)
            act.dma_start(gcs_d, rows[0:64, 5, :]).then_inc(K["gcs_out"], 16)

            def evac_g(h, j):
                act.wait_ge(K["quarter_done"], 4 * (tile_no("G", h, j) + 1))
                if j < 3:
                    nc.scalar.copy(g_raw[:, j, TAPS - 1:], PA[j % 2][:, 0:L]).then_inc(K["projev"], 1)
                else:
                    nc.scalar.copy(gate_raw, PA[j % 2][:, 0:SEQ]).then_inc(K["projev"], 1)

            for j in range(G_TILES):
                cut_tile("G", 0, j + 1)
                evac_g(0, j)
            act.wait_ge(K["colder"], 4)

            def fill(fill_plan, segment, it, evac_one):
                def at(n, cutting=True, copying=True):
                    if cutting:
                        cuts(cut, segment, it, fill_plan, n)
                    if copying:
                        for q in filled(fill_plan, n):
                            if q % 4 == 3:
                                evac_one(it, q // 4)
                return at

            def mixer_g(h, evac):
                h1 = plus1(act, h)
                w = act.wait_ge
                w(K["rows_in"], 16 * h1)
                w(K["gm_done"], 2 * h1)
                for c in range(NC):
                    A(E[:, c, :], GE[:, c, :], ACT.Exp, bias=col_gcs[:, c, ds(32 + h, 1)]).then_inc(K["e_done"], 1)
                for c in range(2):
                    A(ET[:, c, :], GT[:, c, :], ACT.Exp, bias=col_ngcs[:, 1 + c, ds(32 + h, 1)]) \
                        .then_inc(K["et_done"], 1)
                A(EG[:, :, :], g_row[:, 1:3, :], ACT.Exp).then_inc(K["eg_done"], 1)
                w(K["conv_tap"], 3 * TAPS * h1)
                A(qkv[:, :, PAD:TC], cv[:, :, :], ACT.Silu).then_inc(K["silu_done"], 1)
                w(K["projev"], G_TILES * h1)
                if not is_first(h):
                    w(K["og_done"], h)
                A(gate_s, gate_raw, ACT.Silu).then_inc(K["gsilu"], 1)
                w(K["silu_done"], h1)
                A(qk_sq[:, :, :], qkv[:, 0:2, PAD:TC], ACT.Square).then_inc(K["qk_sqd"], 1)
                evac(0)
                w(K["qk_ss"], h1)
                for i in range(2):
                    A(qk_n[:, i, :], m[i][:, 0:L], ACT.Sqrt, bias=C["eps"]).then_inc(K["qk_std"], 1)
                evac(1)
                evac(2)
                evac(3)
                w(K["b2_done"], h1)
                nc.scalar.copy(B2[:, :, :], m[1][:, 0:TC].rearrange("p (c q) -> p c q", q=Q)).then_inc(K["b2s_done"], 1)
                nc.scalar.copy(B2T[:, :, :], m[2][:, 0:TC].rearrange("p (c q) -> p c q", q=Q)).then_inc(K["b2s_done"], 1)
                evac(4)
                w(K["b4_done"], h1)
                nc.scalar.copy(B4[:, :, :], m[0][:, 0:TC].rearrange("p (c q) -> p c q", q=Q)).then_inc(K["b4s_done"], 1)
                nc.scalar.copy(B4T[:, :, :], m[3][:, 0:TC].rearrange("p (c q) -> p c q", q=Q)).then_inc(K["b4s_done"], 1)
                evac(5)
                w(K["b8_done"], h1)
                nc.scalar.copy(B8T[:, :, :], m[1][:, 0:TC].rearrange("p (c q) -> p c q", q=Q)).then_inc(K["b8s_done"], 1)
                evac(6)
                evac(7)
                w(K["t0t_done"], h1)
                nc.scalar.copy(TT[:, :, :], m[3][:, 0:TC].rearrange("p (c q) -> p c q", q=Q)).then_inc(K["t0ts_done"], 1)
                evac(8)

                def copy_y(bank, n):
                    w(K["y_done"], 3 * h + n)
                    nc.scalar.copy(Y[:, :, :], bank[:, 0:2 * Q].rearrange("p (c q) -> p c q", q=Q)) \
                        .then_inc(K["ys_done"], 1)

                copy_y(m[1], 1)
                evac(9)
                w(K["s1_done"], h1)
                nc.scalar.copy(S, m[5][:, 0:Q]).then_inc(K["s1s_done"], 1)
                evac(10)
                copy_y(m[0], 2)
                evac(11)
                evac(12)
                copy_y(m[1], 3)
                for n in range(13, 19):
                    evac(n)
                w(K["o_done"], 2 * h1)
                A(o_sq, m[1][:, 0:SEQ], ACT.Square).then_inc(K["osq_done"], 1)
                evac(19)
                w(K["on_done"], h1)
                A(o_n, m[0][:, 0:SEQ], ACT.Sqrt, bias=C["eps"], scale=1.0 / DK).then_inc(K["onstd_done"], 1)
                evac(20)

            mixer_g(0, fill(G_FILL, "G", 1, evac_g))
            with act.Fori(1, GDN_HEADS - 1) as h:
                mixer_g(h, fill(G_FILL, "G", h + 1, evac_g))

            def evac_s(g, j):
                act.wait_ge(K["quarter_done"], 4 * (tile_no("S", g, j) + 1))
                if j < 2 + XB:
                    nc.scalar.copy(s_raw[:, j, TAPS - 1:], PA[j % 2][:, 0:L]).then_inc(K["projev"], 1)
                else:
                    nc.scalar.copy(z_raw[:, j - 2 - XB, :], PA[j % 2][:, 0:SEQ]).then_inc(K["projev"], 1)

            mixer_g(GDN_HEADS - 1, fill(G_FILL_LAST, "S", 0, evac_s))
            act.wait_ge(K["og_done"], GDN_HEADS)

            def group_s(g, evac):
                g1 = plus1(act, g)
                w = act.wait_ge
                if not is_first(g):
                    w(K["s_y"], 2 * g)
                w(K["srows_in"], 16 * g1)
                A(EC[:, :, :], s_row[:, :, :], ACT.Exp).then_inc(K["s_ec"], 1)
                w(K["s_ec"], g1)
                if not is_first(g):
                    w(K["s_s2"], g)
                nc.scalar.copy(decay_s, EC[:, :, Q - 1]).then_inc(K["s_dec"], 1)
                w(K["s_gm"], g1)
                for r in range(R):
                    for c in range(2):
                        A(WE[:, r, c * Q:(c + 1) * Q], WE[:, r, c * Q:(c + 1) * Q], ACT.Exp,
                          bias=col_ngcs[:, 1 + c, ds(R * g + r, 1)]).then_inc(K["s_we"], 1)
                evac(0, copying=False)
                w(K["s_tap"], (2 + XB) * TAPS * g1)
                A(xbc[:, :, PAD:TC], cv6[:, :, :], ACT.Silu).then_inc(K["s_silu"], 1)
                w(K["projev"], GDN_HEADS * G_TILES + S_TILES * g1)
                A(z_s[:, :, :], z_raw[:, :, :], ACT.Silu).then_inc(K["s_zsilu"], 1)
                evac(0, cutting=False)
                evac(1)
                w(K["s_bt"], g1)
                nc.scalar.copy(Btok[:, :, :], m[0][:, 0:2 * Q].rearrange("p (c q) -> p c q", q=Q)) \
                    .then_inc(K["s_btok"], 1)
                evac(2)
                w(K["s_s1"], g1)
                nc.scalar.copy(SS[:, 0, :], m[5][:, :]).then_inc(K["s_s1c"], 1)
                for n in range(3, 7):
                    evac(n)
                w(K["s_yz"], g1)
                A(y_sq[:, :, :], y_g[:, :, :], ACT.Square).then_inc(K["s_ysq"], 1)
                w(K["s_ss"], g1)
                A(y_rn, m[5][:, 0:SEQ], ACT.Sqrt, bias=C["eps"], scale=1.0 / (XB * P)).then_inc(K["s_std"], 1)
                evac(7)

            group_s(0, fill(S_FILL, "S", 1, evac_s))
            with act.Fori(1, SSD_GROUPS - 1) as g:
                group_s(g, fill(S_FILL, "S", g + 1, evac_s))
            group_s(SSD_GROUPS - 1, lambda n, **what: None)
            for i, (y, key, n) in enumerate(((y_ssd, "s_out", SSD_HEADS // 2), (y_gdn, "og_done", GDN_HEADS))):
                act.wait_ge(K[key], n)
                for part in range(4):
                    ks = slice(part * QT, (part + 1) * QT)
                    nc.scalar.copy(y_hl[i][0][:, ks, :], y[:, ks, :]).then_inc(K["x_hi"], 1)

            def merge(n):
                for i in range(2):
                    cut_tile("M", n, 2 * i + 1)
                    if not is_first(n):
                        act.wait_ge(K["m_muld"], 2 * n + i - 1)
                    A(m_sig[:, i, :], (PA[0], m[0])[i][:, 0:SEQ], ACT.Sigmoid).then_inc(K["m_sigd"], 1)
                    cut_tile("M", n, 2 * i + 2)

            merge(0)
            with act.Fori(1, KT) as n:
                merge(n)
            act.wait_ge(K["quarter_done"], 4 * O_AT)
            act.dma_start(h_in[:, :, :], xT_d[:, :, N_META:L]).then_inc(K["h_moved"], 16)
            with act.Fori(0, O_TILES // ROUND) as n:
                for j in range(ROUND):
                    cut_tile("O", n, j + 1)
            act.wait_ge(K["h2_done"], KT)
            A(h2_sq[:, :, :], h2[:, :, :], ACT.Square).then_inc(K["norm_sq"], 1)
            act.dma_start(h2_d, h2[:, :, :].rearrange("p k t -> p (k t)")).then_inc(K["h_moved"], 16)
            act.wait_ge(K["norm_ss"], 2)
            A(f_rn, m[0][:, 0:SEQ], ACT.Sqrt, bias=C["eps"], scale=1.0 / D_MODEL).then_inc(K["norm_std"], 1)
            for part in range(4):
                act.wait_ge(K["normed"], KT + QT * (part + 1))
                ks = slice(part * QT, (part + 1) * QT)
                nc.scalar.copy(nf[0][:, ks, :], h2_sq[:, ks, :]).then_inc(K["x_hi"], 1)

            def queries(n, last=False):
                for e in range(2):
                    if not is_first(n):
                        act.wait_ge(K["sc_ps"], 2 * n + e - 1)
                    for k in range(2):
                        j = 2 * e + k
                        if not (last and j == ROUND - 1):
                            cut_tile("Q", n, j + 1)
                        act.wait_ge(K["quarter_done"], 4 * (tile_no("Q", n, j) + 1))
                        nc.scalar.copy(qT[:, j, :], (m[2], m[3], m[4], m[5])[j][:, 0:SEQ]).then_inc(K["q_copy"], 1)
                for e in range(2):
                    for half in range(2):
                        act.wait_ge(K["r_neg"], 2 * (2 * n + e) + 2)
                        A(ebest[:, half, :], best[:, half, :], ACT.Exp, bias=soft[:, 0, half:half + 1],
                          accum_out=soft[:, 1, half:half + 1]).then_inc(K["r_exp"], 1)

            queries(0)
            with act.Fori(1, Q_TILES // ROUND - 1) as n:
                queries(n)
            queries(Q_TILES // ROUND - 1, last=True)

            def spread(n):
                for e in range(2):
                    act.wait_ge(K["oh_ps"], 2 * n + e + 1)
                    nc.scalar.copy(gates[:, :, ds(8 * n + 4 * e, 4)].rearrange("p i u -> p u i"),
                                   m[2 + e][:, :].rearrange("p (u i) -> p u i", i=P)).then_inc(K["oh_cp"], 1)

            act.wait_ge(K["t_cp"], 2)
            act.wait_ge(K["h_moved"], 32)
            spread(0)
            with act.Fori(1, SEQ // 8) as n:
                spread(n)

            cut_tile("D", 0, 0)

            def down(n):
                for j in range(ROUND):
                    cut_tile("D", n, j + 1)
                    act.wait_ge(K["quarter_done"], 4 * (tile_no("D", n, j) + 1))
                    if not (is_first(n) and j < 2):
                        act.wait_ge(K["d_gate"], ROUND * n + j - 1)
                    A(gelu[:, j % 2, :], m[2 + j][:, 0:SEQ], ACT.Gelu).then_inc(K["d_gelu"], 1)

            down(0)
            with act.Fori(1, N_KEYS // ROUND) as n:
                down(n)
            act.wait_ge(K["d_gate"], N_KEYS)

            def cut_gates(n, j):
                act.wait_ge(K["quarter_done"], 4 * (tile_no("U", n, j) - 1))
                nc.scalar.copy(a_hl[0][:, j % 2, :], gates[:, n * ROUND + j, :]).then_inc(K["a_hi"], 1)

            def up(n, last=False):
                for j in range(ROUND):
                    if not (last and j == ROUND - 1):
                        cut_gates(n, j + 1)
                        cut_tile("U", n, j + 1)

            act.wait_ge(K["quarter_done"], 4 * U_AT)
            cut_gates(0, 0)
            with act.Fori(0, N_KEYS // ROUND - 1) as n:
                up(n)
            up(N_KEYS // ROUND - 1, last=True)
            act.wait_ge(K["quarter_done"], 4 * END)
            act.dma_start(h2b[:, :, :].rearrange("p k t -> p (k t)"), h2_d).then_inc(K["h_moved"], 16)
            act.wait_ge(K["h3_done"], KT // 2)
            A(h3_sq[:, :, :], h3[:, :, :], ACT.Square).then_inc(K["norm_sq"], 1)
            act.wait_ge(K["norm_ss"], 3)
            A(h3_rn, banks[0][:, 0:SEQ], ACT.Sqrt, bias=C["eps"], scale=1.0 / D_MODEL).then_inc(K["norm_std"], 1)
            act.wait_ge(K["out_done"], KT)
            act.dma_start(out_d, h3[:, :, :].rearrange("p k t -> p (k t)")).then_inc(K["out_in"], 16)
            act.wait_ge(K["out_in"], 16)

        @block.vector
        def _(dve):
            def cut(segment, it, j, part):
                q = 4 * tile_no(segment, it, j) + part
                slot = half_slot(segment, j, part // 2)
                dve.wait_ge(K["cut_h"], q + 1)
                V.tensor_tensor(lo[:, part, :], ring[:, slot, (part % 2) * QW:(part % 2 + 1) * QW],
                                hi[:, part, :].bitcast(F32), ALU.subtract).then_inc(K["cut_l"], 1)

            def cut_tile(segment, it, j):
                for part in range(4):
                    cut(segment, it, j, part)

            V.memset(rows[0:64, 5:10, :], 0.0).then_inc(K["zeroed"], 1)
            V.memset(rows[0:64, 10, :], 0.0).then_inc(K["zeroed"], 1)
            V.memset(rows[0:64, 11, :], 1.0).then_inc(K["zeroed"], 1)
            V.memset(g_raw[:, :, 0:TAPS - 1], 0.0).then_inc(K["zeroed"], 1)
            V.memset(s_raw[:, :, 0:TAPS - 1], 0.0).then_inc(K["zeroed"], 1)
            dve.wait_ge(K["norm_std"], 1)
            V.reciprocal(x_rn, x_rn).then_inc(K["norm_rec"], 1)
            dve.wait_ge(K["norm_rec"], 1)
            for k in range(KT):
                V.scalar_tensor_tensor(out=xT[:, k, :], in0=xT[:, k, :], scalar=C["w_mix"][:, k:k + 1], in1=x_rn,
                                       op0=ALU.mult, op1=ALU.mult).then_inc(K["normed"], 1)
            cut_tile("G", 0, -1)
            for part in range(4):
                dve.wait_ge(K["x_hi"], part + 1)
                ks = slice(part * QT, (part + 1) * QT)
                V.tensor_tensor(n_hl[1][:, ks, :], xT[:, ks, :], n_hl[0][:, ks, :].bitcast(F32), ALU.subtract) \
                    .then_inc(K["x_lo"], 1)
            cut_tile("G", 0, 0)
            sp = K["sp_part"]
            dve.wait_ge(K["quarter_done"], 4)
            V.tensor_scalar(rows[0:64, 0, 0:L], m[1][0:64, 0:L], C["dtb"][0:64, :], None, ALU.add).then_inc(sp, 1)
            dve.wait_ge(K["sp_act"], 2)
            V.tensor_scalar(rows[0:64, 3, 0:L], rows[0:64, 2, 0:L], 1.0, None, ALU.add).then_inc(sp, 1)
            dve.wait_ge(sp, 2)
            V.tensor_scalar(rows[0:64, 12, 0:L], rows[0:64, 3, 0:L], -1.0, None, ALU.add).then_inc(sp, 1)
            dve.wait_ge(sp, 3)
            V.tensor_tensor(rows[0:64, 13, 0:L], rows[0:64, 2, 0:L], rows[0:64, 12, 0:L], ALU.subtract).then_inc(sp, 1)
            V.reciprocal(rows[0:64, 14, 0:L], rows[0:64, 3, 0:L]).then_inc(sp, 1)
            dve.wait_ge(sp, 5)
            V.tensor_tensor(rows[0:64, 15, 0:L], rows[0:64, 13, 0:L], rows[0:64, 14, 0:L], ALU.mult).then_inc(sp, 1)
            dve.wait_ge(K["sp_act"], 4)
            dve.wait_ge(sp, 6)
            V.tensor_tensor(rows[0:64, 16, 0:L], rows[0:64, 4, 0:L], rows[0:64, 15, 0:L], ALU.add).then_inc(sp, 1)
            dve.wait_ge(sp, 7)
            dve.wait_ge(K["zeroed"], 5)
            V.scalar_tensor_tensor(out=rows[0:64, 7, PAD:TC], in0=rows[0:64, 0, 0:L], scalar=0.0,
                                   in1=rows[0:64, 16, 0:L], op0=ALU.max, op1=ALU.add).then_inc(sp, 1)
            dve.wait_ge(K["sp_act"], 3)
            V.tensor_scalar(C["alog"][0:64, :], C["alog"][0:64, :], -1.0, None, ALU.mult).then_inc(sp, 1)
            dve.wait_ge(sp, 9)
            V.tensor_scalar(rows[0:64, 10, PAD:TC], rows[0:64, 7, PAD:TC], C["alog"][0:64, :], None, ALU.mult) \
                .then_inc(sp, 1)
            dve.wait_ge(sp, 10)
            for c in range(NC):
                V.tensor_tensor_scan(out=rows[0:64, 5, c * Q:(c + 1) * Q], data0=rows[0:64, 11, c * Q:(c + 1) * Q],
                                     data1=rows[0:64, 10, c * Q:(c + 1) * Q], initial=0.0, op0=ALU.mult,
                                     op1=ALU.add).then_inc(K["csum"], 1)
            for j in range(G_TILES):
                cut_tile("G", 0, j + 1)
            for n, dst in enumerate((col_gcs, col_te, col_dt, col_eg)):
                dve.wait_ge(K["colps"], n + 1)
                V.tensor_copy(dst[:, :, :], m[2 + n % 2][:, 0:NC * 64].rearrange("p (c h) -> p c h", h=64)) \
                    .then_inc(K["colcp"], 1)
            dve.wait_ge(K["colps"], 5)
            V.tensor_copy(col_beta[:, :, :], m[2][:, 0:NC * 64].rearrange("p (c h) -> p c h", h=64)[:, :, 0:16]) \
                .then_inc(K["colcp"], 1)
            dve.wait_ge(K["colcp"], 5)
            V.tensor_scalar(col_ngcs[:, :, :], col_gcs[:, :, :], -1.0, None, ALU.mult).then_inc(K["colder"], 1)
            V.tensor_scalar(col_nbeta[:, :, :], col_beta[:, :, :], -1.0, None, ALU.mult).then_inc(K["colder"], 1)
            dve.wait_ge(K["colder"], 2)
            V.tensor_tensor(col_nbeg[:, :, :], col_nbeta[:, :, :], col_eg[:, :, 32:48], ALU.mult).then_inc(K["colder"], 1)
            V.memset(qkv[:, :, 0:PAD], 0.0).then_inc(K["colder"], 1)
            V.memset(KN[:, 0, :], 0.0).then_inc(K["colder"], 1)
            dve.wait_ge(K["colder"], 5)

            def conv(raw, n, weights, block_of, acc, out, done, bias=None, between=None):
                for tap in range(TAPS):
                    if between is not None:
                        between(tap)
                    if tap:
                        dve.wait_ge(K[acc], done + n * tap)
                    for b in range(n):
                        wcol = weights[:, ds(block_of(b) * TAPS + tap, 1)]
                        src = raw[:, b, tap:tap + L]
                        if tap == 0:
                            V.tensor_scalar(out[:, b, :], src, wcol, None if bias is None else bias[:, ds(block_of(b), 1)],
                                            ALU.mult, ALU.bypass if bias is None else ALU.add).then_inc(K[acc], 1)
                        else:
                            V.scalar_tensor_tensor(out=out[:, b, :], in0=src, scalar=wcol, in1=out[:, b, :],
                                                   op0=ALU.mult, op1=ALU.add).then_inc(K[acc], 1)

            def three(bank, n=NC):
                return bank[:, 0:n * Q].rearrange("p (c q) -> p c q", q=Q)

            def fill(fill_plan, segment, it):
                return lambda n: cuts(cut, segment, it, fill_plan, n)

            def mixer_g(h, fill):
                h1 = plus1(dve, h)
                w = dve.wait_ge
                w(K["projev"], h * G_TILES + 3)
                conv(g_raw, 3, C["g_conv"], lambda b: b * GDN_HEADS + h, "conv_tap", cv, 3 * TAPS * h)
                fill(0)
                w(K["qk_std"], 2 * h1)
                V.reciprocal(qk_rn[:, 1, :], qk_n[:, 1, :]).then_inc(K["qk_rec"], 1)
                w(K["qk_rec"], 2 * h + 1)
                V.tensor_tensor(arena_kn, qkv[:, 1, PAD:TC], qk_rn[:, 1, :], ALU.mult).then_inc(K["kn_done"], 1)
                V.reciprocal(qk_rn[:, 0, N_META:L], qk_n[:, 0, N_META:L]).then_inc(K["qk_rec"], 1)
                w(K["qk_rec"], 2 * h1)
                V.scalar_tensor_tensor(out=QN[:, :, :], in0=three2(qkv[:, 0, Q:TC]), scalar=DK ** -0.5,
                                       in1=three2(qk_rn[:, 0, N_META:L]), op0=ALU.mult, op1=ALU.mult) \
                    .then_inc(K["qn_done"], 1)
                w(K["vt_done"], h1)
                V.tensor_tensor(VB[:, :, :], three(m[2]), bc(col_beta[:, :, ds(h, 1)], [P, NC, Q]), ALU.mult) \
                    .then_inc(K["vb_done"], 1)
                fill(1)
                w(K["e_done"], 3 * h1)
                w(K["kk_done"], h1)
                for c in range(NC):
                    V.scalar_tensor_tensor(out=X[:, c, :], in0=m[4][:, c * Q:(c + 1) * Q],
                                           scalar=col_nbeta[:, c, ds(h, 1)], in1=E[:, c, :], op0=ALU.mult,
                                           op1=ALU.mult).then_inc(K["x_done"], 1)
                w(K["x_done"], 3 * h1)
                V.tensor_tensor(B[:, :, :], X[:, :, :], bc(C["same16"].unsqueeze(1), [P, NC, Q]), ALU.mult) \
                    .then_inc(K["b_done"], 1)
                w(K["qk_done"], h1)
                w(K["et_done"], 2 * h1)
                V.tensor_tensor(AT[:, :, :], three(m[5], 2), ET[:, :, :], ALU.mult).then_inc(K["at_done"], 1)
                w(K["kt_done"], h1)
                V.tensor_tensor(KD[:, :, :], three(m[3], 2), bc(col_te[:, 0:2, ds(32 + h, 1)], [P, 2, Q]), ALU.mult) \
                    .then_inc(K["kd_done"], 1)
                fill(2)
                w(K["xt_done"], h1)
                V.tensor_tensor(BT[:, :, :], three(m[0]), bc(C["same16"].unsqueeze(1), [P, NC, Q]), ALU.mult) \
                    .then_inc(K["bt_done"], 1)
                w(K["b_done"], h1)
                V.tensor_tensor(PP[:, :, :], B[:, :, :], bc(ident.unsqueeze(1), [P, NC, Q]), ALU.add) \
                    .then_inc(K["p1_done"], 1)
                for n in range(3):
                    V.tensor_tensor(LT[:, n, :, :], m[0][:, Q:TC].rearrange("p (c q) -> p c q", q=Q),
                                    bc(level[:, n:n + 1, :], [P, 2, Q]), ALU.mult).then_inc(K["lt_done"], 1)
                fill(3)
                fill(4)
                w(K["b4_done"], h1)
                w(K["p1_done"], h1)
                V.tensor_tensor(PP[:, :, :], three(m[4]), PP[:, :, :], ALU.add).then_inc(K["p2_done"], 1)
                fill(5)
                w(K["b8_done"], h1)
                w(K["p2_done"], h1)
                V.tensor_tensor(PP[:, :, :], three(m[2]), PP[:, :, :], ALU.add).then_inc(K["p3_done"], 1)
                fill(6)
                w(K["pb8_done"], h1)
                w(K["p3_done"], h1)
                V.tensor_tensor(T[:, :, :], three(m[0]), PP[:, :, :], ALU.add).then_inc(K["t0_done"], 1)
                fill(7)
                fill(8)
                w(K["vn0_done"], h1)
                V.tensor_copy(VN, m[4][:, 0:Q]).then_inc(K["vn0s_done"], 1)

                def grow(bank, n):
                    w(K["tn_done"], 3 * h + n)
                    V.tensor_tensor(T[:, 1:3, :], bank[:, 0:2 * Q].rearrange("p (c q) -> p c q", q=Q), T[:, 1:3, :],
                                    ALU.add).then_inc(K["tu_done"], 1)
                    V.tensor_tensor(TT[:, 1:3, :], bank[:, 2 * Q:4 * Q].rearrange("p (c q) -> p c q", q=Q),
                                    TT[:, 1:3, :], ALU.add).then_inc(K["tu_done"], 1)

                w(K["t0_done"], h1)
                w(K["t0ts_done"], h1)
                fill(9)
                grow(m[2], 1)
                fill(10)
                w(K["ks_done"], 2 * h + 1)
                V.scalar_tensor_tensor(out=RR, in0=m[4][:, 0:Q], scalar=col_nbeg[:, 1, ds(h, 1)], in1=VB[:, 1, :],
                                       op0=ALU.mult, op1=ALU.add).then_inc(K["r_done"], 1)
                fill(11)
                grow(m[3], 2)
                fill(12)
                fill(13)
                w(K["tn_done"], 3 * h + 3)
                V.tensor_tensor(TT[:, 1:3, :], m[2][:, 0:2 * Q].rearrange("p (c q) -> p c q", q=Q), TT[:, 1:3, :],
                                ALU.add).then_inc(K["tu_done"], 1)
                fill(14)
                w(K["vn_done"], 2 * h + 1)
                V.tensor_copy(VN, m[5][:, 0:Q]).then_inc(K["vns_done"], 1)
                fill(15)
                w(K["su_done"], h1)
                w(K["eg_done"], h1)
                w(K["o_done"], 2 * h + 1)
                V.scalar_tensor_tensor(out=S, in0=S, scalar=EG[:, 0, Q - 1:Q], in1=m[0][:, 0:Q], op0=ALU.mult,
                                       op1=ALU.add).then_inc(K["s2_done"], 1)
                fill(16)
                w(K["ks_done"], 2 * h + 2)
                V.scalar_tensor_tensor(out=RR, in0=m[4][:, 0:Q], scalar=col_nbeg[:, 2, ds(h, 1)], in1=VB[:, 2, :],
                                       op0=ALU.mult, op1=ALU.add).then_inc(K["r_done"], 1)
                fill(17)
                w(K["vn_done"], 2 * h + 2)
                V.tensor_copy(VN, m[5][:, 0:Q]).then_inc(K["vns_done"], 1)
                fill(18)
                fill(19)
                w(K["onstd_done"], h1)
                V.reciprocal(o_rn, o_n).then_inc(K["onrec_done"], 1)
                w(K["gsilu"], h1)
                w(K["onrec_done"], 2 * h + 1)
                V.scalar_tensor_tensor(out=o_rn, in0=o_rn, scalar=C["g_nw"], in1=gate_s, op0=ALU.mult,
                                       op1=ALU.mult).then_inc(K["onrec_done"], 1)
                w(K["onrec_done"], 2 * h + 2)
                V.tensor_tensor(y_gdn[:, h, :], m[1][:, 0:SEQ], o_rn, ALU.mult).then_inc(K["og_done"], 1)
                fill(20)

            arena_kn = KN[:, :, :].rearrange("p c q -> p (c q)")[:, PAD:TC]

            def three2(ap):
                return ap.rearrange("p (c q) -> p c q", q=Q)

            mixer_g(0, fill(G_FILL, "G", 1))
            with dve.Fori(1, GDN_HEADS - 1) as h:
                mixer_g(h, fill(G_FILL, "G", h + 1))
            mixer_g(GDN_HEADS - 1, fill(G_FILL_LAST, "S", 0))
            V.memset(xbc[:, :, 0:PAD], 0.0).then_inc(K["s_zero"], 1)
            dve.wait_ge(K["s_zero"], 1)

            def group_s(g, fill):
                g1 = plus1(dve, g)
                w = dve.wait_ge
                w(K["projev"], GDN_HEADS * G_TILES + g * S_TILES + 2 + XB)
                conv(s_raw, 2 + XB, C["s_conv"],
                     lambda b: (XB * SSD_GROUPS + SSD_GROUPS * b + g) if b < 2 else (XB * g + b - 2),
                     "s_tap", cv6, (2 + XB) * TAPS * g, bias=C["s_convb"],
                     between=lambda tap: fill(0) if tap == 2 else None)
                fill(1)
                for c in range(NC):
                    w(K["s_xt"], NC * g + c + 1)
                    V.tensor_tensor(XC[:, c, :].rearrange("p (r d) -> p r d", d=SSD_HD),
                                    m[1 + c][:, :].rearrange("p (r d) -> p r d", d=SSD_HD),
                                    bc(col_dt[:, c, ds(R * g, R)].unsqueeze(2), [P, R, SSD_HD]), ALU.mult) \
                        .then_inc(K["s_xc"], 1)
                fill(2)
                w(K["s_we"], 2 * R * g1)
                w(K["s_cbt"], g1)
                for c in range(2):
                    tok = slice(c * Q, (c + 1) * Q)
                    V.tensor_tensor(WE[:, :, tok], WE[:, :, tok], bc(m[4][:, tok].unsqueeze(1), [P, R, Q]),
                                    ALU.mult).then_inc(K["s_w"], 1)
                fill(3)
                fill(4)
                w(K["s_dec"], g1)
                w(K["s_s1c"], g1)
                V.tensor_tensor(SS[:, 1, :].rearrange("p (r d) -> p r d", d=SSD_HD),
                                SS[:, 0, :].rearrange("p (r d) -> p r d", d=SSD_HD),
                                bc(decay_s.unsqueeze(2), [P, R, SSD_HD]), ALU.mult).then_inc(K["s_s2a"], 1)
                w(K["s_s2a"], g1)
                w(K["s_su"], g1)
                V.tensor_tensor(SS[:, 1, :], m[0][:, :], SS[:, 1, :], ALU.add).then_inc(K["s_s2"], 1)
                fill(5)
                fill(6)
                w(K["s_y"], 2 * g1)
                for b in range(XB):
                    V.scalar_tensor_tensor(out=y_g[:, b, :], in0=xbc[:, 2 + b, Q:TC],
                                           scalar=C["s_D"][:, ds(XB * g + b, 1)], in1=m[1 + b][:, 0:SEQ],
                                           op0=ALU.mult, op1=ALU.add).then_inc(K["s_yd"], 1)
                w(K["s_yd"], XB * g1)
                w(K["s_zsilu"], g1)
                V.tensor_tensor(y_g[:, :, :], y_g[:, :, :], z_s[:, :, :], ALU.mult).then_inc(K["s_yz"], 1)
                fill(7)
                w(K["s_std"], g1)
                V.reciprocal(y_rn, y_rn).then_inc(K["s_rec"], 1)
                w(K["s_rec"], g1)
                for b in range(XB):
                    V.scalar_tensor_tensor(out=y_ssd[:, XB * g + b, :], in0=y_g[:, b, :],
                                           scalar=C["s_nw"][:, ds(XB * g + b, 1)], in1=y_rn, op0=ALU.mult,
                                           op1=ALU.mult).then_inc(K["s_out"], 1)

            group_s(0, fill(S_FILL, "S", 1))
            with dve.Fori(1, SSD_GROUPS - 1) as g:
                group_s(g, fill(S_FILL, "S", g + 1))
            group_s(SSD_GROUPS - 1, lambda n: None)

            def merge(n):
                n1 = plus1(dve, n)
                if not is_first(n):
                    dve.wait_ge(K["m_out"], 2 * n)
                for i in range(2):
                    cut_tile("M", n, 2 * i + 1)
                    if is_first(n):
                        for part in range(4):
                            dve.wait_ge(K["x_hi"], 4 + 4 * i + part + 1)
                            ks = slice(part * QT, (part + 1) * QT)
                            V.tensor_tensor(y_hl[i][1][:, ks, :], (y_ssd, y_gdn)[i][:, ks, :],
                                            y_hl[i][0][:, ks, :].bitcast(F32), ALU.subtract).then_inc(K["x_lo"], 1)
                    cut_tile("M", n, 2 * i + 2)
                    dve.wait_ge(K["m_sigd"], 2 * n + i + 1)
                    dve.wait_ge(K["quarter_done"], 4 * (tile_no("M", n, 2 * i + 1) + 1))
                    V.tensor_tensor(m_mul[:, i, :], (PA[1], m[1])[i][:, 0:SEQ], m_sig[:, i, :], ALU.mult) \
                        .then_inc(K["m_muld"], 1)
                dve.wait_ge(K["m_muld"], 2 * n1)
                V.tensor_tensor(m_mul[:, 2, :], m_mul[:, 0, :], m_mul[:, 1, :], ALU.add).then_inc(K["m_out"], 1)
                dve.wait_ge(K["m_out"], 2 * n + 1)
                V.tensor_copy(m_hl[0][:, n, :], m_mul[:, 2, :]).then_inc(K["m_out"], 1)
                dve.wait_ge(K["m_out"], 2 * n1)
                V.tensor_tensor(m_hl[1][:, n, :], m_mul[:, 2, :], m_hl[0][:, n, :].bitcast(F32), ALU.subtract) \
                    .then_inc(K["m_lo"], 1)

            merge(0)
            with dve.Fori(1, KT) as n:
                merge(n)
            o_banks = (m[2], m[3], m[4], m[5])
            with dve.Fori(0, O_TILES // ROUND) as n:
                for j in range(ROUND):
                    cut_tile("O", n, j + 1)
                    dve.wait_ge(K["h_moved"], 16)
                    dve.wait_ge(K["quarter_done"], 4 * (tile_no("O", n, j) + 1))
                    V.tensor_tensor(h2[:, n * ROUND + j, :], h2[:, n * ROUND + j, :], o_banks[j][:, 0:SEQ], ALU.add) \
                        .then_inc(K["h2_done"], 1)
            dve.wait_ge(K["norm_std"], 2)
            V.reciprocal(f_rn, f_rn).then_inc(K["norm_rec"], 1)
            dve.wait_ge(K["norm_rec"], 2)
            for k in range(KT):
                V.scalar_tensor_tensor(out=h2_sq[:, k, :], in0=h2[:, k, :], scalar=C["w_ffn"][:, k:k + 1], in1=f_rn,
                                       op0=ALU.mult, op1=ALU.mult).then_inc(K["normed"], 1)
            for part in range(4):
                dve.wait_ge(K["x_hi"], 12 + part + 1)
                ks = slice(part * QT, (part + 1) * QT)
                V.tensor_tensor(nf[1][:, ks, :], h2_sq[:, ks, :], nf[0][:, ks, :].bitcast(F32), ALU.subtract) \
                    .then_inc(K["x_lo"], 1)

            def top16(values, spare, n, out_s, out_i, top_key, idx_key, done, ready, n_ready):
                def w(key, value):
                    dve.wait_ge(K[key], value)
                    V.memset(soft[:, 2, :], 0.0)

                w(ready, n_ready)
                for r in range(n):
                    V.max(out_s[:, r, 0:8], values[r]).then_inc(K[top_key], 1)
                w(top_key, done + n)
                for r in range(n):
                    V.match_replace(out=spare[r], in_to_replace=out_s[:, r, 0:8], in_values=values[r],
                                    imm_value=-3.0e38).then_inc(K[top_key], 1)
                for r in range(n):
                    V.max_index(out_i[:, r, 0:8], out_s[:, r, 0:8], values[r]).then_inc(K[idx_key], 1)
                w(top_key, done + 2 * n)
                for r in range(n):
                    V.max(out_s[:, r, 8:16], spare[r]).then_inc(K[top_key], 1)
                w(top_key, done + 3 * n)
                for r in range(n):
                    V.max_index(out_i[:, r, 8:16], out_s[:, r, 8:16], spare[r]).then_inc(K[idx_key], 1)

            def route(n, e):
                hd = 2 * n + e
                hd1 = plus1(dve, hd)
                w = dve.wait_ge
                w(K["sc_ps"], hd1)
                V.tensor_copy(sc[:, e, :, :], PA[e][:, :].rearrange("p (a b) -> p a b", b=N_KEYS)).then_inc(K["sc_cp"], 1)
                top16([sc[:, e, a, :] for a in range(4)], [sc2[:, a, :] for a in range(4)], 4, top_s, top_u,
                      "r_top", "r_idx", 12 * hd, "sc_cp", hd1)
                w(K["r_idx"], 8 * hd1)
                V.tensor_copy(top_i[:, :, :], top_u).then_inc(K["r_cast"], 1)
                for half in range(2):
                    V.tensor_tensor(cand[:, half, :, :], bc(top_s[:, half, :].unsqueeze(2), [P, TOPK, TOPK]),
                                    bc(top_s[:, 2 + half, :].unsqueeze(1), [P, TOPK, TOPK]), ALU.add) \
                        .then_inc(K["r_cand"], 1)
                top16([cand[:, a, :, :].rearrange("p a b -> p (a b)") for a in range(2)],
                      [cand2[:, a, :] for a in range(2)], 2, best, pos_u, "r_best", "r_pos", 6 * hd, "r_cand", 2 * hd1)
                for half in range(2):
                    V.tensor_scalar(soft[:, 0, half:half + 1], best[:, half, 0:1], -1.0, None, ALU.mult) \
                        .then_inc(K["r_neg"], 1)
                w(K["r_pos"], 4 * hd1)
                V.tensor_scalar(pos_hi, pos_u, 4, None, ALU.logical_shift_right).then_inc(K["r_bits"], 1)
                V.tensor_scalar(pos_lo, pos_u, 15, None, ALU.bitwise_and).then_inc(K["r_bits"], 1)
                w(K["r_bits"], 4 * hd + 2)
                V.tensor_copy(pos_f[:, 0, :, :], pos_hi).then_inc(K["r_bits"], 1)
                V.tensor_copy(pos_f[:, 1, :, :], pos_lo).then_inc(K["r_bits"], 1)
                w(K["r_bits"], 4 * hd + 4)
                w(K["r_cast"], hd1)
                for f in range(2):
                    V.tensor_tensor(pick[:, f, :, :],
                                    bc(pos_f[:, f, :, :].rearrange("p a b -> p (a b)").unsqueeze(2), [P, 2 * TOPK, TOPK]),
                                    bc(C["rank"].unsqueeze(1), [P, 2 * TOPK, TOPK]), ALU.is_equal) \
                        .then_inc(K["r_mul"], 1)
                w(K["r_mul"], 6 * hd + 2)
                for f in range(2):
                    for half in range(2):
                        V.tensor_tensor(pick[:, f, half * TOPK:(half + 1) * TOPK, :],
                                        pick[:, f, half * TOPK:(half + 1) * TOPK, :],
                                        bc(top_i[:, 2 * f + half, :].unsqueeze(1), [P, TOPK, TOPK]), ALU.mult) \
                            .then_inc(K["r_mul"], 1)
                w(K["r_mul"], 6 * hd1)
                for f in range(2):
                    for half in range(2):
                        V.tensor_reduce(tab_t[:, f, half, ds(hd * TOPK, TOPK)],
                                        pick[:, f, half * TOPK:(half + 1) * TOPK, :], AX.X, ALU.add) \
                            .then_inc(K["r_pick"], 1)
                w(K["r_exp"], 2 * hd1)
                V.reciprocal(soft[:, 2, :], soft[:, 1, :]).then_inc(K["r_neg2"], 1)
                w(K["r_neg2"], hd1)
                for half in range(2):
                    V.tensor_scalar(tab_t[:, 2, half, ds(hd * TOPK, TOPK)], ebest[:, half, :],
                                    soft[:, 2, half:half + 1], None, ALU.mult).then_inc(K["r_gate"], 1)

            def queries(n, last=False):
                for e in range(2):
                    for k in range(2):
                        if not (last and (e, k) == (1, 1)):
                            cut_tile("Q", n, 2 * e + k + 1)
                for e in range(2):
                    route(n, e)

            queries(0)
            with dve.Fori(1, Q_TILES // ROUND - 1) as n:
                queries(n)
            queries(Q_TILES // ROUND - 1, last=True)

            dve.wait_ge(K["t_ps"], 1)
            V.tensor_copy(tab_hk[:, 0:2, :], m[0][:, :].rearrange("p (f t) -> p f t", t=SEQ)).then_inc(K["t_cp"], 1)
            V.tensor_copy(tab_hk[:, 2, :], m[1][:, 0:SEQ]).then_inc(K["t_cp"], 1)
            dve.wait_ge(K["t_cp"], 2)

            def spread(n):
                for e in range(2):
                    if not is_first(n):
                        dve.wait_ge(K["oh_ps"], 2 * n + e - 1)
                    for u in range(4):
                        t = n * 8 + 4 * e + u
                        V.tensor_scalar(oh[:, e, u, 0, :], iota, tab_hk[:, 0, ds(t, 1)], None, ALU.is_equal) \
                            .then_inc(K["oh_d"], 1)
                        V.tensor_scalar(oh[:, e, u, 1, :], iota, tab_hk[:, 1, ds(t, 1)], tab_hk[:, 2, ds(t, 1)],
                                        ALU.is_equal, ALU.mult).then_inc(K["oh_d"], 1)

            spread(0)
            with dve.Fori(1, SEQ // 8) as n:
                spread(n)
            dve.wait_ge(K["oh_cp"], SEQ // 4)

            cut_tile("D", 0, 0)
            with dve.Fori(0, N_KEYS // ROUND) as n:
                for j in range(ROUND):
                    cut_tile("D", n, j + 1)
                    i = n * ROUND + j
                    dve.wait_ge(K["d_gelu"], i + 1)
                    V.tensor_tensor(gates[:, i, :], gates[:, i, :], gelu[:, j % 2, :], ALU.mult) \
                        .then_inc(K["d_gate"], 1)
            dve.wait_ge(K["d_gate"], N_KEYS)

            def cut_gates(n, j):
                i = n * ROUND + j
                dve.wait_ge(K["a_hi"], i + 1)
                V.tensor_tensor(a_hl[1][:, j % 2, :], gates[:, i, :], a_hl[0][:, j % 2, :].bitcast(F32), ALU.subtract) \
                    .then_inc(K["a_lo"], 1)

            def up(n, last=False):
                for j in range(ROUND):
                    if not (last and j == ROUND - 1):
                        cut_gates(n, j + 1)
                        cut_tile("U", n, j + 1)

            cut_gates(0, 0)
            with dve.Fori(0, N_KEYS // ROUND - 1) as n:
                up(n)
            up(N_KEYS // ROUND - 1, last=True)
            dve.wait_ge(K["quarter_done"], 4 * END)
            dve.wait_ge(K["h_moved"], 48)
            for b in range(KT // 2):
                V.tensor_tensor(h3[:, 2 * b:2 * b + 2, :], banks[b][:, :].rearrange("p (a t) -> p a t", t=SEQ),
                                h2b[:, 2 * b:2 * b + 2, :], ALU.add).then_inc(K["h3_done"], 1)
            dve.wait_ge(K["norm_std"], 3)
            V.reciprocal(h3_rn, h3_rn).then_inc(K["norm_rec"], 1)
            dve.wait_ge(K["norm_rec"], 3)
            for k in range(KT):
                V.scalar_tensor_tensor(out=h3[:, k, :], in0=h3[:, k, :], scalar=C["w_fin"][:, k:k + 1], in1=h3_rn,
                                       op0=ALU.mult, op1=ALU.mult).then_inc(K["out_done"], 1)

        @block.gpsimd
        def _(pool):
            def load_g(h):
                pool.dma_start(g_row[:, :, :], gcs_d[ds(32 + h, 1), :].rearrange("o (c q) -> (o c) q", q=Q)
                               .partition_broadcast(P)).then_inc(K["rows_in"], 16)

            def load_s(g):
                pool.dma_start(s_row[:, :, :], bc(gcs_d[ds(R * g, R), Q:TC].unsqueeze(0), [P, R, 2 * Q])) \
                    .then_inc(K["srows_in"], 16)

            pool.wait_ge(K["gcs_out"], 16)
            load_g(0)
            load_s(0)
            pool.wait_ge(K["colder"], 5)

            def mixer_g(h, last=False):
                h1 = plus1(pool, h)
                pool.wait_ge(K["rows_in"], 16 * h1)
                if not is_first(h):
                    pool.wait_ge(K["eg_done"], h)
                G.tensor_tensor(GE[:, :, :], bc(C["below"].unsqueeze(1), [P, NC, Q]), g_row[:, :, :], ALU.subtract) \
                    .then_inc(K["gm_done"], 1)
                G.tensor_tensor(GT[:, :, :], g_row[:, 1:3, :], C["upto"].rearrange("p (c q) -> p c q", q=Q), ALU.add) \
                    .then_inc(K["gm_done"], 1)
                pool.wait_ge(K["gm_done"], 2 * h1)
                pool.wait_ge(K["eg_done"], h1)
                if not last:
                    load_g(h + 1)
                pool.wait_ge(K["qn_done"], h1)
                G.tensor_tensor(QG[:, :, :], QN[:, :, :], EG[:, :, :], ALU.mult).then_inc(K["qg_done"], 1)

            mixer_g(0)
            with pool.Fori(1, GDN_HEADS - 1) as h:
                mixer_g(h)
            mixer_g(GDN_HEADS - 1, last=True)
            pool.wait_ge(K["og_done"], GDN_HEADS)

            def group_s(g, last=False):
                g1 = plus1(pool, g)
                pool.wait_ge(K["srows_in"], 16 * g1)
                if not is_first(g):
                    pool.wait_ge(K["s_y"], 2 * g)
                G.tensor_tensor(WE[:, :, :], s_row[:, :, :], bc(C["upto"].unsqueeze(1), [P, R, 2 * Q]),
                                ALU.add).then_inc(K["s_gm"], 1)
                pool.wait_ge(K["s_gm"], g1)
                pool.wait_ge(K["s_dec"], g1)
                if not last:
                    load_s(g + 1)
                pool.wait_ge(K["s_silu"], g1)
                G.tensor_tensor(EC[:, :, :], EC[:, :, :], bc(xbc[:, 1:2, Q:TC], [P, R, 2 * Q]), ALU.mult) \
                    .then_inc(K["s_cg"], 1)
                for c in range(2):
                    pool.wait_ge(K["s_xc"], NC * g + c + 1)
                    G.tensor_tensor(XE[:, c, :].rearrange("p (r d) -> p r d", d=SSD_HD),
                                    XC[:, c, :].rearrange("p (r d) -> p r d", d=SSD_HD),
                                    bc(col_te[:, c, ds(R * g, R)].unsqueeze(2), [P, R, SSD_HD]), ALU.mult) \
                        .then_inc(K["s_xe"], 1)

            group_s(0)
            with pool.Fori(1, SSD_GROUPS - 1) as g:
                group_s(g)
            group_s(SSD_GROUPS - 1, last=True)


def layout(x, meta_tokens, norm_mix_w, w_in, ssd_conv_w, ssd_conv_b, ssd_dt_bias, ssd_A_log, ssd_D,
           ssd_norm_w, gdn_conv_w, gdn_dt_bias, gdn_A_log, gdn_norm_w, w_branch_ssd, w_branch_gdn,
           w_out, norm_ffn_w, peer_w_query, peer_sub_keys, peer_expert_down, peer_expert_up, final_norm_w):
    import numpy as np

    f = np.float32
    h = np.concatenate([np.asarray(meta_tokens), np.asarray(x)[0]], 0)
    xT = np.ascontiguousarray(h.T.reshape(KT, P, L).transpose(1, 0, 2))

    w = np.asarray(w_in)[0]
    d_inner, conv = SSD_HEADS * SSD_HD, SSD_HEADS * SSD_HD + 2 * SSD_GROUPS * SSD_STATE
    z0, x0 = 0, d_inner
    b0 = x0 + d_inner
    c0 = b0 + SSD_GROUPS * SSD_STATE
    dt0 = x0 + conv
    q0 = dt0 + SSD_HEADS
    k0, v0 = q0 + GDN_HEADS * DK, q0 + 2 * GDN_HEADS * DK
    gate0 = v0 + GDN_HEADS * DK
    a0 = gate0 + GDN_HEADS * DK
    bb0 = a0 + GDN_HEADS
    m0 = bb0 + GDN_HEADS
    stream = np.zeros((N_TILES, P, KT * P), f)

    def put(n, mat, col, width=P, at=0):
        stream[n].reshape(P, KT, P)[:, :, at:at + width] = \
            mat[:, col:col + width].reshape(KT, P, width).transpose(1, 0, 2)

    put(0, w, dt0, SSD_HEADS, 0)
    put(0, w, a0, GDN_HEADS, 32)
    put(0, w, bb0, GDN_HEADS, 64)
    for i in range(GDN_HEADS):
        for j, c in enumerate((q0, k0, v0, gate0)):
            put(G_AT + G_TILES * i + j, w, c + i * P)
    for g in range(SSD_GROUPS):
        put(S_AT + S_TILES * g, w, b0 + g * P)
        put(S_AT + S_TILES * g + 1, w, c0 + g * P)
        for b in range(XB):
            put(S_AT + S_TILES * g + 2 + b, w, x0 + (g * XB + b) * P)
            put(S_AT + S_TILES * g + 2 + XB + b, w, z0 + (g * XB + b) * P)
    ws, wg, wo, wq = (np.asarray(a)[0] for a in (w_branch_ssd, w_branch_gdn, w_out, peer_w_query))
    for n in range(KT):
        put(M_AT + M_TILES * n, w, m0 + n * P)
        put(M_AT + M_TILES * n + 1, ws, n * P)
        put(M_AT + M_TILES * n + 2, w, m0 + D_MODEL + n * P)
        put(M_AT + M_TILES * n + 3, wg, n * P)
        put(O_AT + n, wo, n * P)
        put(Q_AT + n, wq, n * P)

    down = np.asarray(peer_expert_down)[0].reshape(N_KEYS, P, KT, P)
    down = np.ascontiguousarray(down.transpose(0, 3, 2, 1)).reshape(N_KEYS, P, KT * P)
    up = np.ascontiguousarray(np.asarray(peer_expert_up)[0].reshape(N_KEYS, P, D_MODEL))

    c = np.zeros((P, N_CONST), f)

    def const(name, a):
        at, n = CONST[name]
        a = np.asarray(a).reshape(-1, n)
        c[0:len(a), at:at + n] = a

    i = np.arange(P)
    const("ident", i[:, None] == i)
    const("ones", np.ones((P, P)))
    const("same16", (i[:, None] // 16) == (i // 16))
    const("level", np.concatenate([((i[:, None] // (2 * s)) == (i // (2 * s))) & ((i[:, None] // s) != (i // s))
                                   for s in (16, 32, 64)], 1))
    const("below", np.where(i[:, None] > i, 0.0, NEG))
    const("upto", np.tile(np.where(i[:, None] <= i, 0.0, NEG), (1, 2)))
    const("iota", np.tile(i, (P, 1)))
    const("rank", np.tile(np.arange(TOPK), (P, 1)))

    def blocks(a):
        t = a.shape[0]
        return a.reshape(t, -1, P).transpose(2, 1, 0).reshape(P, -1)

    const("g_conv", blocks(np.asarray(gdn_conv_w)[0]))
    const("s_conv", blocks(np.asarray(ssd_conv_w)[0]))
    const("s_convb", blocks(np.asarray(ssd_conv_b)))
    const("s_D", blocks(np.repeat(np.asarray(ssd_D)[0], SSD_HD)[None]))
    const("s_nw", blocks(np.asarray(ssd_norm_w)))
    const("g_nw", np.asarray(gdn_norm_w)[0])
    const("w_mix", blocks(np.asarray(norm_mix_w)))
    const("w_ffn", blocks(np.asarray(norm_ffn_w)))
    const("w_fin", blocks(np.asarray(final_norm_w)[None]))
    const("dtb", np.concatenate([np.asarray(ssd_dt_bias)[0], np.asarray(gdn_dt_bias)[0]]))
    const("alog", np.concatenate([np.asarray(ssd_A_log)[0], np.asarray(gdn_A_log)[0]]))
    const("eps", np.full((P, 1), EPS))
    const("keysT", np.asarray(peer_sub_keys)[0].transpose(2, 0, 1).reshape(P, -1))
    return xT, stream, down, up, c


def kernel(**inputs):
    import numpy as np
    import concourse.bacc as bacc
    from concourse.bass_utils import run_bass_kernel_spmd as run

    nc = bacc.Bacc("TRN2", target_bir_lowering=False, num_devices=1)
    names = ("xT", "w_stream", "down", "up", "const")
    arrays = dict(zip(names, layout(**inputs)))
    args = [nc.dram_tensor(n, arrays[n].shape, F32, kind="ExternalInput").ap() for n in names]
    out = nc.dram_tensor("out", (P, KT * SEQ), F32, kind="ExternalOutput").ap()
    build(nc, *args, out)
    r = run(nc, [arrays], core_ids=[0])
    o = r.results[0]["out"].reshape(P, KT, SEQ)
    return np.ascontiguousarray(o.transpose(2, 1, 0)).reshape(1, SEQ, D_MODEL)
```

```python
import concourse.bass as bass
from concourse import mybir
from contextlib import ExitStack

F32 = mybir.dt.float32
F32R = mybir.dt.float32r
U32 = mybir.dt.uint32
ALU = mybir.AluOpType
ACT = mybir.ActivationFunctionType
AX = mybir.AxisListType
ds = bass.ds

P = 128
D_MODEL = 2048
KT = D_MODEL // P
N_META = 16
SEQ = 256
L = N_META + SEQ
Q = 128
NC = 3
TC = NC * Q
PAD = TC - L
TAPS = 4
SSD_HEADS, SSD_HD, SSD_GROUPS, SSD_STATE = 32, 64, 4, 128
R = SSD_HEADS // SSD_GROUPS
XB = R * SSD_HD // P
GDN_HEADS, DK = 16, 128
PEER_HEADS, N_KEYS, TOPK = 8, 128, 16
HK = PEER_HEADS * TOPK
EPS = 1e-6
NEG = -1e30

G_TILES, S_TILES, M_TILES, O_TILES, Q_TILES = 4, 2 + 2 * XB, 4, 16, 16
ROUND = 4
D_ROUND = 8
D_ROUTING = 10
G_AT = 1
S_AT = G_AT + G_TILES * GDN_HEADS
M_AT = S_AT + S_TILES * SSD_GROUPS
O_AT = M_AT + M_TILES * KT
Q_AT = O_AT + O_TILES
N_TILES = Q_AT + Q_TILES
D_AT, U_AT = N_TILES, N_TILES + N_KEYS
END = U_AT + N_KEYS
SEGMENTS = {"G": (G_AT, G_TILES), "S": (S_AT, S_TILES), "M": (M_AT, ROUND), "O": (O_AT, ROUND),
            "Q": (Q_AT, ROUND), "D": (D_AT, D_ROUND), "U": (U_AT, ROUND)}
QT = KT // 4
QW = QT * P
HALVES = 4


def tile_no(segment, it, j):
    at, per = SEGMENTS[segment]
    return at + j + per * it


def half_slot(segment, j, half):
    return (2 * (SEGMENTS[segment][0] + j) + half) % HALVES


def half_use(segment, it, j, half):
    at, per = SEGMENTS[segment]
    return (2 * (at + j) + half) // HALVES + (per // 2) * it


G_FILL = (1, 1, 2, 1, 1, 1, 1, 1, 1, 1, 1, 0, 0, 0, 1, 1, 1, 1, 0, 0, 0)
G_FILL_LAST = (5, 5, 2, 2, 2, 2, 2, 2, 2, 2, 1, 1, 1, 1, 1, 2, 1, 2, 2, 1, 1)
S_FILL = (3, 5, 6, 6, 4, 4, 8, 4)
S_FILL_LAST = (4, 4, 0, 0, 0, 0, 0, 0)
AHEAD = 3
G_TAPS_AT = (11, 12, 13, 14)
S_TAPS_FIRST = (10, 12, 14, 16)
G_SILU_AT, G_SUMS_AT, G_ROOTS_AT = 15, 18, 18
S_TAPS_AT = (24, 26, 28, 33)
S_OUT_AT, S_SQUARES_AT = 30, 33
assert sum(G_FILL) == 4 * G_TILES and sum(G_FILL_LAST) == sum(S_FILL) == 4 * S_TILES


def filled(fill, n):
    before = sum(fill[:n])
    return range(before, before + fill[n])


CONST = {}
_at = 0
for _name, _n in (("ident", P), ("ones", P), ("same16", P), ("level", 3 * P), ("below", P), ("upto", 2 * P),
                  ("iota", P), ("rank", TOPK), ("g_conv", 48 * TAPS), ("s_conv", 24 * TAPS), ("s_convb", 24), ("s_D", 16),
                  ("s_nw", 16), ("g_nw", 1), ("w_mix", 16), ("w_ffn", 16), ("w_fin", 16), ("dtb", 1),
                  ("alog", 1), ("eps", 1), ("keysT", 2 * N_KEYS)):
    CONST[_name] = (_at, _n)
    _at += _n
N_CONST = _at


def build(nc, xT_d, w_d, down_d, up_d, const_d, out_d):
    ctx = ExitStack()
    with ctx:
        N_ARENA = 44608
        ring = ctx.enter_context(nc.sbuf_tensor("ring", [P, HALVES, 2 * QW], F32))
        hi = ctx.enter_context(nc.sbuf_tensor("w_hi", [P, 4, QW], F32R))
        w_hi_at = nc.sbuf_base - 4 * 4 * QW
        lo = ctx.enter_context(nc.sbuf_tensor("w_lo", [P, 4, QW], F32R))
        arena = ctx.enter_context(nc.sbuf_tensor("arena", [P, N_ARENA], F32))
        base = nc.sbuf_base - 4 * N_ARENA
        banks = [ctx.enter_context(nc.psum_tensor(f"bank{i}", [P, 512], F32)) for i in range(8)]
        PA = banks[0:2]
        m = banks[2:8]
        gcs_d = nc.dram_tensor("gcs_scratch", [64, TC], F32, kind="Internal").ap()
        h2_d = nc.dram_tensor("h2_scratch", [P, KT * SEQ], F32, kind="Internal").ap()

        def sem(name):
            return ctx.enter_context(nc.semaphore(name))

        top = [0]

        def take(*shape, at=None):
            n = 1
            for s in shape:
                n *= s
            if at is not None:
                top[0] = at
            a = arena[:, top[0]:top[0] + n]
            top[0] += n
            assert top[0] <= N_ARENA, (top[0], shape)
            if len(shape) == 2:
                return a.rearrange("p (a b) -> p a b", b=shape[1])
            if len(shape) == 3:
                return a.rearrange("p (a b c) -> p a b c", b=shape[1], c=shape[2])
            if len(shape) == 4:
                return a.rearrange("p (a b c d) -> p a b c d", b=shape[1], c=shape[2], d=shape[3])
            return a

        def in_parts(name, at, *shape):
            n = shape[0] * shape[1]
            return [nc.alloc_sbuf_tensor_at(f"{name}_{part}", [P, *shape], F32R, offset=base + 4 * (at + n * i))[:, :, :]
                    for i, part in enumerate(("hi", "lo"))]

        const = take(N_CONST)
        take(-N_CONST % 8)
        C = {k: const[:, a:a + n] for k, (a, n) in CONST.items()}
        ident, ones, iota = C["ident"], C["ones"], C["iota"]
        level = C["level"].rearrange("p (a b) -> p a b", b=P)
        low_end = top[0]

        n_hl = in_parts("n", low_end, KT, L)
        take(2 * KT, L)
        g_row = take(NC, Q)
        s_row = take(R, 2 * Q)
        y_at = top[0]
        y_gdn = take(KT, SEQ)
        y_ssd = take(KT, SEQ)
        col_gcs, col_ngcs, col_te, col_dt, col_eg = (take(NC, 64) for _ in range(5))
        col_beta, col_nbeta, col_nbeg = (take(NC, 16) for _ in range(3))
        raw_at = top[0]
        g_raw = take(3, TAPS - 1 + L)
        gate_raw = take(SEQ)
        s_raw = take(2 + XB, TAPS - 1 + L)
        z_raw = take(XB, SEQ)
        local = top[0] + -top[0] % 8

        xT = take(KT, L, at=local)
        x_sq = take(KT, L)
        x_rn = take(L)
        rows = take(18, TC)
        cv = take(3, L, at=local)
        qkv = take(3, TC)
        qk_sq = take(2, L)
        qk_n = take(2, L)
        qk_rn = take(2, L)
        KN = take(NC, Q)
        QN = take(2, Q)
        QG = take(2, Q)
        EG = take(2, Q)
        GE = take(NC, Q)
        GT = take(2, Q)
        E = take(NC, Q)
        ET = take(2, Q)
        X = take(NC, Q)
        VB = take(NC, Q)
        KD = take(2, Q)
        AT = take(2, Q)
        B, BT, PP = take(NC, Q), take(NC, Q), take(NC, Q)
        LT = take(3, 2, Q)
        B2, B2T, B4, B4T, B8T = (take(NC, Q) for _ in range(5))
        T, TT = take(NC, Q), take(NC, Q)
        Y = take(2, Q)
        VN, RR, S = take(Q), take(Q), take(Q)
        gate_s, o_sq, o_n, o_rn = (take(SEQ) for _ in range(4))
        assert top[0] <= N_ARENA
        cv6 = take(2 + XB, L, at=local)
        xbc = take(2 + XB, TC)
        Btok = take(2, Q)
        XC = take(NC, R * SSD_HD)
        XE = take(2, R * SSD_HD)
        WE = take(R, 2 * Q)
        EC = take(R, 2 * Q)
        SS = take(2, R * SSD_HD)
        z_s = take(XB, SEQ)
        y_sq = take(XB, SEQ)
        decay_s = take(R)
        y_rn = take(SEQ)
        y_g = take(XB, SEQ)
        y_hl = [in_parts(f"y{i}", local + 2 * KT * SEQ * i, KT, SEQ) for i in range(2)]
        take(4 * KT, SEQ, at=local)
        m_hl = in_parts("m", y_at, KT, SEQ)
        m_sig = take(2, SEQ, at=raw_at)
        m_mul = take(3, SEQ)
        h_in = take(KT, SEQ, at=local)
        h2, h2_sq = h_in, take(KT, SEQ)
        nf = in_parts("nf", low_end, KT, SEQ)
        a_hl = in_parts("a", low_end, 2, SEQ)
        take(2 * KT, SEQ, at=low_end)
        tab_hk = take(3, SEQ)
        f_rn = take(SEQ)
        acts_at = top[0]
        acts = take(N_KEYS, SEQ)
        oh_i = take(4, 4, P, at=low_end + 4 * SEQ)
        oh_j = take(4, 4, P)
        tab_t = take(3, 2, HK, at=acts_at + D_ROUTING * D_ROUND * SEQ)
        qT = take(4, SEQ)
        sc_all = take(4 * PEER_HEADS, N_KEYS)
        sc, sc2 = take(4, N_KEYS), take(4, N_KEYS)
        top_s, top_i = take(4, TOPK), take(4, TOPK)
        top_u = take(4 * TOPK).bitcast(U32).rearrange("p (a b) -> p a b", b=TOPK)
        cand = take(2, TOPK, TOPK)
        cand2 = take(2, TOPK * TOPK)
        best = take(2, TOPK)
        pos_u, pos_hi, pos_lo = (take(2 * TOPK).bitcast(U32).rearrange("p (a b) -> p a b", b=TOPK) for _ in range(3))
        pos_f = take(2, 2, TOPK)
        pick = take(2, 2 * TOPK, TOPK)
        soft = take(3, 2)
        ebest = take(2, TOPK)
        h3 = take(KT, SEQ, at=acts_at)
        h2b = take(KT, SEQ)
        h3_sq = take(KT, SEQ)
        h3_rn = take(SEQ)

        names = """const_in x_in0 x_in1 x_in2 x_in3 quarter_done cut_h cut_l x_hi x_lo m_lo a_hi a_lo w_in0 w_in1 w_in2 w_in3
            normed sp_act sp_part
            beta_rows csum row_exps colps colcp colder gcs_out rows_in srows_in zeroed
            projev conv_tap silu_done gsilu gm_done e_done et_done eg_done
            qk_sqd qk_ss qk_std qk_rec qn_done kn_done vt_done kt_done kk_done qk_done vb_done kd_done
            x_done at_done xt_done b_done bt_done lt_done p1_done b2_done b2s_done b4_done b4s_done p2_done
            b8_done b8s_done p3_done pb8_done t0_done t0t_done t0ts_done y_done ys_done tn_done tu_done
            vn0_done vn0s_done s1_done s1s_done ks_done r_done vn_done vns_done su_done s2_done qg_done
            o_done osq_done on_done onstd_done onrec_done og_done
            norm_sq norm_ss norm_std norm_rec s_zero s_tap s_silu s_zsilu s_gm s_we s_ec s_dec s_cg s_bt s_btok s_xt s_cbt s_xc s_xe s_w s_s1 s_s1c
            s_su s_s2a s_s2 s_y s_yd s_yz s_ysq s_ss s_std s_rec s_out
            m_sigd m_muld m_out h_moved h2_done
            q_copy sc_ps sc_cp r_top r_idx r_cast r_cand r_best r_pos r_bits r_pick r_mul r_neg r_neg2 r_exp
            r_gate r_in t_ps t_cp dist_done ohi_done ohj_done oh_ps d_gelu gated h3_done
            out_done out_in""".split()
        K = {n: sem(n) for n in names}
        X_IN = [K[f"x_in{part}"] for part in range(4)]
        W_IN = [K[f"w_in{s}"] for s in range(HALVES)]

        mm = nc.tensor.matmul
        tr = nc.tensor.transpose
        V = nc.vector
        A = nc.scalar.activation
        G = nc.gpsimd

        def own(c):
            return slice(PAD if c == 0 else 0, Q)

        def bank_own(c):
            return slice(PAD if c == 0 else c * Q, (c + 1) * Q)

        def tokens_of(ap):
            return ap[:, :, :].rearrange("p c q -> p (c q)")[:, PAD:TC]

        def is_first(n):
            return type(n) is int and n == 0

        def plus1(eng, n):
            return n + 1 if type(n) is int else eng.snap(n + 1)

        def bc(ap, shape):
            return ap.to_broadcast(shape)

        def cuts(cut, segment, it, fill, n, then=None):
            for q in filled(fill, n):
                cut(segment, it, (q + AHEAD) // 4, (q + AHEAD) % 4)
                if then is not None:
                    then(q)

        block = ctx.enter_context(nc.Block())

        @block.sync
        def _(sp):
            for part in range(4):
                ks = slice(part * QT, (part + 1) * QT)
                sp.dma_start(xT[:, ks, :], xT_d[:, ks, :]).then_inc(X_IN[part], 16)
            sp.dma_start(const[:, :], const_d).then_inc(K["const_in"], 16)

            def load(segment, it, j, src=None):
                t = tile_no(segment, it, j)
                for half in range(2):
                    if not (type(t) is int and t < HALVES // 2):
                        sp.wait_ge(K["cut_l"], 4 * t + 2 * half - 6)
                    w = w_d[t] if src is None else src.rearrange("o p n -> (o p) n")
                    slot = half_slot(segment, j, half)
                    sp.dma_start(ring[:, slot, :], w[:, half * 2 * QW:(half + 1) * 2 * QW]).then_inc(W_IN[slot], 16)

            load("G", 0, -1)
            for j in range(G_TILES):
                load("G", 0, j)
            with sp.Fori(1, GDN_HEADS) as h:
                for j in range(G_TILES):
                    load("G", h, j)
            with sp.Fori(0, SSD_GROUPS) as g:
                for j in range(S_TILES):
                    load("S", g, j)
            with sp.Fori(0, KT) as n:
                for j in range(ROUND):
                    load("M", n, j)
            for segment, tiles in (("O", O_TILES), ("Q", Q_TILES)):
                with sp.Fori(0, tiles // ROUND) as n:
                    for j in range(ROUND):
                        load(segment, n, j)
            for segment, table, per in (("D", down_d, D_ROUND), ("U", up_d, ROUND)):
                with sp.Fori(0, N_KEYS // per) as n:
                    for j in range(per):
                        load(segment, n, j, src=table[ds(n * per + j, 1)])
            sp.wait_ge(K["quarter_done"], 4 * (U_AT + 3 * KT))
            sp.wait_ge(K["h_moved"], 32)
            sp.dma_start(h2b[:, :, :].rearrange("p k t -> p (k t)"), h2_d).then_inc(K["h_moved"], 16)
            for part in range(4):
                sp.wait_ge(K["out_done"], QT * (part + 1))
                cols = slice(part * QT * SEQ, (part + 1) * QT * SEQ)
                sp.dma_start(out_d[:, cols], h3[:, :, :].rearrange("p k t -> p (k t)")[:, cols]).then_inc(K["out_in"], 16)
            sp.wait_ge(K["out_in"], 4 * 16)

        @block.tensor
        def _(pe):
            def quarter(segment, it, j, part, out, moving, tokens=slice(None)):
                q = 4 * tile_no(segment, it, j) + part
                pe.wait_ge(K["cut_l"], q + 1)
                for k in range(QT):
                    kk = part * QT + k
                    w = slice(k * P, (k + 1) * P)
                    x_hi, x_lo = moving[0][:, kk, tokens], moving[1][:, kk, tokens]
                    mm(out, hi[:, part, w], x_hi, start=(kk == 0), stop=False)
                    mm(out, hi[:, part, w], x_lo, start=False, stop=False)
                    last = mm(out, lo[:, part, w], x_hi, start=False, stop=(kk == KT - 1))
                last.then_inc(K["quarter_done"], 1)

            def project_g(h, q, first=False):
                j, part = q // 4, q % 4
                n = L if j < 3 else SEQ
                if part == 0 and not (first and j < 2):
                    pe.wait_ge(K["projev"], h * G_TILES + j - 1)
                quarter("G", h, j, part, PA[j % 2][:, 0:n], n_hl, slice(L - n, L))

            def project_s(g, q):
                j, part = q // 4, q % 4
                n = L if j < 2 + XB else SEQ
                if part == 0:
                    pe.wait_ge(K["projev"], GDN_HEADS * G_TILES + g * S_TILES + j - 1)
                quarter("S", g, j, part, PA[j % 2][:, 0:n], n_hl, slice(L - n, L))

            def norm_sums(h):
                if not is_first(h):
                    pe.wait_ge(K["tu_done"], 5 * h)
                pe.wait_ge(K["qk_sqd"], h + 1)
                mm(m[2][:, 0:L], ones, qk_sq[:, 0, :], start=True, stop=True)
                mm(m[3][:, 0:L], ones, qk_sq[:, 1, :], start=True, stop=True).then_inc(K["qk_ss"], 1)

            def mixer_g(h, project, nxt=None):
                h1 = plus1(pe, h)
                w = pe.wait_ge

                def fill(n):
                    project(n)
                    if nxt is not None and n == G_SUMS_AT:
                        norm_sums(nxt)

                fill(0)
                w(K["qk_std"], 2 * h1)
                for c in range(NC):
                    last = tr(m[2][:, c * Q:(c + 1) * Q], qkv[:, 2, c * Q:(c + 1) * Q], ident)
                last.then_inc(K["vt_done"], 1)
                fill(1)
                w(K["kn_done"], h1)
                if not is_first(h):
                    w(K["r_done"], 2 * h)
                    w(K["vns_done"], 2 * h)
                for c in range(NC):
                    last = mm(m[4][:, bank_own(c)], KN[:, c, :], KN[:, c, own(c)], start=True, stop=True)
                last.then_inc(K["kk_done"], 1)
                w(K["qn_done"], h1)
                for c in range(2):
                    last = mm(m[5][:, c * Q:(c + 1) * Q], KN[:, c + 1, :], QN[:, c, :], start=True, stop=True)
                last.then_inc(K["qk_done"], 1)
                for c in range(2):
                    last = tr(m[3][:, c * Q:(c + 1) * Q], KN[:, c, :], ident)
                last.then_inc(K["kt_done"], 1)
                fill(2)
                w(K["x_done"], 3 * h1)
                if not is_first(h):
                    w(K["onstd_done"], h)
                for c in range(NC):
                    last = tr(m[0][:, c * Q:(c + 1) * Q], X[:, c, :], ident)
                last.then_inc(K["xt_done"], 1)
                fill(3)
                w(K["b_done"], h1)
                w(K["bt_done"], h1)
                w(K["vb_done"], h1)
                if not is_first(h):
                    w(K["og_done"], h)
                for c in range(NC):
                    mm(m[1][:, bank_own(c)], BT[:, c, :], B[:, c, own(c)], start=True, stop=True)
                    last = mm(m[2][:, bank_own(c)], B[:, c, :], BT[:, c, own(c)], start=True, stop=True)
                last.then_inc(K["b2_done"], 1)
                fill(4)
                w(K["b2s_done"], 2 * h1)
                w(K["lt_done"], 3 * h1)
                w(K["kd_done"], h1)
                w(K["p1_done"], h1)
                for c in range(NC):
                    mm(m[0][:, bank_own(c)], B2T[:, c, :], B2[:, c, own(c)], start=True, stop=True)
                    mm(m[3][:, bank_own(c)], B2[:, c, :], B2T[:, c, own(c)], start=True, stop=True)
                    last = mm(m[4][:, bank_own(c)], B2T[:, c, :], PP[:, c, own(c)], start=True, stop=True)
                last.then_inc(K["b4_done"], 1)
                fill(5)
                w(K["b4s_done"], 2 * h1)
                w(K["p2_done"], h1)
                for c in range(NC):
                    mm(m[1][:, bank_own(c)], B4[:, c, :], B4T[:, c, own(c)], start=True, stop=True)
                    last = mm(m[2][:, bank_own(c)], B4T[:, c, :], PP[:, c, own(c)], start=True, stop=True)
                last.then_inc(K["b8_done"], 1)
                fill(6)
                w(K["b8s_done"], h1)
                w(K["p3_done"], h1)
                for c in range(NC):
                    last = mm(m[0][:, bank_own(c)], B8T[:, c, :], PP[:, c, own(c)], start=True, stop=True)
                last.then_inc(K["pb8_done"], 1)
                fill(7)
                w(K["t0_done"], h1)
                for c in range(NC):
                    last = tr(m[3][:, c * Q:(c + 1) * Q], T[:, c, :], ident)
                last.then_inc(K["t0t_done"], 1)
                fill(8)
                w(K["t0ts_done"], h1)
                for c in range(2):
                    last = mm(m[1][:, c * Q:(c + 1) * Q], LT[:, 0, c, :], T[:, 1 + c, :], start=True, stop=True)
                last.then_inc(K["y_done"], 1)
                mm(m[4][:, 0:Q], TT[:, 0, :], VB[:, 0, :], start=True, stop=True).then_inc(K["vn0_done"], 1)
                fill(9)

                def both(bank, n):
                    w(K["ys_done"], 3 * h + n)
                    for c in range(2):
                        mm(bank[:, c * Q:(c + 1) * Q], TT[:, 1 + c, :], Y[:, c, :], start=True, stop=True)
                        x = mm(bank[:, (2 + c) * Q:(3 + c) * Q], Y[:, c, :], TT[:, 1 + c, :], start=True, stop=True)
                    x.then_inc(K["tn_done"], 1)

                both(m[2], 1)
                w(K["vn0s_done"], h1)
                w(K["at_done"], h1)
                mm(m[5][:, 0:Q], KD[:, 0, :], VN, start=True, stop=True).then_inc(K["s1_done"], 1)
                fill(10)
                w(K["tu_done"], 5 * h + 2)
                for c in range(2):
                    last = mm(m[0][:, c * Q:(c + 1) * Q], LT[:, 1, c, :], T[:, 1 + c, :], start=True, stop=True)
                last.then_inc(K["y_done"], 1)
                w(K["s1s_done"], h1)
                mm(m[4][:, 0:Q], KN[:, 1, :], S, start=True, stop=True).then_inc(K["ks_done"], 1)
                fill(11)
                both(m[3], 2)
                fill(12)
                w(K["tu_done"], 5 * h + 4)
                for c in range(2):
                    last = mm(m[1][:, c * Q:(c + 1) * Q], LT[:, 2, c, :], T[:, 1 + c, :], start=True, stop=True)
                last.then_inc(K["y_done"], 1)
                fill(13)
                w(K["ys_done"], 3 * h + 3)
                for c in range(2):
                    last = mm(m[2][:, c * Q:(c + 1) * Q], Y[:, c, :], TT[:, 1 + c, :], start=True, stop=True)
                last.then_inc(K["tn_done"], 1)
                fill(14)
                w(K["tu_done"], 5 * h + 5)
                w(K["r_done"], 2 * h + 1)
                mm(m[5][:, 0:Q], TT[:, 1, :], RR, start=True, stop=True).then_inc(K["vn_done"], 1)
                fill(15)
                w(K["vns_done"], 2 * h + 1)
                mm(m[0][:, 0:Q], KD[:, 1, :], VN, start=True, stop=True).then_inc(K["su_done"], 1)
                w(K["qg_done"], h1)
                mm(m[1][:, 0:Q], S, QG[:, 0, :], start=True, stop=False)
                mm(m[1][:, 0:Q], VN, AT[:, 0, :], start=False, stop=True).then_inc(K["o_done"], 1)
                fill(16)
                w(K["s2_done"], h1)
                mm(m[4][:, 0:Q], KN[:, 2, :], S, start=True, stop=True).then_inc(K["ks_done"], 1)
                fill(17)
                w(K["r_done"], 2 * h + 2)
                mm(m[5][:, 0:Q], TT[:, 2, :], RR, start=True, stop=True).then_inc(K["vn_done"], 1)
                fill(18)
                w(K["vns_done"], 2 * h + 2)
                mm(m[1][:, Q:2 * Q], S, QG[:, 1, :], start=True, stop=False)
                mm(m[1][:, Q:2 * Q], VN, AT[:, 1, :], start=False, stop=True).then_inc(K["o_done"], 1)
                fill(19)
                w(K["osq_done"], h1)
                mm(m[0][:, 0:SEQ], ones, o_sq, start=True, stop=True).then_inc(K["on_done"], 1)
                fill(20)

            pe.wait_ge(K["const_in"], 16)
            for k in range(KT):
                if k % QT == 0:
                    pe.wait_ge(K["norm_sq"], k // QT + 1)
                last = mm(m[0][:, 0:L], ones, x_sq[:, k, :], start=(k == 0), stop=(k == KT - 1))
            last.then_inc(K["norm_ss"], 1)
            for part in range(4):
                pe.wait_ge(K["x_lo"], part + 1)
                quarter("G", 0, -1, part, m[1][:, 0:L], n_hl)
            for q in range(4 * G_TILES):
                project_g(0, q, first=True)
            for n, (src, key) in enumerate(((5, "csum"), (6, "row_exps"), (7, "sp_part"), (8, "row_exps"), (9, "beta_rows"))):
                if n == 0:
                    pe.wait_ge(K[key], NC)
                elif n in (1, 3):
                    pe.wait_ge(K[key], 2 * NC)
                elif n == 2:
                    pe.wait_ge(K[key], 10)
                else:
                    pe.wait_ge(K[key], 1)
                if n >= 2:
                    pe.wait_ge(K["colcp"], n - 1)
                for c in range(NC):
                    last = tr(m[4 + n % 2][:, c * 64:(c + 1) * 64],
                              rows[0:64, src, c * Q:(c + 1) * Q], ident[0:64, 0:64])
                last.then_inc(K["colps"], 1)

            norm_sums(0)
            mixer_g(0, lambda n: [project_g(1, q) for q in filled(G_FILL, n)], nxt=1)
            with pe.Fori(1, GDN_HEADS - 1) as h:
                mixer_g(h, lambda n: [project_g(h + 1, q) for q in filled(G_FILL, n)], nxt=h + 1)
            mixer_g(GDN_HEADS - 1, lambda n: [project_s(0, q) for q in filled(G_FILL_LAST, n)])

            def group_s(g, fill):
                g1 = plus1(pe, g)
                w = pe.wait_ge
                fill(0)
                fill(1)
                w(K["s_silu"], g1)
                if not is_first(g):
                    w(K["s_yd"], XB * g)
                for c in range(2):
                    last = tr(m[0][:, c * Q:(c + 1) * Q], xbc[:, 0, c * Q:(c + 1) * Q], ident)
                last.then_inc(K["s_bt"], 1)
                for c in range(NC):
                    for b in range(XB):
                        last = tr(m[1 + c][:, b * P:(b + 1) * P], xbc[:, 2 + b, c * Q:(c + 1) * Q], ident)
                    last.then_inc(K["s_xt"], 1)
                for c in range(2):
                    tok = slice((c + 1) * Q, (c + 2) * Q)
                    last = mm(m[4][:, c * Q:(c + 1) * Q], xbc[:, 0, tok], xbc[:, 1, tok], start=True, stop=True)
                last.then_inc(K["s_cbt"], 1)
                fill(2)
                w(K["s_btok"], g1)
                w(K["s_xe"], 2 * g + 1)
                if not is_first(g):
                    w(K["s_std"], g)
                mm(m[5][:, :], Btok[:, 0, :], XE[:, 0, :], start=True, stop=True).then_inc(K["s_s1"], 1)
                fill(3)
                w(K["s_xe"], 2 * g + 2)
                mm(m[0][:, :], Btok[:, 1, :], XE[:, 1, :], start=True, stop=True).then_inc(K["s_su"], 1)
                fill(4)
                for c in range(2):
                    if c == 0:
                        w(K["s_xc"], NC * g1)
                        w(K["s_s1c"], g1)
                        w(K["s_cg"], g1)
                    else:
                        w(K["s_s2"], g1)
                    w(K["s_w"], 2 * g1)
                    for b in range(XB):
                        for e in range(2):
                            r = 2 * b + e
                            rows_ = slice(e * SSD_HD, (e + 1) * SSD_HD)
                            ch = slice(r * SSD_HD, (r + 1) * SSD_HD)
                            tok = slice(c * Q, (c + 1) * Q)
                            mm(m[1 + b][rows_, tok], XC[:, 1 + c, ch], WE[:, r, tok], start=True, stop=False)
                            last = mm(m[1 + b][rows_, tok], SS[:, c, ch], EC[:, r, tok], start=False, stop=True)
                    last.then_inc(K["s_y"], 1)
                    fill(5 + c)
                w(K["s_ysq"], g1)
                for b in range(XB):
                    last = mm(m[5][:, 0:SEQ], ones, y_sq[:, b, :], start=(b == 0), stop=(b == XB - 1))
                last.then_inc(K["s_ss"], 1)
                fill(7)

            group_s(0, lambda n: [project_s(1, q) for q in filled(S_FILL, n)])
            with pe.Fori(1, SSD_GROUPS - 1) as g:
                group_s(g, lambda n: [project_s(g + 1, q) for q in filled(S_FILL, n)])
            tok = slice(N_META, L)

            def gate_quarter(n, q):
                if is_first(n) and q == 0:
                    pe.wait_ge(K["projev"], GDN_HEADS * G_TILES + SSD_GROUPS * S_TILES)
                quarter("M", n, q // 4, q % 4, PA[q // 4][:, 0:SEQ], n_hl, tok)

            group_s(SSD_GROUPS - 1, lambda n: [gate_quarter(0, q) for q in filled(S_FILL_LAST, n)])

            def tile(segment, it, j, out, moving, tokens=slice(None)):
                for part in range(4):
                    quarter(segment, it, j, part, out, moving, tokens)

            def merge(n):
                if not is_first(n):
                    for q in range(8):
                        if q % 4 == 0:
                            pe.wait_ge(K["m_sigd"], 2 * n - 1 + q // 4)
                        gate_quarter(n, q)
                for i in range(2):
                    if is_first(n):
                        if i:
                            pe.wait_ge(K["s_std"], SSD_GROUPS)
                        for part in range(4):
                            pe.wait_ge(K["x_lo"], 4 + 4 * i + part + 1)
                            quarter("M", n, 2 + i, part, m[i][:, 0:SEQ], y_hl[i])
                    else:
                        pe.wait_ge(K["m_muld"], 2 * n - 1 + i)
                        tile("M", n, 2 + i, m[i][:, 0:SEQ], y_hl[i])

            merge(0)
            with pe.Fori(1, KT) as n:
                merge(n)

            o_banks = (m[2], m[3], m[4], m[5])
            pe.wait_ge(K["m_lo"], KT)

            def residual(n):
                for j in range(ROUND):
                    if not is_first(n):
                        pe.wait_ge(K["h2_done"], ROUND * n + j - 3)
                    tile("O", n, j, o_banks[j][:, 0:SEQ], m_hl)

            residual(0)
            with pe.Fori(1, O_TILES // ROUND) as n:
                residual(n)
            for k in range(KT):
                pe.wait_ge(K["norm_sq"], 4 + k + 1)
                last = mm(m[0][:, 0:SEQ], ones, h2_sq[:, k, :], start=(k == 0), stop=(k == KT - 1))
            last.then_inc(K["norm_ss"], 1)
            pe.wait_ge(K["x_lo"], 16)

            def queries(n):
                for e in range(2):
                    for k in range(2):
                        j = 2 * e + k
                        tile("Q", n, j, (m[2], m[3], m[4], m[5])[j][:, 0:SEQ], nf)
                for e in range(2):
                    pe.wait_ge(K["q_copy"], 4 * n + 2 * e + 2)
                    if not is_first(n):
                        pe.wait_ge(K["sc_cp"], 2 * n + e - 1)
                    for k in range(2):
                        for half in range(2):
                            last = mm(PA[e][:, (2 * k + half) * N_KEYS:(2 * k + half + 1) * N_KEYS],
                                      qT[:, 2 * e + k, half * P:(half + 1) * P],
                                      C["keysT"][:, k * N_KEYS:(k + 1) * N_KEYS], start=True, stop=True)
                    last.then_inc(K["sc_ps"], 1)

            queries(0)
            with pe.Fori(1, Q_TILES // ROUND) as n:
                queries(n)

            def down(n):
                for j in range(D_ROUND):
                    if not (is_first(n) and j < 4):
                        pe.wait_ge(K["d_gelu"], D_ROUND * n + j - 3)
                    tile("D", n, j, m[2 + j % 4][:, 0:SEQ], nf)

            down(0)
            with pe.Fori(1, PEER_HEADS + 1) as n:
                down(n)
            pe.wait_ge(K["r_pick"], 4 * PEER_HEADS)
            pe.wait_ge(K["r_gate"], 2 * PEER_HEADS)
            for f in range(3):
                for half in range(2):
                    last = tr(m[0 if f < 2 else 1][:, (2 * (f % 2) + half) * P:(2 * (f % 2) + half + 1) * P],
                              tab_t[:, f, half, :], ident)
            last.then_inc(K["t_ps"], 1)
            with pe.Fori(PEER_HEADS + 1, N_KEYS // D_ROUND) as n:
                down(n)

            def spread(n):
                for e in range(4):
                    pe.wait_ge(K["ohi_done"], 16 * n + 4 * e + 4)
                    pe.wait_ge(K["ohj_done"], 4 * n + e + 1)
                    if is_first(n):
                        pe.wait_ge(K["d_gelu"], N_KEYS)
                    else:
                        pe.wait_ge(K["gated"], 4 * n + e - 3)
                    for u in range(4):
                        last = mm(m[2 + e][:, u * P:(u + 1) * P], oh_j[:, e, u, :], oh_i[:, e, u, :],
                                  start=True, stop=True)
                    last.then_inc(K["oh_ps"], 1)

            spread(0)
            with pe.Fori(1, SEQ // 16) as n:
                spread(n)
            pe.wait_ge(K["gated"], SEQ // 4)

            def up(n):
                for j in range(ROUND):
                    i = n * ROUND + j
                    pe.wait_ge(K["a_lo"], i + 1)
                    for part in range(4):
                        pe.wait_ge(K["cut_l"], 4 * tile_no("U", n, j) + part + 1)
                        for b in range(QT):
                            d = QT * part + b
                            out = banks[d // 2][:, (d % 2) * SEQ:(d % 2 + 1) * SEQ]
                            w = slice(b * P, (b + 1) * P)
                            first = is_first(n) and j == 0 and d % 2 == 0
                            mm(out, hi[:, part, w], a_hl[0][:, j % 2, :], start=first, stop=False, skip_group_check=True)
                            mm(out, hi[:, part, w], a_hl[1][:, j % 2, :], start=False, stop=False, skip_group_check=True)
                            last = mm(out, lo[:, part, w], a_hl[0][:, j % 2, :], start=False, stop=False,
                                      skip_group_check=True)
                        last.then_inc(K["quarter_done"], 1)

            up(0)
            with pe.Fori(1, N_KEYS // ROUND) as n:
                up(n)
            for k in range(KT):
                if k % QT == 0:
                    pe.wait_ge(K["norm_sq"], 4 + KT + k // QT + 1)
                last = mm(banks[0][:, 0:SEQ], ones, h3_sq[:, k, :], start=(k == 0), stop=(k == KT - 1),
                          skip_group_check=True)
            last.then_inc(K["norm_ss"], 1)

        @block.scalar
        def _(act):
            def cut(segment, it, j, part):
                q = 4 * tile_no(segment, it, j) + part
                half = part // 2
                slot = half_slot(segment, j, half)
                if part % 2 == 0:
                    act.wait_ge(W_IN[slot], 16 * (half_use(segment, it, j, half) + 1))
                if not (type(q) is int and q < 4):
                    act.wait_ge(K["quarter_done"], q - 3)
                nc.scalar.copy(hi[:, part, :], ring[:, slot, (part % 2) * QW:(part % 2 + 1) * QW]) \
                    .then_inc(K["cut_h"], 1)

            def cut_tile(segment, it, j):
                for part in range(4):
                    cut(segment, it, j, part)

            for part in range(4):
                act.wait_ge(X_IN[part], 16)
                ks = slice(part * QT, (part + 1) * QT)
                A(x_sq[:, ks, :], xT[:, ks, :], ACT.Square).then_inc(K["norm_sq"], 1)
            cut_tile("G", 0, -1)
            act.wait_ge(K["const_in"], 16)
            act.wait_ge(K["norm_ss"], 1)
            A(x_rn, m[0][:, 0:L], ACT.Sqrt, bias=C["eps"], scale=1.0 / D_MODEL).then_inc(K["norm_std"], 1)

            def high_parts(out, of, normed):
                for part in range(4):
                    act.wait_ge(K["normed"], normed + QT * (part + 1))
                    ks = slice(part * QT, (part + 1) * QT)
                    nc.scalar.copy(out[:, ks, :], of[:, ks, :]).then_inc(K["x_hi"], 1)

            high_parts(n_hl[0], xT, 0)

            def evac_g(h, j):
                act.wait_ge(K["quarter_done"], 4 * (tile_no("G", h, j) + 1))
                if j < 3:
                    nc.scalar.copy(g_raw[:, j, TAPS - 1:], PA[j % 2][:, 0:L]).then_inc(K["projev"], 1)
                else:
                    nc.scalar.copy(gate_raw, PA[j % 2][:, 0:SEQ]).then_inc(K["projev"], 1)

            cut_tile("G", 0, 0)
            act.wait_ge(K["sp_part"], 1)
            A(rows[0:64, 1, 0:L], rows[0:64, 0, 0:L], ACT.Abs).then_inc(K["sp_act"], 1)
            act.wait_ge(K["sp_act"], 1)
            A(rows[0:64, 2, 0:L], rows[0:64, 1, 0:L], ACT.Exp, scale=-1.0).then_inc(K["sp_act"], 1)
            A(C["alog"][0:64, :], C["alog"][0:64, :], ACT.Exp).then_inc(K["sp_act"], 1)
            cut_tile("G", 0, 1)
            evac_g(0, 0)
            act.wait_ge(K["sp_part"], 2)
            A(rows[0:64, 4, 0:L], rows[0:64, 3, 0:L], ACT.Ln).then_inc(K["sp_act"], 1)
            act.wait_ge(K["zeroed"], 1)
            A(rows[0:16, 9, PAD:TC], m[1][64:80, 0:L], ACT.Sigmoid).then_inc(K["beta_rows"], 1)
            cut_tile("G", 0, 2)
            evac_g(0, 1)
            act.wait_ge(K["csum"], NC)
            for c in range(NC):
                A(rows[0:64, 6, c * Q:(c + 1) * Q], rows[0:64, 5, c * Q:(c + 1) * Q], ACT.Exp, scale=-1.0,
                  bias=rows[0:64, 5, (c + 1) * Q - 1:(c + 1) * Q]).then_inc(K["row_exps"], 1)
                A(rows[0:64, 8, c * Q:(c + 1) * Q], rows[0:64, 5, c * Q:(c + 1) * Q], ACT.Exp) \
                    .then_inc(K["row_exps"], 1)
            act.dma_start(gcs_d, rows[0:64, 5, :]).then_inc(K["gcs_out"], 16)
            cut_tile("G", 0, 3)
            evac_g(0, 2)
            for part in range(AHEAD):
                cut("G", 0, 4, part)
            evac_g(0, 3)

            def fill(fill_plan, segment, it, evac_one):
                def at(n, then=None):
                    cuts(cut, segment, it, fill_plan, n, then)
                    for q in filled(fill_plan, n):
                        if q % 4 == 3:
                            evac_one(it, q // 4)
                return at

            def activate(h):
                act.wait_ge(K["conv_tap"], 3 * TAPS * (h + 1))
                A(qkv[:, :, PAD:TC], cv[:, :, :], ACT.Silu).then_inc(K["silu_done"], 1)
                act.wait_ge(K["silu_done"], h + 1)
                A(qk_sq[:, :, :], qkv[:, 0:2, PAD:TC], ACT.Square).then_inc(K["qk_sqd"], 1)

            def norm_roots(h):
                act.wait_ge(K["qk_ss"], h + 1)
                for i in range(2):
                    A(qk_n[:, i, :], m[2 + i][:, 0:L], ACT.Sqrt, bias=C["eps"]).then_inc(K["qk_std"], 1)

            activate(0)
            norm_roots(0)
            act.wait_ge(K["colder"], 3)

            def mixer_g(h, evac, nxt=None):
                h1 = plus1(act, h)
                w = act.wait_ge
                w(K["rows_in"], 16 * h1)
                w(K["gm_done"], 2 * h1)
                for c in range(NC):
                    A(E[:, c, :], GE[:, c, :], ACT.Exp, bias=col_gcs[:, c, ds(32 + h, 1)]).then_inc(K["e_done"], 1)
                for c in range(2):
                    A(ET[:, c, :], GT[:, c, :], ACT.Exp, bias=col_ngcs[:, 1 + c, ds(32 + h, 1)]) \
                        .then_inc(K["et_done"], 1)
                A(EG[:, :, :], g_row[:, 1:3, :], ACT.Exp).then_inc(K["eg_done"], 1)
                evac(0)
                evac(1)
                evac(2)
                evac(3)
                w(K["b2_done"], h1)
                nc.scalar.copy(tokens_of(B2), m[1][:, PAD:TC]).then_inc(K["b2s_done"], 1)
                nc.scalar.copy(tokens_of(B2T), m[2][:, PAD:TC]).then_inc(K["b2s_done"], 1)
                evac(4)
                w(K["b4_done"], h1)
                nc.scalar.copy(tokens_of(B4), m[0][:, PAD:TC]).then_inc(K["b4s_done"], 1)
                nc.scalar.copy(tokens_of(B4T), m[3][:, PAD:TC]).then_inc(K["b4s_done"], 1)
                evac(5)
                w(K["b8_done"], h1)
                nc.scalar.copy(tokens_of(B8T), m[1][:, PAD:TC]).then_inc(K["b8s_done"], 1)
                evac(6)
                evac(7)
                w(K["t0t_done"], h1)
                nc.scalar.copy(tokens_of(TT), m[3][:, PAD:TC]).then_inc(K["t0ts_done"], 1)
                evac(8)

                def copy_y(bank, n):
                    w(K["y_done"], 3 * h + n)
                    nc.scalar.copy(Y[:, :, :], bank[:, 0:2 * Q].rearrange("p (c q) -> p c q", q=Q)) \
                        .then_inc(K["ys_done"], 1)

                copy_y(m[1], 1)
                evac(9)
                w(K["s1_done"], h1)
                nc.scalar.copy(S, m[5][:, 0:Q]).then_inc(K["s1s_done"], 1)
                evac(10)
                copy_y(m[0], 2)
                evac(11)
                evac(12)
                copy_y(m[1], 3)
                for n in range(13, 20):
                    if n == 19:
                        w(K["o_done"], 2 * h1)
                        A(o_sq, m[1][:, 0:SEQ], ACT.Square).then_inc(K["osq_done"], 1)
                    evac(n)
                    if n == G_SILU_AT:
                        w(K["projev"], G_TILES * h1)
                        if not is_first(h):
                            w(K["og_done"], h)
                        A(gate_s, gate_raw, ACT.Silu).then_inc(K["gsilu"], 1)
                        if nxt is not None:
                            activate(nxt)
                    if nxt is not None and n == G_ROOTS_AT:
                        norm_roots(nxt)
                w(K["on_done"], h1)
                A(o_n, m[0][:, 0:SEQ], ACT.Sqrt, bias=C["eps"], scale=1.0 / DK).then_inc(K["onstd_done"], 1)
                evac(20)

            mixer_g(0, fill(G_FILL, "G", 1, evac_g), nxt=1)
            with act.Fori(1, GDN_HEADS - 1) as h:
                mixer_g(h, fill(G_FILL, "G", h + 1, evac_g), nxt=h + 1)

            def evac_s(g, j):
                act.wait_ge(K["quarter_done"], 4 * (tile_no("S", g, j) + 1))
                if j < 2 + XB:
                    nc.scalar.copy(s_raw[:, j, TAPS - 1:], PA[j % 2][:, 0:L]).then_inc(K["projev"], 1)
                else:
                    nc.scalar.copy(z_raw[:, j - 2 - XB, :], PA[j % 2][:, 0:SEQ]).then_inc(K["projev"], 1)

            mixer_g(GDN_HEADS - 1, fill(G_FILL_LAST, "S", 0, evac_s))
            act.wait_ge(K["og_done"], GDN_HEADS)

            def high_y(i, part):
                ks = slice(part * QT, (part + 1) * QT)
                nc.scalar.copy(y_hl[i][0][:, ks, :], (y_gdn, y_ssd)[i][:, ks, :]).then_inc(K["x_hi"], 1)

            def group_s(g, evac, last=False):
                g1 = plus1(act, g)
                w = act.wait_ge
                evac(0)
                w(K["s_tap"], (2 + XB) * TAPS * g1)
                A(xbc[:, :, PAD:TC], cv6[:, :, :], ACT.Silu).then_inc(K["s_silu"], 1)
                w(K["projev"], GDN_HEADS * G_TILES + S_TILES * g1)
                A(z_s[:, :, :], z_raw[:, :, :], ACT.Silu).then_inc(K["s_zsilu"], 1)
                evac(1)
                if not is_first(g):
                    w(K["s_y"], 2 * g)
                w(K["srows_in"], 16 * g1)
                A(EC[:, :, :], s_row[:, :, :], ACT.Exp).then_inc(K["s_ec"], 1)
                w(K["s_ec"], g1)
                if not is_first(g):
                    w(K["s_s2"], g)
                nc.scalar.copy(decay_s, EC[:, :, Q - 1]).then_inc(K["s_dec"], 1)
                w(K["s_gm"], g1)

                def exponents(heads):
                    for r in heads:
                        for c in range(2):
                            A(WE[:, r, c * Q:(c + 1) * Q], WE[:, r, c * Q:(c + 1) * Q], ACT.Exp,
                              bias=col_ngcs[:, 1 + c, ds(R * g + r, 1)]).then_inc(K["s_we"], 1)

                w(K["s_bt"], g1)
                nc.scalar.copy(Btok[:, :, :], m[0][:, 0:2 * Q].rearrange("p (c q) -> p c q", q=Q)) \
                    .then_inc(K["s_btok"], 1)
                exponents(range(0, R // 2))
                evac(2)
                exponents(range(R // 2, R))
                w(K["s_s1"], g1)
                nc.scalar.copy(SS[:, 0, :], m[5][:, :]).then_inc(K["s_s1c"], 1)
                for n in range(3, 6):
                    evac(n)

                def squares(q):
                    if q == S_SQUARES_AT:
                        w(K["s_yz"], g1)
                        A(y_sq[:, :, :], y_g[:, :, :], ACT.Square).then_inc(K["s_ysq"], 1)

                evac(6, squares)
                if last:
                    squares(S_SQUARES_AT)
                    high_y(0, 0)
                    high_y(0, 1)
                w(K["s_ss"], g1)
                A(y_rn, m[5][:, 0:SEQ], ACT.Sqrt, bias=C["eps"], scale=1.0 / (XB * P)).then_inc(K["s_std"], 1)
                evac(7)

            group_s(0, fill(S_FILL, "S", 1, evac_s))
            with act.Fori(1, SSD_GROUPS - 1) as g:
                group_s(g, fill(S_FILL, "S", g + 1, evac_s))
            group_s(SSD_GROUPS - 1, fill(S_FILL_LAST, "M", 0, lambda n, i: None), last=True)
            for part in range(AHEAD, 4):
                cut("M", 0, 2, part)
            high_y(0, 2)
            high_y(0, 3)
            act.wait_ge(K["s_out"], SSD_HEADS // 2)
            for part in range(4):
                high_y(1, part)

            def gate(n, i):
                act.wait_ge(K["quarter_done"], 4 * (tile_no("M", n, i) + 1))
                if not is_first(n):
                    act.wait_ge(K["m_muld"], 2 * n - i)
                A(m_sig[:, i, :], PA[i][:, 0:SEQ], ACT.Sigmoid).then_inc(K["m_sigd"], 1)

            gate(0, 0)
            gate(0, 1)
            cut_tile("M", 0, 3)
            cut_tile("M", 0, 4)
            with act.Fori(1, KT) as n:
                for j in range(ROUND):
                    cut_tile("M", n, j + 1)
                    if j < 2:
                        gate(n, j)
            act.wait_ge(K["quarter_done"], 4 * O_AT)
            act.dma_start(h_in[:, :, :], xT_d[:, :, N_META:L]).then_inc(K["h_moved"], 16)
            with act.Fori(0, O_TILES // ROUND) as n:
                for j in range(ROUND):
                    cut_tile("O", n, j + 1)
                    act.wait_ge(K["h2_done"], ROUND * n + j + 1)
                    A(h2_sq[:, n * ROUND + j, :], h2[:, n * ROUND + j, :], ACT.Square).then_inc(K["norm_sq"], 1)
            act.dma_start(h2_d, h2[:, :, :].rearrange("p k t -> p (k t)")).then_inc(K["h_moved"], 16)
            act.wait_ge(K["norm_ss"], 2)
            A(f_rn, m[0][:, 0:SEQ], ACT.Sqrt, bias=C["eps"], scale=1.0 / D_MODEL).then_inc(K["norm_std"], 1)
            high_parts(nf[0], h2_sq, KT)

            def queries(n):
                for e in range(2):
                    if not is_first(n):
                        act.wait_ge(K["sc_ps"], 2 * n + e - 1)
                    for k in range(2):
                        j = 2 * e + k
                        cut_tile("Q", n, j + 1)
                        act.wait_ge(K["quarter_done"], 4 * (tile_no("Q", n, j) + 1))
                        nc.scalar.copy(qT[:, j, :], (m[2], m[3], m[4], m[5])[j][:, 0:SEQ]).then_inc(K["q_copy"], 1)
                for e in range(2):
                    act.wait_ge(K["sc_ps"], 2 * n + e + 1)
                    nc.scalar.copy(sc_all[:, ds(4 * (2 * n + e), 4), :],
                                   PA[e][:, :].rearrange("p (a b) -> p a b", b=N_KEYS)).then_inc(K["sc_cp"], 1)

            queries(0)
            with act.Fori(1, Q_TILES // ROUND) as n:
                queries(n)

            act.wait_ge(K["h_moved"], 32)

            def down(n, routing=False):
                for j in range(D_ROUND):
                    cut_tile("D", n, j + 1)
                    act.wait_ge(K["quarter_done"], 4 * (tile_no("D", n, j) + 1))
                    A(acts[:, n * D_ROUND + j, :], m[2 + j % 4][:, 0:SEQ], ACT.Gelu).then_inc(K["d_gelu"], 1)
                    if routing and j == 5:
                        for half in range(2):
                            act.wait_ge(K["r_neg"], 2 * n + 2)
                            A(ebest[:, half, :], best[:, half, :], ACT.Exp, bias=soft[:, 0, half:half + 1],
                              accum_out=soft[:, 1, half:half + 1]).then_inc(K["r_exp"], 1)

            with act.Fori(0, PEER_HEADS) as n:
                down(n, routing=True)
            with act.Fori(PEER_HEADS, D_ROUTING) as n:
                down(n)
            act.wait_ge(K["t_cp"], 3)
            with act.Fori(D_ROUTING, N_KEYS // D_ROUND) as n:
                down(n)
            act.wait_ge(K["quarter_done"], 4 * U_AT)

            def distances(n, e):
                for u in range(4):
                    A(oh_j[:, e, u, :], iota, ACT.Abs, bias=tab_hk[:, 1, ds(n * 16 + 4 * e + u, 1)]) \
                        .then_inc(K["dist_done"], 1)

            def one_hots(n, e):
                act.wait_ge(K["dist_done"], 16 * n + 4 * e + 4)
                A(oh_j[:, e, :, :], oh_j[:, e, :, :], ACT.Relu, scale=-1.0, bias=ones[:, 0:1]) \
                    .then_inc(K["ohj_done"], 1)

            distances(0, 0)
            for e in range(3):
                distances(0, e + 1)
                one_hots(0, e)
            with act.Fori(1, SEQ // 16) as n:
                for e in range(4):
                    act.wait_ge(K["oh_ps"], 4 * n + e - 3)
                    distances(n, e)
                    one_hots(n + (e - 1) // 4, (e - 1) % 4)
            one_hots(SEQ // 16 - 1, 3)
            act.wait_ge(K["gated"], SEQ // 4)

            def cut_gates(n, j, first=False):
                if not first:
                    act.wait_ge(K["quarter_done"], 4 * (tile_no("U", n, j) - 1))
                nc.scalar.copy(a_hl[0][:, j % 2, :], acts[:, n * ROUND + j, :]).then_inc(K["a_hi"], 1)

            def up(n, last=False):
                for j in range(ROUND):
                    if not (last and j == ROUND - 1):
                        cut_gates(n, j + 1)
                        cut_tile("U", n, j + 1)

            cut_gates(0, 0, first=True)
            with act.Fori(0, N_KEYS // ROUND - 1) as n:
                up(n)
            up(N_KEYS // ROUND - 1, last=True)
            for part in range(4):
                act.wait_ge(K["h3_done"], 2 * (part + 1))
                ks = slice(part * QT, (part + 1) * QT)
                A(h3_sq[:, ks, :], h3[:, ks, :], ACT.Square).then_inc(K["norm_sq"], 1)
            act.wait_ge(K["norm_ss"], 3)
            A(h3_rn, banks[0][:, 0:SEQ], ACT.Sqrt, bias=C["eps"], scale=1.0 / D_MODEL).then_inc(K["norm_std"], 1)

        @block.vector
        def _(dve):
            def cut(segment, it, j, part):
                q = 4 * tile_no(segment, it, j) + part
                slot = half_slot(segment, j, part // 2)
                dve.wait_ge(K["cut_h"], q + 1)
                V.tensor_tensor(lo[:, part, :], ring[:, slot, (part % 2) * QW:(part % 2 + 1) * QW],
                                hi[:, part, :].bitcast(F32), ALU.subtract).then_inc(K["cut_l"], 1)

            def cut_tile(segment, it, j):
                for part in range(4):
                    cut(segment, it, j, part)

            V.memset(rows[0:64, 5:10, :], 0.0).then_inc(K["zeroed"], 1)
            V.memset(rows[0:64, 10, :], 0.0).then_inc(K["zeroed"], 1)
            V.memset(rows[0:64, 11, :], 1.0).then_inc(K["zeroed"], 1)
            V.memset(g_raw[:, :, 0:TAPS - 1], 0.0).then_inc(K["zeroed"], 1)
            V.memset(s_raw[:, :, 0:TAPS - 1], 0.0).then_inc(K["zeroed"], 1)
            cut_tile("G", 0, -1)
            dve.wait_ge(K["norm_std"], 1)
            V.reciprocal(x_rn, x_rn).then_inc(K["norm_rec"], 1)
            dve.wait_ge(K["norm_rec"], 1)

            def normed_parts(out, lows, x, w, rn, highs, n):
                for part in range(5):
                    if part < 4:
                        for k in range(part * QT, (part + 1) * QT):
                            V.scalar_tensor_tensor(out=out[:, k, :], in0=x[:, k, :], scalar=w[:, k:k + 1], in1=rn,
                                                   op0=ALU.mult, op1=ALU.mult).then_inc(K["normed"], 1)
                    if part:
                        dve.wait_ge(K["x_hi"], n + part)
                        ks = slice((part - 1) * QT, part * QT)
                        V.tensor_tensor(lows[:, ks, :], out[:, ks, :], highs[:, ks, :].bitcast(F32), ALU.subtract) \
                            .then_inc(K["x_lo"], 1)

            normed_parts(xT, n_hl[1], xT, C["w_mix"], x_rn, n_hl[0], 0)
            cut_tile("G", 0, 0)
            sp = K["sp_part"]
            dve.wait_ge(K["quarter_done"], 4)
            V.tensor_scalar(rows[0:64, 0, 0:L], m[1][0:64, 0:L], C["dtb"][0:64, :], None, ALU.add).then_inc(sp, 1)
            cut_tile("G", 0, 1)
            dve.wait_ge(K["sp_act"], 2)
            V.tensor_scalar(rows[0:64, 3, 0:L], rows[0:64, 2, 0:L], 1.0, None, ALU.add).then_inc(sp, 1)
            dve.wait_ge(sp, 2)
            V.tensor_scalar(rows[0:64, 12, 0:L], rows[0:64, 3, 0:L], -1.0, None, ALU.add).then_inc(sp, 1)
            dve.wait_ge(sp, 3)
            V.tensor_tensor(rows[0:64, 13, 0:L], rows[0:64, 2, 0:L], rows[0:64, 12, 0:L], ALU.subtract).then_inc(sp, 1)
            V.reciprocal(rows[0:64, 14, 0:L], rows[0:64, 3, 0:L]).then_inc(sp, 1)
            dve.wait_ge(sp, 5)
            V.tensor_tensor(rows[0:64, 15, 0:L], rows[0:64, 13, 0:L], rows[0:64, 14, 0:L], ALU.mult).then_inc(sp, 1)
            cut_tile("G", 0, 2)
            dve.wait_ge(K["sp_act"], 4)
            dve.wait_ge(sp, 6)
            V.tensor_tensor(rows[0:64, 16, 0:L], rows[0:64, 4, 0:L], rows[0:64, 15, 0:L], ALU.add).then_inc(sp, 1)
            dve.wait_ge(sp, 7)
            dve.wait_ge(K["zeroed"], 5)
            V.scalar_tensor_tensor(out=rows[0:64, 7, PAD:TC], in0=rows[0:64, 0, 0:L], scalar=0.0,
                                   in1=rows[0:64, 16, 0:L], op0=ALU.max, op1=ALU.add).then_inc(sp, 1)
            dve.wait_ge(K["sp_act"], 3)
            V.tensor_scalar(C["alog"][0:64, :], C["alog"][0:64, :], -1.0, None, ALU.mult).then_inc(sp, 1)
            dve.wait_ge(sp, 9)
            V.tensor_scalar(rows[0:64, 10, PAD:TC], rows[0:64, 7, PAD:TC], C["alog"][0:64, :], None, ALU.mult) \
                .then_inc(sp, 1)
            dve.wait_ge(sp, 10)
            for c in range(NC):
                V.tensor_tensor_scan(out=rows[0:64, 5, c * Q:(c + 1) * Q], data0=rows[0:64, 11, c * Q:(c + 1) * Q],
                                     data1=rows[0:64, 10, c * Q:(c + 1) * Q], initial=0.0, op0=ALU.mult,
                                     op1=ALU.add).then_inc(K["csum"], 1)
            cut_tile("G", 0, 3)
            V.memset(qkv[:, :, 0:PAD], 0.0).then_inc(K["zeroed"], 1)
            V.memset(KN[:, 0, :], 0.0).then_inc(K["zeroed"], 1)
            dve.wait_ge(K["zeroed"], 7)

            def conv_tap(tap, raw, n, weights, block_of, acc, out, done, bias=None):
                if tap:
                    dve.wait_ge(K[acc], done + n * tap)
                for b in range(n):
                    wcol = weights[:, ds(block_of(b) * TAPS + tap, 1)]
                    src = raw[:, b, tap:tap + L]
                    if tap == 0:
                        V.tensor_scalar(out[:, b, :], src, wcol, None if bias is None else bias[:, ds(block_of(b), 1)],
                                        ALU.mult, ALU.bypass if bias is None else ALU.add).then_inc(K[acc], 1)
                    else:
                        V.scalar_tensor_tensor(out=out[:, b, :], in0=src, scalar=wcol, in1=out[:, b, :],
                                               op0=ALU.mult, op1=ALU.add).then_inc(K[acc], 1)

            def three(bank, n=NC):
                return bank[:, 0:n * Q].rearrange("p (c q) -> p c q", q=Q)

            def fill(fill_plan, segment, it):
                return lambda n, then=None: cuts(cut, segment, it, fill_plan, n, then)

            kn_tokens = KN[:, :, :].rearrange("p c q -> p (c q)")[:, PAD:TC]

            def by_chunk(ap):
                return ap.rearrange("p (c q) -> p c q", q=Q)

            def conv_g(h, tap):
                if tap == 0:
                    dve.wait_ge(K["projev"], h * G_TILES + 3)
                conv_tap(tap, g_raw, 3, C["g_conv"], lambda b: b * GDN_HEADS + h, "conv_tap", cv, 3 * TAPS * h)

            def normed_qk(h):
                dve.wait_ge(K["qk_std"], 2 * (h + 1))
                V.reciprocal(qk_rn[:, 1, :], qk_n[:, 1, :]).then_inc(K["qk_rec"], 1)
                dve.wait_ge(K["qk_rec"], 2 * h + 1)
                V.tensor_tensor(kn_tokens, qkv[:, 1, PAD:TC], qk_rn[:, 1, :], ALU.mult).then_inc(K["kn_done"], 1)
                V.reciprocal(qk_rn[:, 0, N_META:L], qk_n[:, 0, N_META:L]).then_inc(K["qk_rec"], 1)
                dve.wait_ge(K["qk_rec"], 2 * h + 2)
                if not is_first(h):
                    dve.wait_ge(K["qg_done"], h)
                V.scalar_tensor_tensor(out=QN[:, :, :], in0=by_chunk(qkv[:, 0, Q:TC]), scalar=DK ** -0.5,
                                       in1=by_chunk(qk_rn[:, 0, N_META:L]), op0=ALU.mult, op1=ALU.mult) \
                    .then_inc(K["qn_done"], 1)

            def conv_s(g, tap):
                if tap == 0:
                    dve.wait_ge(K["projev"], GDN_HEADS * G_TILES + g * S_TILES + 2 + XB)
                conv_tap(tap, s_raw, 2 + XB, C["s_conv"],
                         lambda b: (XB * SSD_GROUPS + SSD_GROUPS * b + g) if b < 2 else (XB * g + b - 2),
                         "s_tap", cv6, (2 + XB) * TAPS * g, bias=C["s_convb"])

            for tap in range(TAPS):
                if tap < AHEAD:
                    cut("G", 0, 4, tap)
                conv_g(0, tap)
            for n, dst in enumerate((col_gcs, col_te, col_dt, col_eg)):
                dve.wait_ge(K["colps"], n + 1)
                V.tensor_copy(dst[:, :, :], m[4 + n % 2][:, 0:NC * 64].rearrange("p (c h) -> p c h", h=64)) \
                    .then_inc(K["colcp"], 1)
            dve.wait_ge(K["colps"], 5)
            V.tensor_copy(col_beta[:, :, :], m[4][:, 0:NC * 64].rearrange("p (c h) -> p c h", h=64)[:, :, 0:16]) \
                .then_inc(K["colcp"], 1)
            dve.wait_ge(K["colcp"], 5)
            V.tensor_scalar(col_ngcs[:, :, :], col_gcs[:, :, :], -1.0, None, ALU.mult).then_inc(K["colder"], 1)
            V.tensor_scalar(col_nbeta[:, :, :], col_beta[:, :, :], -1.0, None, ALU.mult).then_inc(K["colder"], 1)
            dve.wait_ge(K["colder"], 2)
            V.tensor_tensor(col_nbeg[:, :, :], col_nbeta[:, :, :], col_eg[:, :, 32:48], ALU.mult).then_inc(K["colder"], 1)
            dve.wait_ge(K["gcs_out"], 16)
            for chunks in (X, B2, B2T, B4, B4T, B8T, T, TT):
                V.memset(chunks[:, 0, 0:PAD], 0.0).then_inc(K["zeroed"], 1)
            dve.wait_ge(K["zeroed"], 15)
            dve.wait_ge(K["colder"], 3)
            normed_qk(0)

            def gated_o(h):
                h1 = plus1(dve, h)
                w = dve.wait_ge
                w(K["onstd_done"], h1)
                V.reciprocal(o_rn, o_n).then_inc(K["onrec_done"], 1)
                w(K["gsilu"], h1)
                w(K["onrec_done"], 2 * h + 1)
                V.scalar_tensor_tensor(out=o_rn, in0=o_rn, scalar=C["g_nw"], in1=gate_s, op0=ALU.mult,
                                       op1=ALU.mult).then_inc(K["onrec_done"], 1)
                w(K["onrec_done"], 2 * h + 2)
                V.tensor_tensor(y_gdn[:, h, :], m[1][:, 0:SEQ], o_rn, ALU.mult).then_inc(K["og_done"], 1)

            def mixer_g(h, cut_ahead, nxt=None):
                h1 = plus1(dve, h)
                w = dve.wait_ge

                def fill(n):
                    cut_ahead(n)
                    for tap in range(TAPS):
                        if nxt is not None and G_TAPS_AT[tap] == n:
                            conv_g(nxt, tap)
                        if nxt is None and S_TAPS_FIRST[tap] == n:
                            conv_s(0, tap)

                fill(0)
                w(K["vt_done"], h1)
                V.tensor_tensor(VB[:, :, :], three(m[2]), bc(col_beta[:, :, ds(h, 1)], [P, NC, Q]), ALU.mult) \
                    .then_inc(K["vb_done"], 1)
                fill(1)
                w(K["e_done"], 3 * h1)
                w(K["kk_done"], h1)
                for c in range(NC):
                    V.scalar_tensor_tensor(out=X[:, c, own(c)], in0=m[4][:, bank_own(c)],
                                           scalar=col_nbeta[:, c, ds(h, 1)], in1=E[:, c, own(c)], op0=ALU.mult,
                                           op1=ALU.mult).then_inc(K["x_done"], 1)
                w(K["x_done"], 3 * h1)
                V.tensor_tensor(B[:, :, :], X[:, :, :], bc(C["same16"].unsqueeze(1), [P, NC, Q]), ALU.mult) \
                    .then_inc(K["b_done"], 1)
                w(K["qk_done"], h1)
                w(K["et_done"], 2 * h1)
                V.tensor_tensor(AT[:, :, :], three(m[5], 2), ET[:, :, :], ALU.mult).then_inc(K["at_done"], 1)
                w(K["kt_done"], h1)
                V.tensor_tensor(KD[:, :, :], three(m[3], 2), bc(col_te[:, 0:2, ds(32 + h, 1)], [P, 2, Q]), ALU.mult) \
                    .then_inc(K["kd_done"], 1)
                fill(2)
                w(K["xt_done"], h1)
                V.tensor_tensor(BT[:, :, :], three(m[0]), bc(C["same16"].unsqueeze(1), [P, NC, Q]), ALU.mult) \
                    .then_inc(K["bt_done"], 1)
                w(K["b_done"], h1)
                V.tensor_tensor(PP[:, :, :], B[:, :, :], bc(ident.unsqueeze(1), [P, NC, Q]), ALU.add) \
                    .then_inc(K["p1_done"], 1)
                for n in range(3):
                    V.tensor_tensor(LT[:, n, :, :], m[0][:, Q:TC].rearrange("p (c q) -> p c q", q=Q),
                                    bc(level[:, n:n + 1, :], [P, 2, Q]), ALU.mult).then_inc(K["lt_done"], 1)
                fill(3)
                fill(4)
                w(K["b4_done"], h1)
                w(K["p1_done"], h1)
                V.tensor_tensor(tokens_of(PP), m[4][:, PAD:TC], tokens_of(PP), ALU.add).then_inc(K["p2_done"], 1)
                fill(5)
                w(K["b8_done"], h1)
                w(K["p2_done"], h1)
                V.tensor_tensor(tokens_of(PP), m[2][:, PAD:TC], tokens_of(PP), ALU.add).then_inc(K["p3_done"], 1)
                fill(6)
                w(K["pb8_done"], h1)
                w(K["p3_done"], h1)
                V.tensor_tensor(tokens_of(T), m[0][:, PAD:TC], tokens_of(PP), ALU.add).then_inc(K["t0_done"], 1)
                fill(7)
                fill(8)
                w(K["vn0_done"], h1)
                V.tensor_copy(VN, m[4][:, 0:Q]).then_inc(K["vn0s_done"], 1)

                def grow(bank, n):
                    w(K["tn_done"], 3 * h + n)
                    V.tensor_tensor(T[:, 1:3, :], bank[:, 0:2 * Q].rearrange("p (c q) -> p c q", q=Q), T[:, 1:3, :],
                                    ALU.add).then_inc(K["tu_done"], 1)
                    V.tensor_tensor(TT[:, 1:3, :], bank[:, 2 * Q:4 * Q].rearrange("p (c q) -> p c q", q=Q),
                                    TT[:, 1:3, :], ALU.add).then_inc(K["tu_done"], 1)

                w(K["t0_done"], h1)
                w(K["t0ts_done"], h1)
                fill(9)
                grow(m[2], 1)
                fill(10)
                w(K["ks_done"], 2 * h + 1)
                V.scalar_tensor_tensor(out=RR, in0=m[4][:, 0:Q], scalar=col_nbeg[:, 1, ds(h, 1)], in1=VB[:, 1, :],
                                       op0=ALU.mult, op1=ALU.add).then_inc(K["r_done"], 1)
                fill(11)
                grow(m[3], 2)
                fill(12)
                fill(13)
                w(K["tn_done"], 3 * h + 3)
                V.tensor_tensor(TT[:, 1:3, :], m[2][:, 0:2 * Q].rearrange("p (c q) -> p c q", q=Q), TT[:, 1:3, :],
                                ALU.add).then_inc(K["tu_done"], 1)
                fill(14)
                w(K["vn_done"], 2 * h + 1)
                V.tensor_copy(VN, m[5][:, 0:Q]).then_inc(K["vns_done"], 1)
                fill(15)
                w(K["su_done"], h1)
                w(K["eg_done"], h1)
                w(K["o_done"], 2 * h + 1)
                V.scalar_tensor_tensor(out=S, in0=S, scalar=EG[:, 0, Q - 1:Q], in1=m[0][:, 0:Q], op0=ALU.mult,
                                       op1=ALU.add).then_inc(K["s2_done"], 1)
                fill(16)
                w(K["ks_done"], 2 * h + 2)
                V.scalar_tensor_tensor(out=RR, in0=m[4][:, 0:Q], scalar=col_nbeg[:, 2, ds(h, 1)], in1=VB[:, 2, :],
                                       op0=ALU.mult, op1=ALU.add).then_inc(K["r_done"], 1)
                fill(17)
                w(K["vn_done"], 2 * h + 2)
                V.tensor_copy(VN, m[5][:, 0:Q]).then_inc(K["vns_done"], 1)
                fill(18)
                fill(19)
                if nxt is not None:
                    normed_qk(nxt)
                gated_o(h)
                fill(20)

            mixer_g(0, fill(G_FILL, "G", 1), nxt=1)
            with dve.Fori(1, GDN_HEADS - 1) as h:
                mixer_g(h, fill(G_FILL, "G", h + 1), nxt=h + 1)
            mixer_g(GDN_HEADS - 1, fill(G_FILL_LAST, "S", 0))
            V.memset(xbc[:, :, 0:PAD], 0.0).then_inc(K["s_zero"], 1)
            dve.wait_ge(K["s_zero"], 1)

            def low_y(i, part):
                dve.wait_ge(K["x_hi"], 4 + 4 * i + part + 1)
                ks = slice(part * QT, (part + 1) * QT)
                V.tensor_tensor(y_hl[i][1][:, ks, :], (y_gdn, y_ssd)[i][:, ks, :],
                                y_hl[i][0][:, ks, :].bitcast(F32), ALU.subtract).then_inc(K["x_lo"], 1)

            def group_s(g, cut_ahead, nxt=None):
                last = nxt is None
                g1 = plus1(dve, g)
                w = dve.wait_ge

                def between(q):
                    for tap in range(TAPS):
                        if not last and S_TAPS_AT[tap] == q:
                            conv_s(nxt, tap)
                    if q == S_OUT_AT:
                        w(K["s_y"], 2 * g1)
                        for b in range(XB):
                            V.scalar_tensor_tensor(out=y_g[:, b, :], in0=xbc[:, 2 + b, Q:TC],
                                                   scalar=C["s_D"][:, ds(XB * g + b, 1)], in1=m[1 + b][:, 0:SEQ],
                                                   op0=ALU.mult, op1=ALU.add).then_inc(K["s_yd"], 1)
                        w(K["s_yd"], XB * g1)
                        w(K["s_zsilu"], g1)
                        V.tensor_tensor(y_g[:, :, :], y_g[:, :, :], z_s[:, :, :], ALU.mult).then_inc(K["s_yz"], 1)

                def fill(n):
                    cut_ahead(n, between)

                fill(0)
                fill(1)
                for c in range(NC):
                    w(K["s_xt"], NC * g + c + 1)
                    V.tensor_tensor(XC[:, c, :].rearrange("p (r d) -> p r d", d=SSD_HD),
                                    m[1 + c][:, :].rearrange("p (r d) -> p r d", d=SSD_HD),
                                    bc(col_dt[:, c, ds(R * g, R)].unsqueeze(2), [P, R, SSD_HD]), ALU.mult) \
                        .then_inc(K["s_xc"], 1)
                fill(2)
                w(K["s_we"], 2 * R * g1)
                w(K["s_cbt"], g1)
                for c in range(2):
                    tok = slice(c * Q, (c + 1) * Q)
                    V.tensor_tensor(WE[:, :, tok], WE[:, :, tok], bc(m[4][:, tok].unsqueeze(1), [P, R, Q]),
                                    ALU.mult).then_inc(K["s_w"], 1)
                fill(3)
                fill(4)
                w(K["s_dec"], g1)
                w(K["s_s1c"], g1)
                V.tensor_tensor(SS[:, 1, :].rearrange("p (r d) -> p r d", d=SSD_HD),
                                SS[:, 0, :].rearrange("p (r d) -> p r d", d=SSD_HD),
                                bc(decay_s.unsqueeze(2), [P, R, SSD_HD]), ALU.mult).then_inc(K["s_s2a"], 1)
                w(K["s_s2a"], g1)
                w(K["s_su"], g1)
                V.tensor_tensor(SS[:, 1, :], m[0][:, :], SS[:, 1, :], ALU.add).then_inc(K["s_s2"], 1)
                fill(5)
                fill(6)
                if last:
                    between(S_OUT_AT)
                fill(7)
                if last:
                    low_y(0, 0)
                    low_y(0, 1)
                w(K["s_std"], g1)
                V.reciprocal(y_rn, y_rn).then_inc(K["s_rec"], 1)
                w(K["s_rec"], g1)
                for b in range(XB):
                    V.scalar_tensor_tensor(out=y_ssd[:, XB * g + b, :], in0=y_g[:, b, :],
                                           scalar=C["s_nw"][:, ds(XB * g + b, 1)], in1=y_rn, op0=ALU.mult,
                                           op1=ALU.mult).then_inc(K["s_out"], 1)

            group_s(0, fill(S_FILL, "S", 1), nxt=1)
            with dve.Fori(1, SSD_GROUPS - 1) as g:
                group_s(g, fill(S_FILL, "S", g + 1), nxt=g + 1)
            group_s(SSD_GROUPS - 1, fill(S_FILL_LAST, "M", 0))
            for part in range(AHEAD, 4):
                cut("M", 0, 2, part)
            low_y(0, 2)
            low_y(0, 3)
            for part in range(4):
                low_y(1, part)

            def merge(n):
                n1 = plus1(dve, n)
                if not is_first(n):
                    cut_tile("M", n, 1)
                    cut_tile("M", n, 2)
                    dve.wait_ge(K["m_out"], 2 * n)
                for i in range(2):
                    cut_tile("M", n, 3 + i)
                    dve.wait_ge(K["m_sigd"], 2 * n1)
                    dve.wait_ge(K["quarter_done"], 4 * (tile_no("M", n, 2 + i) + 1))
                    V.tensor_tensor(m_mul[:, i, :], m[i][:, 0:SEQ], m_sig[:, 1 - i, :], ALU.mult) \
                        .then_inc(K["m_muld"], 1)
                dve.wait_ge(K["m_muld"], 2 * n1)
                V.tensor_tensor(m_mul[:, 2, :], m_mul[:, 0, :], m_mul[:, 1, :], ALU.add).then_inc(K["m_out"], 1)
                dve.wait_ge(K["m_out"], 2 * n + 1)
                V.tensor_copy(m_hl[0][:, n, :], m_mul[:, 2, :]).then_inc(K["m_out"], 1)
                dve.wait_ge(K["m_out"], 2 * n1)
                V.tensor_tensor(m_hl[1][:, n, :], m_mul[:, 2, :], m_hl[0][:, n, :].bitcast(F32), ALU.subtract) \
                    .then_inc(K["m_lo"], 1)

            merge(0)
            with dve.Fori(1, KT) as n:
                merge(n)
            o_banks = (m[2], m[3], m[4], m[5])
            with dve.Fori(0, O_TILES // ROUND) as n:
                for j in range(ROUND):
                    cut_tile("O", n, j + 1)
                    dve.wait_ge(K["h_moved"], 16)
                    dve.wait_ge(K["quarter_done"], 4 * (tile_no("O", n, j) + 1))
                    V.tensor_tensor(h2[:, n * ROUND + j, :], h2[:, n * ROUND + j, :], o_banks[j][:, 0:SEQ], ALU.add) \
                        .then_inc(K["h2_done"], 1)
            dve.wait_ge(K["norm_std"], 2)
            V.reciprocal(f_rn, f_rn).then_inc(K["norm_rec"], 1)
            dve.wait_ge(K["norm_rec"], 2)
            normed_parts(h2_sq, nf[1], h2, C["w_ffn"], f_rn, nf[0], 12)

            with dve.Fori(0, Q_TILES // ROUND) as n:
                for j in range(ROUND):
                    cut_tile("Q", n, j + 1)

            def wait(key, value):
                dve.wait_ge(K[key], value)
                V.memset(soft[:, 2, :], 0.0)

            def first8(values, spare, out_s, key):
                for r in range(len(values)):
                    V.max(out_s[:, r, 0:8], values[r]).then_inc(K[key[0]], 1)
                wait(key[0], key[1] + len(values))
                for r in range(len(values)):
                    V.match_replace(out=spare[r], in_to_replace=out_s[:, r, 0:8], in_values=values[r],
                                    imm_value=-3.0e38).then_inc(K[key[0]], 1)

            def where8(values, at, out_s, out_i, key):
                for r in range(len(values)):
                    V.max_index(out_i[:, r, at:at + 8], out_s[:, r, at:at + 8], values[r]).then_inc(K[key], 1)

            def next8(spare, out_s, key):
                wait(key[0], key[1] + 2 * len(spare))
                for r in range(len(spare)):
                    V.max(out_s[:, r, 8:16], spare[r]).then_inc(K[key[0]], 1)

            keys = [sc[:, a, :] for a in range(4)]
            keys2 = [sc2[:, a, :] for a in range(4)]
            cands = [cand[:, a, :, :].rearrange("p a b -> p (a b)") for a in range(2)]
            cands2 = [cand2[:, a, :] for a in range(2)]

            def key_scores(hd):
                dve.wait_ge(K["sc_cp"], PEER_HEADS)
                V.tensor_copy(sc[:, :, :], sc_all[:, ds(4 * hd, 4), :]).then_inc(K["r_in"], 1)
                wait("r_in", hd + 1)
                first8(keys, keys2, top_s, ("r_top", 12 * hd))

            def key_places(hd):
                where8(keys, 0, top_s, top_u, "r_idx")
                next8(keys2, top_s, ("r_top", 12 * hd))

            def pair_sums(hd):
                wait("r_top", 12 * hd + 12)
                where8(keys2, 8, top_s, top_u, "r_idx")
                dve.wait_ge(K["r_idx"], 8 * (hd + 1))
                V.tensor_copy(top_i[:, :, :], top_u).then_inc(K["r_cast"], 1)
                for half in range(2):
                    V.tensor_tensor(cand[:, half, :, :], bc(top_s[:, half, :].unsqueeze(2), [P, TOPK, TOPK]),
                                    bc(top_s[:, 2 + half, :].unsqueeze(1), [P, TOPK, TOPK]), ALU.add) \
                        .then_inc(K["r_cand"], 1)

            def pair_scores(hd):
                wait("r_cand", 2 * (hd + 1))
                first8(cands, cands2, best, ("r_best", 6 * hd))

            def pair_places(hd):
                where8(cands, 0, best, pos_u, "r_pos")
                next8(cands2, best, ("r_best", 6 * hd))
                wait("r_best", 6 * hd + 6)
                where8(cands2, 8, best, pos_u, "r_pos")
                for half in range(2):
                    V.tensor_scalar(soft[:, 0, half:half + 1], best[:, half, 0:1], -1.0, None, ALU.mult) \
                        .then_inc(K["r_neg"], 1)

            def ranks(hd):
                dve.wait_ge(K["r_pos"], 4 * (hd + 1))
                V.tensor_scalar(pos_hi, pos_u, 4, None, ALU.logical_shift_right).then_inc(K["r_bits"], 1)
                V.tensor_scalar(pos_lo, pos_u, 15, None, ALU.bitwise_and).then_inc(K["r_bits"], 1)
                dve.wait_ge(K["r_bits"], 4 * hd + 2)
                V.tensor_copy(pos_f[:, 0, :, :], pos_hi).then_inc(K["r_bits"], 1)
                V.tensor_copy(pos_f[:, 1, :, :], pos_lo).then_inc(K["r_bits"], 1)
                dve.wait_ge(K["r_bits"], 4 * hd + 4)
                dve.wait_ge(K["r_cast"], hd + 1)
                for f in range(2):
                    V.tensor_tensor(pick[:, f, :, :],
                                    bc(pos_f[:, f, :, :].rearrange("p a b -> p (a b)").unsqueeze(2), [P, 2 * TOPK, TOPK]),
                                    bc(C["rank"].unsqueeze(1), [P, 2 * TOPK, TOPK]), ALU.is_equal) \
                        .then_inc(K["r_mul"], 1)

            def key_picks(hd):
                dve.wait_ge(K["r_mul"], 6 * hd + 2)
                for f in range(2):
                    for half in range(2):
                        V.tensor_tensor(pick[:, f, half * TOPK:(half + 1) * TOPK, :],
                                        pick[:, f, half * TOPK:(half + 1) * TOPK, :],
                                        bc(top_i[:, 2 * f + half, :].unsqueeze(1), [P, TOPK, TOPK]), ALU.mult) \
                            .then_inc(K["r_mul"], 1)

            def tables(hd):
                dve.wait_ge(K["r_mul"], 6 * (hd + 1))
                for f in range(2):
                    for half in range(2):
                        V.tensor_reduce(tab_t[:, f, half, ds(hd * TOPK, TOPK)],
                                        pick[:, f, half * TOPK:(half + 1) * TOPK, :], AX.X, ALU.add) \
                            .then_inc(K["r_pick"], 1)
                dve.wait_ge(K["r_exp"], 2 * (hd + 1))
                V.reciprocal(soft[:, 2, :], soft[:, 1, :]).then_inc(K["r_neg2"], 1)
                dve.wait_ge(K["r_neg2"], hd + 1)
                for half in range(2):
                    V.tensor_scalar(tab_t[:, 2, half, ds(hd * TOPK, TOPK)], ebest[:, half, :],
                                    soft[:, 2, half:half + 1], None, ALU.mult).then_inc(K["r_gate"], 1)

            steps = (key_scores, key_places, pair_sums, pair_scores, pair_places, ranks, key_picks, tables)
            with dve.Fori(0, PEER_HEADS) as n:
                for j in range(D_ROUND):
                    cut_tile("D", n, j + 1)
                    steps[j](n)

            def down(n):
                for j in range(D_ROUND):
                    cut_tile("D", n, j + 1)

            down(PEER_HEADS)
            dve.wait_ge(K["t_ps"], 1)
            V.tensor_copy(tab_hk[:, 0, :], m[0][:, 0:SEQ]).then_inc(K["t_cp"], 1)
            V.tensor_scalar(tab_hk[:, 1, :], m[0][:, SEQ:2 * SEQ], -1.0, None, ALU.mult).then_inc(K["t_cp"], 1)
            V.tensor_copy(tab_hk[:, 2, :], m[1][:, 0:SEQ]).then_inc(K["t_cp"], 1)
            with dve.Fori(PEER_HEADS + 1, N_KEYS // D_ROUND) as n:
                down(n)
            dve.wait_ge(K["t_cp"], 3)
            dve.wait_ge(K["quarter_done"], 4 * U_AT)

            def one_hots(n, e):
                for u in range(4):
                    t = n * 16 + 4 * e + u
                    V.tensor_scalar(oh_i[:, e, u, :], iota, tab_hk[:, 0, ds(t, 1)], tab_hk[:, 2, ds(t, 1)],
                                    ALU.is_equal, ALU.mult).then_inc(K["ohi_done"], 1)

            def gate(n, e):
                dve.wait_ge(K["oh_ps"], 4 * n + e + 1)
                a = acts[:, :, ds(16 * n + 4 * e, 4)].rearrange("p i u -> p u i")
                V.tensor_tensor(a, m[2 + e][:, :].rearrange("p (u i) -> p u i", i=P), a, ALU.mult) \
                    .then_inc(K["gated"], 1)

            one_hots(0, 0)
            with dve.Fori(0, SEQ // 16 - 1) as n:
                for e in range(4):
                    one_hots(n + (e + 1) // 4, (e + 1) % 4)
                    gate(n, e)
            for e in range(3):
                one_hots(SEQ // 16 - 1, e + 1)
                gate(SEQ // 16 - 1, e)
            gate(SEQ // 16 - 1, 3)
            dve.wait_ge(K["gated"], SEQ // 4)

            def cut_gates(n, j):
                i = n * ROUND + j
                dve.wait_ge(K["a_hi"], i + 1)
                V.tensor_tensor(a_hl[1][:, j % 2, :], acts[:, i, :], a_hl[0][:, j % 2, :].bitcast(F32), ALU.subtract) \
                    .then_inc(K["a_lo"], 1)

            def up(n, last=False):
                for j in range(ROUND):
                    if not (last and j == ROUND - 1):
                        cut_gates(n, j + 1)
                        cut_tile("U", n, j + 1)

            cut_gates(0, 0)
            with dve.Fori(0, N_KEYS // ROUND - 1) as n:
                up(n)
            up(N_KEYS // ROUND - 1, last=True)
            dve.wait_ge(K["h_moved"], 48)
            for b in range(KT // 2):
                dve.wait_ge(K["quarter_done"], 4 * (END - 1) + b // 2 + 1)
                V.tensor_tensor(h3[:, 2 * b:2 * b + 2, :], banks[b][:, :].rearrange("p (a t) -> p a t", t=SEQ),
                                h2b[:, 2 * b:2 * b + 2, :], ALU.add).then_inc(K["h3_done"], 1)
            dve.wait_ge(K["norm_std"], 3)
            V.reciprocal(h3_rn, h3_rn).then_inc(K["norm_rec"], 1)
            dve.wait_ge(K["norm_rec"], 3)
            for k in range(KT):
                V.scalar_tensor_tensor(out=h3[:, k, :], in0=h3[:, k, :], scalar=C["w_fin"][:, k:k + 1], in1=h3_rn,
                                       op0=ALU.mult, op1=ALU.mult).then_inc(K["out_done"], 1)

        @block.gpsimd
        def _(pool):
            def load_g(h):
                pool.dma_start(g_row[:, :, :], gcs_d[ds(32 + h, 1), :].rearrange("o (c q) -> (o c) q", q=Q)
                               .partition_broadcast(P)).then_inc(K["rows_in"], 16)

            def load_s(g):
                pool.dma_start(s_row[:, :, :], bc(gcs_d[ds(R * g, R), Q:TC].unsqueeze(0), [P, R, 2 * Q])) \
                    .then_inc(K["srows_in"], 16)

            pool.wait_ge(K["gcs_out"], 16)
            load_g(0)
            load_s(0)
            pool.wait_ge(K["colder"], 3)

            def mixer_g(h, last=False):
                h1 = plus1(pool, h)
                pool.wait_ge(K["rows_in"], 16 * h1)
                if not is_first(h):
                    pool.wait_ge(K["eg_done"], h)
                G.tensor_tensor(GE[:, :, :], bc(C["below"].unsqueeze(1), [P, NC, Q]), g_row[:, :, :], ALU.subtract) \
                    .then_inc(K["gm_done"], 1)
                G.tensor_tensor(GT[:, :, :], g_row[:, 1:3, :], C["upto"].rearrange("p (c q) -> p c q", q=Q), ALU.add) \
                    .then_inc(K["gm_done"], 1)
                pool.wait_ge(K["gm_done"], 2 * h1)
                pool.wait_ge(K["eg_done"], h1)
                if not last:
                    load_g(h + 1)
                pool.wait_ge(K["qn_done"], h1)
                G.tensor_tensor(QG[:, :, :], QN[:, :, :], EG[:, :, :], ALU.mult).then_inc(K["qg_done"], 1)

            mixer_g(0)
            with pool.Fori(1, GDN_HEADS - 1) as h:
                mixer_g(h)
            mixer_g(GDN_HEADS - 1, last=True)
            pool.wait_ge(K["og_done"], GDN_HEADS)

            def group_s(g, last=False):
                g1 = plus1(pool, g)
                pool.wait_ge(K["srows_in"], 16 * g1)
                if not is_first(g):
                    pool.wait_ge(K["s_y"], 2 * g)
                G.tensor_tensor(WE[:, :, :], s_row[:, :, :], bc(C["upto"].unsqueeze(1), [P, R, 2 * Q]),
                                ALU.add).then_inc(K["s_gm"], 1)
                pool.wait_ge(K["s_gm"], g1)
                pool.wait_ge(K["s_dec"], g1)
                if not last:
                    load_s(g + 1)
                pool.wait_ge(K["s_silu"], g1)
                G.tensor_tensor(EC[:, :, :], EC[:, :, :], bc(xbc[:, 1:2, Q:TC], [P, R, 2 * Q]), ALU.mult) \
                    .then_inc(K["s_cg"], 1)
                for c in range(2):
                    pool.wait_ge(K["s_xc"], NC * g + c + 1)
                    G.tensor_tensor(XE[:, c, :].rearrange("p (r d) -> p r d", d=SSD_HD),
                                    XC[:, c, :].rearrange("p (r d) -> p r d", d=SSD_HD),
                                    bc(col_te[:, c, ds(R * g, R)].unsqueeze(2), [P, R, SSD_HD]), ALU.mult) \
                        .then_inc(K["s_xe"], 1)

            group_s(0)
            with pool.Fori(1, SSD_GROUPS - 1) as g:
                group_s(g)
            group_s(SSD_GROUPS - 1, last=True)


def layout(x, meta_tokens, norm_mix_w, w_in, ssd_conv_w, ssd_conv_b, ssd_dt_bias, ssd_A_log, ssd_D,
           ssd_norm_w, gdn_conv_w, gdn_dt_bias, gdn_A_log, gdn_norm_w, w_branch_ssd, w_branch_gdn,
           w_out, norm_ffn_w, peer_w_query, peer_sub_keys, peer_expert_down, peer_expert_up, final_norm_w):
    import numpy as np

    f = np.float32
    h = np.concatenate([np.asarray(meta_tokens), np.asarray(x)[0]], 0)
    xT = np.ascontiguousarray(h.T.reshape(KT, P, L).transpose(1, 0, 2))

    w = np.asarray(w_in)[0]
    d_inner, conv = SSD_HEADS * SSD_HD, SSD_HEADS * SSD_HD + 2 * SSD_GROUPS * SSD_STATE
    z0, x0 = 0, d_inner
    b0 = x0 + d_inner
    c0 = b0 + SSD_GROUPS * SSD_STATE
    dt0 = x0 + conv
    q0 = dt0 + SSD_HEADS
    k0, v0 = q0 + GDN_HEADS * DK, q0 + 2 * GDN_HEADS * DK
    gate0 = v0 + GDN_HEADS * DK
    a0 = gate0 + GDN_HEADS * DK
    bb0 = a0 + GDN_HEADS
    m0 = bb0 + GDN_HEADS
    stream = np.zeros((N_TILES, P, KT * P), f)

    def put(n, mat, col, width=P, at=0):
        stream[n].reshape(P, KT, P)[:, :, at:at + width] = \
            mat[:, col:col + width].reshape(KT, P, width).transpose(1, 0, 2)

    put(0, w, dt0, SSD_HEADS, 0)
    put(0, w, a0, GDN_HEADS, 32)
    put(0, w, bb0, GDN_HEADS, 64)
    for i in range(GDN_HEADS):
        for j, c in enumerate((q0, k0, v0, gate0)):
            put(G_AT + G_TILES * i + j, w, c + i * P)
    for g in range(SSD_GROUPS):
        put(S_AT + S_TILES * g, w, b0 + g * P)
        put(S_AT + S_TILES * g + 1, w, c0 + g * P)
        for b in range(XB):
            put(S_AT + S_TILES * g + 2 + b, w, x0 + (g * XB + b) * P)
            put(S_AT + S_TILES * g + 2 + XB + b, w, z0 + (g * XB + b) * P)
    ws, wg, wo, wq = (np.asarray(a)[0] for a in (w_branch_ssd, w_branch_gdn, w_out, peer_w_query))
    for n in range(KT):
        put(M_AT + M_TILES * n, w, m0 + n * P)
        put(M_AT + M_TILES * n + 1, w, m0 + D_MODEL + n * P)
        put(M_AT + M_TILES * n + 2, wg, n * P)
        put(M_AT + M_TILES * n + 3, ws, n * P)
        put(O_AT + n, wo, n * P)
        put(Q_AT + n, wq, n * P)

    down = np.asarray(peer_expert_down)[0].reshape(N_KEYS, P, KT, P)
    down = np.ascontiguousarray(down.transpose(0, 3, 2, 1)).reshape(N_KEYS, P, KT * P)
    up = np.ascontiguousarray(np.asarray(peer_expert_up)[0].reshape(N_KEYS, P, D_MODEL))

    c = np.zeros((P, N_CONST), f)

    def const(name, a):
        at, n = CONST[name]
        a = np.asarray(a).reshape(-1, n)
        c[0:len(a), at:at + n] = a

    i = np.arange(P)
    const("ident", i[:, None] == i)
    const("ones", np.ones((P, P)))
    const("same16", (i[:, None] // 16) == (i // 16))
    const("level", np.concatenate([((i[:, None] // (2 * s)) == (i // (2 * s))) & ((i[:, None] // s) != (i // s))
                                   for s in (16, 32, 64)], 1))
    const("below", np.where(i[:, None] > i, 0.0, NEG))
    const("upto", np.tile(np.where(i[:, None] <= i, 0.0, NEG), (1, 2)))
    const("iota", np.tile(i, (P, 1)))
    const("rank", np.tile(np.arange(TOPK), (P, 1)))

    def blocks(a):
        t = a.shape[0]
        return a.reshape(t, -1, P).transpose(2, 1, 0).reshape(P, -1)

    const("g_conv", blocks(np.asarray(gdn_conv_w)[0]))
    const("s_conv", blocks(np.asarray(ssd_conv_w)[0]))
    const("s_convb", blocks(np.asarray(ssd_conv_b)))
    const("s_D", blocks(np.repeat(np.asarray(ssd_D)[0], SSD_HD)[None]))
    const("s_nw", blocks(np.asarray(ssd_norm_w)))
    const("g_nw", np.asarray(gdn_norm_w)[0])
    const("w_mix", blocks(np.asarray(norm_mix_w)))
    const("w_ffn", blocks(np.asarray(norm_ffn_w)))
    const("w_fin", blocks(np.asarray(final_norm_w)[None]))
    const("dtb", np.concatenate([np.asarray(ssd_dt_bias)[0], np.asarray(gdn_dt_bias)[0]]))
    const("alog", np.concatenate([np.asarray(ssd_A_log)[0], np.asarray(gdn_A_log)[0]]))
    const("eps", np.full((P, 1), EPS))
    const("keysT", np.asarray(peer_sub_keys)[0].transpose(2, 0, 1).reshape(P, -1))
    return xT, stream, down, up, c


def kernel(**inputs):
    import numpy as np
    import concourse.bacc as bacc
    from concourse.bass_utils import run_bass_kernel_spmd as run

    nc = bacc.Bacc("TRN2", target_bir_lowering=False, num_devices=1)
    names = ("xT", "w_stream", "down", "up", "const")
    arrays = dict(zip(names, layout(**inputs)))
    args = [nc.dram_tensor(n, arrays[n].shape, F32, kind="ExternalInput").ap() for n in names]
    out = nc.dram_tensor("out", (P, KT * SEQ), F32, kind="ExternalOutput").ap()
    build(nc, *args, out)
    r = run(nc, [arrays], core_ids=[0])
    o = r.results[0]["out"].reshape(P, KT, SEQ)
    return np.ascontiguousarray(o.transpose(2, 1, 0)).reshape(1, SEQ, D_MODEL)
```
